# Optimizing a Trainium2 kernel written in Bass

```python
import math
import jax, jax.numpy as jnp
from jax import lax
import numpy as np

D_MODEL = 1024
BATCH = 1
SEQ = 2048
DEPTH = 1

D_G = D_MODEL // 4
N_GROUPS = 5
D_MIX = N_GROUPS * D_G
N_SUB = 4
HEAD_DIM = D_G // N_SUB
CONV_A = 3
CONV_D = 31
CHUNK = 128
POOL_WINDOWS = (2, 4, 8, 16)
MEM_LEN = 256
LN_EPS = 1e-5
DEEPNORM_ALPHA = (2.0 * DEPTH) ** 0.25
DEEPNORM_BETA = (8.0 * DEPTH) ** -0.25

SPLIT_SIZES = (D_G, D_G, D_G, D_G, D_G, D_G, D_G, D_G, D_G, D_MIX)
D_IN = sum(SPLIT_SIZES)
SPLIT_OFFSETS = tuple(int(o) for o in np.cumsum(SPLIT_SIZES)[:-1])


def layer_norm(x, g, b):
    xf = x.astype(jnp.float32)
    mu = jnp.mean(xf, axis=-1, keepdims=True)
    var = jnp.mean(jnp.square(xf - mu), axis=-1, keepdims=True)
    y = (xf - mu) * lax.rsqrt(var + LN_EPS) * g.astype(jnp.float32) + b.astype(jnp.float32)
    return y.astype(x.dtype)

def causal_depthwise_conv(x, w):
    k, c = w.shape
    return lax.conv_general_dilated(
        x, w[:, None, :].astype(x.dtype), window_strides=(1,), padding=[(k - 1, 0)],
        dimension_numbers=("NWC", "WIO", "NWC"), feature_group_count=c)

def short_gated_conv(xa, ba, ca, w_conv):
    return ba * causal_depthwise_conv(ca * xa, w_conv)

def spatial_gating(u, v, ln_g, ln_b, w_s, b_s):
    bn, s, _ = v.shape
    u = jax.nn.gelu(u)
    v = layer_norm(jax.nn.gelu(v), ln_g, ln_b)
    v = v.reshape(bn, s // CHUNK, CHUNK, N_SUB, HEAD_DIM)
    mask = jnp.tril(jnp.ones((CHUNK, CHUNK), dtype=bool))
    w = jnp.where(mask[None], w_s, jnp.zeros_like(w_s))
    mixed = jnp.einsum("hts,bcshd->bcthd", w, v) + b_s.T[:, :, None]
    return u * mixed.reshape(bn, s, D_G)

def multiscale_pool(xc, w_grp, scale):
    bn, s, _ = xc.shape
    xf = xc.astype(jnp.float32).reshape(bn, s, N_SUB, HEAD_DIM)
    cs = jnp.pad(jnp.cumsum(xf, axis=1), ((0, 0), (1, 0), (0, 0), (0, 0)))
    t = jnp.arange(s)
    win = jnp.array(POOL_WINDOWS, dtype=jnp.int32)
    lo = jnp.maximum(t[:, None] + 1 - win[None, :], 0)
    window_sum = cs[:, 1:] - cs[:, lo, jnp.arange(N_SUB)[None, :]]
    count = jnp.minimum(t[:, None] + 1, win[None, :]).astype(jnp.float32)
    y = (window_sum / count[None, :, :, None] - xf).astype(xc.dtype)
    y = jnp.einsum("bsgc,gcd->bsgd", y, w_grp)
    return y.reshape(bn, s, D_G) * scale

def conformer_conv(a, g, w_dw, b_dw, ln_g, ln_b, w_pw):
    h = a * jax.nn.sigmoid(g)
    h = causal_depthwise_conv(h, w_dw) + b_dw
    h = jax.nn.silu(layer_norm(h, ln_g, ln_b))
    return h @ w_pw

def memory_cross_attention(q, mem, w_kv):
    bn, s, _ = q.shape
    k, v = jnp.split(mem @ w_kv, 2, axis=-1)
    q = q.reshape(bn, s, N_SUB, HEAD_DIM)
    k = k.reshape(bn, -1, N_SUB, HEAD_DIM)
    v = v.reshape(bn, -1, N_SUB, HEAD_DIM)
    scores = jnp.einsum("bshd,bmhd->bhsm", q, k).astype(jnp.float32) * (1.0 / math.sqrt(HEAD_DIM))
    p = jax.nn.softmax(scores, axis=-1).astype(v.dtype)
    return jnp.einsum("bhsm,bmhd->bshd", p, v).reshape(bn, s, D_G)

def hybrid_mixer(x, mem, w_in, conv_a_w, sg_ln_g, sg_ln_b, sg_w, sg_b, pool_w, pool_scale,
                 cc_dw_w, cc_dw_b, cc_ln_g, cc_ln_b, cc_pw_w, w_kv, w_out):
    proj = x @ w_in
    xa, ba, ca, u, v, xc, da, dg, q, gate = jnp.split(proj, SPLIT_OFFSETS, axis=-1)
    y_a = short_gated_conv(xa, ba, ca, conv_a_w)
    y_b = spatial_gating(u, v, sg_ln_g, sg_ln_b, sg_w, sg_b)
    y_c = multiscale_pool(xc, pool_w, pool_scale)
    y_d = conformer_conv(da, dg, cc_dw_w, cc_dw_b, cc_ln_g, cc_ln_b, cc_pw_w)
    y_e = memory_cross_attention(q, mem, w_kv)
    h = jnp.concatenate([y_a, y_b, y_c, y_d, y_e], axis=-1) * jax.nn.silu(gate)
    return h @ w_out

def first_inputs(seed: int = 0) -> dict:
    key = jax.random.key(seed)
    ks = jax.random.split(key, 20)
    L = DEPTH

    def nrm(k, shape, scale):
        return jax.random.normal(k, shape, jnp.float32) * scale

    return {
        "x": nrm(ks[0], (BATCH, SEQ, D_MODEL), 1.0),
        "mem": nrm(ks[1], (BATCH, MEM_LEN, D_MODEL), 1.0),
        "w_in": nrm(ks[2], (L, D_MODEL, D_IN), D_MODEL ** -0.5),
        "conv_a_w": nrm(ks[3], (L, CONV_A, D_G), CONV_A ** -0.5),
        "sg_ln_g": 1.0 + nrm(ks[4], (L, D_G), 0.05),
        "sg_ln_b": nrm(ks[5], (L, D_G), 0.05),
        "sg_w": nrm(ks[6], (L, N_SUB, CHUNK, CHUNK), CHUNK ** -0.5),
        "sg_b": 1.0 + nrm(ks[7], (L, N_SUB, CHUNK), 0.1),
        "pool_w": nrm(ks[8], (L, N_SUB, HEAD_DIM, HEAD_DIM), HEAD_DIM ** -0.5),
        "pool_scale": 1.0 + nrm(ks[9], (L, D_G), 0.1),
        "cc_dw_w": nrm(ks[10], (L, CONV_D, D_G), CONV_D ** -0.5),
        "cc_dw_b": nrm(ks[11], (L, D_G), 0.02),
        "cc_ln_g": 1.0 + nrm(ks[12], (L, D_G), 0.05),
        "cc_ln_b": nrm(ks[13], (L, D_G), 0.05),
        "cc_pw_w": nrm(ks[14], (L, D_G, D_G), D_G ** -0.5),
        "w_kv": nrm(ks[15], (L, D_MODEL, 2 * D_G), D_MODEL ** -0.5),
        "w_out": nrm(ks[16], (L, D_MIX, D_MODEL), D_MIX ** -0.5 * DEEPNORM_BETA),
        "ln_g": 1.0 + nrm(ks[17], (L, D_MODEL), 0.05),
        "ln_b": nrm(ks[18], (L, D_MODEL), 0.05),
    }

def first_block(x, mem, w_in, conv_a_w, sg_ln_g, sg_ln_b, sg_w, sg_b, pool_w, pool_scale,
              cc_dw_w, cc_dw_b, cc_ln_g, cc_ln_b, cc_pw_w, w_kv, w_out, ln_g, ln_b):
    for l in range(DEPTH):
        y = hybrid_mixer(x, mem, w_in[l], conv_a_w[l], sg_ln_g[l], sg_ln_b[l], sg_w[l], sg_b[l],
                         pool_w[l], pool_scale[l], cc_dw_w[l], cc_dw_b[l], cc_ln_g[l], cc_ln_b[l],
                         cc_pw_w[l], w_kv[l], w_out[l])
        x = layer_norm(DEEPNORM_ALPHA * x + y, ln_g[l], ln_b[l])
    return x


N_META = 16
GRID_W = 64
Q_BLOCK = 128
ROPE_THETA = 10000.0

MLA_HEADS = 4
Q_LORA = 256
KV_LORA = 128
NOPE_DIM = 128
ROPE_DIM = 64
V_DIM = 128
QK_DIM = NOPE_DIM + ROPE_DIM

GQA_HEADS = 4
GQA_KV_HEADS = 2
GQA_DIM = 128
AXIAL_HALF = GQA_DIM // 2

MLA_WIDTH = MLA_HEADS * V_DIM
GQA_WIDTH = GQA_HEADS * GQA_DIM
MIX_WIDTH = MLA_WIDTH + GQA_WIDTH

IN_SPLITS = (Q_LORA, KV_LORA, ROPE_DIM, GQA_HEADS * GQA_DIM, GQA_KV_HEADS * GQA_DIM, GQA_KV_HEADS * GQA_DIM)
IN_COLS = sum(IN_SPLITS)
IN_OFFSETS = tuple(int(o) for o in np.cumsum(IN_SPLITS)[:-1])

N_EXPERTS = 32
TOP_K = 4
D_FF = D_MODEL
SWIGLU_LIMIT = 7.0
SWIGLU_ALPHA = 1.702

RMS_EPS = 1e-6
DEEPNORM_ALPHA_2 = (2.0 * DEPTH) ** 0.25
DEEPNORM_BETA_2 = (8.0 * DEPTH) ** -0.25


def _rmsnorm(x, g):
    xf = x.astype(jnp.float32)
    y = xf * lax.rsqrt(jnp.mean(xf * xf, axis=-1, keepdims=True) + RMS_EPS)
    return (y * g.astype(jnp.float32)).astype(x.dtype)

def _layernorm(x, g, b):
    xf = x.astype(jnp.float32)
    mu = jnp.mean(xf, axis=-1, keepdims=True)
    var = jnp.mean(jnp.square(xf - mu), axis=-1, keepdims=True)
    y = (xf - mu) * lax.rsqrt(var + LN_EPS)
    return (y * g.astype(jnp.float32) + b.astype(jnp.float32)).astype(x.dtype)

def _rope_cos_sin(pos, dim):
    inv = ROPE_THETA ** (-jnp.arange(0, dim, 2, dtype=jnp.float32) / dim)
    ang = pos.astype(jnp.float32)[:, None] * inv[None, :]
    return jnp.cos(ang)[:, None, :], jnp.sin(ang)[:, None, :]

def _rotate(x, cos, sin):
    xf = x.astype(jnp.float32)
    x1, x2 = jnp.split(xf, 2, axis=-1)
    return jnp.concatenate([x1 * cos - x2 * sin, x1 * sin + x2 * cos], axis=-1).astype(x.dtype)

def _attend(q, k, v, scale):
    s = jnp.einsum('bqkgd,bskd->bkgqs', q, k).astype(jnp.float32) * scale
    p = jax.nn.softmax(s, axis=-1).astype(v.dtype)
    return jnp.einsum('bkgqs,bskd->bqkgd', p, v)

def _blocked_attention(q, k, v, scale):
    B, L, H, Dq = q.shape
    Hk = k.shape[2]
    G = H // Hk
    Dv = v.shape[-1]
    q = q.reshape(B, L, Hk, G, Dq)
    o_meta = _attend(q[:, :N_META], k, v, scale)
    n_blk = (L - N_META) // Q_BLOCK
    qb = q[:, N_META:].reshape(B, n_blk, Q_BLOCK, Hk, G, Dq).transpose(1, 0, 2, 3, 4, 5)
    ob = lax.map(lambda qi: _attend(qi, k, v, scale), qb)
    ob = ob.transpose(1, 0, 2, 3, 4, 5).reshape(B, L - N_META, Hk, G, Dv)
    return jnp.concatenate([o_meta, ob], axis=1).reshape(B, L, H, Dv)

def _mixer(h, pos_1d, row, col, w_in, g_q_a, w_q_b, g_kv_a, w_kv_b, g_q_gqa, g_k_gqa, g_o_mla, g_o_gqa, w_o):
    B, L, _ = h.shape
    z = jnp.einsum('bld,dc->blc', h, w_in)
    q_a, kv_a, k_pe, q_g, k_g, v_g = jnp.split(z, IN_OFFSETS, axis=-1)

    cos1, sin1 = _rope_cos_sin(pos_1d, ROPE_DIM)
    q = jnp.einsum('blr,rc->blc', _rmsnorm(q_a, g_q_a), w_q_b).reshape(B, L, MLA_HEADS, QK_DIM)
    q_m = jnp.concatenate([q[..., :NOPE_DIM], _rotate(q[..., NOPE_DIM:], cos1, sin1)], axis=-1)
    kv = jnp.einsum('blr,rc->blc', _rmsnorm(kv_a, g_kv_a), w_kv_b).reshape(B, L, MLA_HEADS, NOPE_DIM + V_DIM)
    k_rot = _rotate(k_pe[:, :, None, :], cos1, sin1)
    k_m = jnp.concatenate([kv[..., :NOPE_DIM], jnp.broadcast_to(k_rot, (B, L, MLA_HEADS, ROPE_DIM))], axis=-1)
    v_m = kv[..., NOPE_DIM:]
    o_mla = _blocked_attention(q_m, k_m, v_m, QK_DIM ** -0.5).reshape(B, L, MLA_WIDTH)

    cos_r, sin_r = _rope_cos_sin(row, AXIAL_HALF)
    cos_c, sin_c = _rope_cos_sin(col, AXIAL_HALF)

    def axial(t):
        return jnp.concatenate([_rotate(t[..., :AXIAL_HALF], cos_r, sin_r),
                                _rotate(t[..., AXIAL_HALF:], cos_c, sin_c)], axis=-1)

    qg = axial(_rmsnorm(q_g.reshape(B, L, GQA_HEADS, GQA_DIM), g_q_gqa))
    kg = axial(_rmsnorm(k_g.reshape(B, L, GQA_KV_HEADS, GQA_DIM), g_k_gqa))
    vg = v_g.reshape(B, L, GQA_KV_HEADS, GQA_DIM)
    o_gqa = _blocked_attention(qg, kg, vg, GQA_DIM ** -0.5).reshape(B, L, GQA_WIDTH)

    o = jnp.concatenate([_rmsnorm(o_mla, g_o_mla), _rmsnorm(o_gqa, g_o_gqa)], axis=-1)
    return jnp.einsum('blc,cd->bld', o, w_o)

def _clamped_swiglu(hgu):
    x_glu = jnp.minimum(hgu[..., ::2], SWIGLU_LIMIT)
    x_lin = jnp.clip(hgu[..., 1::2], -SWIGLU_LIMIT, SWIGLU_LIMIT)
    return x_glu * jax.nn.sigmoid(SWIGLU_ALPHA * x_glu) * (x_lin + 1.0)

def _moe_sequence(h, w_router, b_router, w_gate_up, b_gate_up, w_down, b_down):
    L = h.shape[0]
    logits = (jnp.einsum('ld,de->le', h, w_router) + b_router).astype(jnp.float32)
    top_val, top_idx = lax.top_k(logits, TOP_K)
    gates = jax.nn.softmax(top_val, axis=-1).astype(h.dtype)
    flat_e = top_idx.reshape(-1)
    order = jnp.argsort(flat_e)
    tok = order // TOP_K
    e_sorted = flat_e[order]
    group_sizes = jnp.bincount(flat_e, length=N_EXPERTS).astype(jnp.int32)
    xs = h[tok]
    hgu = lax.ragged_dot(xs, w_gate_up, group_sizes) + b_gate_up[e_sorted]
    act = _clamped_swiglu(hgu)
    out = lax.ragged_dot(act, w_down, group_sizes) + b_down[e_sorted]
    out = out * gates.reshape(-1)[order][:, None]
    return jax.ops.segment_sum(out, tok, num_segments=L)

def second_inputs(seed: int = 0) -> dict:
    key = jax.random.key(seed)
    ks = jax.random.split(key, 28)
    f32 = jnp.float32

    def nrm(k, shape, scale):
        return jax.random.normal(k, shape, f32) * scale

    def gain(k, shape):
        return 1.0 + 0.05 * jax.random.normal(k, shape, f32)

    Dp = DEPTH
    return {
        'x': jax.random.normal(ks[0], (BATCH, SEQ, D_MODEL), f32),
        'meta_tokens': nrm(ks[1], (N_META, D_MODEL), 1.0),
        'ln_emb_g': gain(ks[2], (D_MODEL,)),
        'ln_emb_b': nrm(ks[3], (D_MODEL,), 0.02),
        'w_in': nrm(ks[4], (Dp, D_MODEL, IN_COLS), D_MODEL ** -0.5),
        'g_q_a': gain(ks[5], (Dp, Q_LORA)),
        'w_q_b': nrm(ks[6], (Dp, Q_LORA, MLA_HEADS * QK_DIM), Q_LORA ** -0.5),
        'g_kv_a': gain(ks[7], (Dp, KV_LORA)),
        'w_kv_b': nrm(ks[8], (Dp, KV_LORA, MLA_HEADS * (NOPE_DIM + V_DIM)), KV_LORA ** -0.5),
        'g_q_gqa': gain(ks[9], (Dp, GQA_DIM)),
        'g_k_gqa': gain(ks[10], (Dp, GQA_DIM)),
        'g_o_mla': gain(ks[11], (Dp, MLA_WIDTH)),
        'g_o_gqa': gain(ks[12], (Dp, GQA_WIDTH)),
        'w_o': nrm(ks[13], (Dp, MIX_WIDTH, D_MODEL), DEEPNORM_BETA_2 * MIX_WIDTH ** -0.5),
        'ln1_g': gain(ks[14], (Dp, D_MODEL)),
        'ln1_b': nrm(ks[15], (Dp, D_MODEL), 0.02),
        'w_router': nrm(ks[16], (Dp, D_MODEL, N_EXPERTS), D_MODEL ** -0.5),
        'b_router': nrm(ks[17], (Dp, N_EXPERTS), 0.01),
        'w_gate_up': nrm(ks[18], (Dp, N_EXPERTS, D_MODEL, 2 * D_FF), D_MODEL ** -0.5),
        'b_gate_up': nrm(ks[19], (Dp, N_EXPERTS, 2 * D_FF), 0.02),
        'w_down': nrm(ks[20], (Dp, N_EXPERTS, D_FF, D_MODEL), DEEPNORM_BETA_2 * D_FF ** -0.5),
        'b_down': nrm(ks[21], (Dp, N_EXPERTS, D_MODEL), 0.02),
        'ln2_g': gain(ks[22], (Dp, D_MODEL)),
        'ln2_b': nrm(ks[23], (Dp, D_MODEL), 0.02),
    }

def second_block(x, meta_tokens, ln_emb_g, ln_emb_b, w_in, g_q_a, w_q_b, g_kv_a, w_kv_b,
              g_q_gqa, g_k_gqa, g_o_mla, g_o_gqa, w_o, ln1_g, ln1_b,
              w_router, b_router, w_gate_up, b_gate_up, w_down, b_down, ln2_g, ln2_b):
    B, S, D = x.shape
    meta = jnp.broadcast_to(meta_tokens.astype(x.dtype)[None], (B, N_META, D))
    h = _layernorm(jnp.concatenate([meta, x], axis=1), ln_emb_g, ln_emb_b)
    L = S + N_META

    rows = S // GRID_W
    pos_1d = jnp.arange(L, dtype=jnp.int32)
    row = jnp.concatenate([jnp.full((N_META,), -1, jnp.int32), jnp.repeat(jnp.arange(rows, dtype=jnp.int32), GRID_W)])
    col = jnp.concatenate([jnp.arange(N_META, dtype=jnp.int32), jnp.tile(jnp.arange(GRID_W, dtype=jnp.int32), rows)])

    for i in range(DEPTH):
        mix = _mixer(h, pos_1d, row, col, w_in[i], g_q_a[i], w_q_b[i], g_kv_a[i], w_kv_b[i],
                     g_q_gqa[i], g_k_gqa[i], g_o_mla[i], g_o_gqa[i], w_o[i])
        h = _layernorm(DEEPNORM_ALPHA_2 * h + mix, ln1_g[i], ln1_b[i])
        moe = lax.map(lambda hs: _moe_sequence(hs, w_router[i], b_router[i], w_gate_up[i],
                                               b_gate_up[i], w_down[i], b_down[i]), h)
        h = _layernorm(DEEPNORM_ALPHA_2 * h + moe, ln2_g[i], ln2_b[i])

    return h[:, N_META:]


def setup_inputs(seed=0):
    out = dict(first_inputs(seed))
    for name, value in second_inputs(seed + 1).items():
        if name != "x":
            out[name + "_2"] = value
    return out


def reference(
    x, mem, w_in, conv_a_w, sg_ln_g, sg_ln_b, sg_w, sg_b, pool_w, pool_scale, cc_dw_w, cc_dw_b,
    cc_ln_g, cc_ln_b, cc_pw_w, w_kv, w_out, ln_g, ln_b, meta_tokens_2, ln_emb_g_2, ln_emb_b_2,
    w_in_2, g_q_a_2, w_q_b_2, g_kv_a_2, w_kv_b_2, g_q_gqa_2, g_k_gqa_2, g_o_mla_2, g_o_gqa_2,
    w_o_2, ln1_g_2, ln1_b_2, w_router_2, b_router_2, w_gate_up_2, b_gate_up_2, w_down_2,
    b_down_2, ln2_g_2, ln2_b_2,
):
    x = first_block(
        x, mem, w_in, conv_a_w, sg_ln_g, sg_ln_b, sg_w, sg_b, pool_w, pool_scale, cc_dw_w,
        cc_dw_b, cc_ln_g, cc_ln_b, cc_pw_w, w_kv, w_out, ln_g, ln_b,
    )
    return second_block(
        x, meta_tokens_2, ln_emb_g_2, ln_emb_b_2, w_in_2, g_q_a_2, w_q_b_2, g_kv_a_2, w_kv_b_2,
        g_q_gqa_2, g_k_gqa_2, g_o_mla_2, g_o_gqa_2, w_o_2, ln1_g_2, ln1_b_2, w_router_2,
        b_router_2, w_gate_up_2, b_gate_up_2, w_down_2, b_down_2, ln2_g_2, ln2_b_2,
    )


_drawn_inputs = setup_inputs


def setup_inputs(seed=0):
    import zlib

    import numpy as np

    out = dict(_drawn_inputs(seed))
    spreads = {}
    factors = {'sg_ln_g': 5.808,
     'sg_ln_b': 6.113,
     'sg_b': 3.312,
     'pool_scale': 2.736,
     'cc_dw_b': 3.941,
     'cc_ln_g': 3.944,
     'cc_ln_b': 3.445,
     'g_q_gqa_2': 3.469,
     'g_k_gqa_2': 3.15,
     'b_router_2': 3.089,
     'b_gate_up_2': 8.0,
     'b_down_2': 6.446,
     'ln2_b_2': 2.85}
    for name, (base, spread) in spreads.items():
        noise = np.random.default_rng([zlib.crc32(name.encode()), seed]).standard_normal(out[name].shape)
        drawn = base * np.exp(spread * noise) if base else spread * noise
        out[name] = __import__('jax').numpy.asarray(drawn.astype(out[name].dtype))
    for name, factor in factors.items():
        out[name] = (out[name] * factor).astype(out[name].dtype)
    return out
```

```python
from contextlib import ExitStack

import numpy as np

import concourse.bass as bass
from concourse import mybir

ALU = mybir.AluOpType
ACT = mybir.ActivationFunctionType
AX = mybir.AxisListType.X
F32 = mybir.dt.float32
I32 = mybir.dt.int32
U32 = mybir.dt.uint32

S = 2048
D = 1024
NM = 16
L = S + NM
NE = 32
CAP = 2048
YB = 96
ALPHA = 2.0 ** 0.25
LN_EPS = 1e-5
RMS_EPS = 1e-6
CH = 512
SQK_M = 192 ** -0.5
SQK_G = 128 ** -0.5

PC_CONVA, PC_DW, PC_DWB, PC_CLG, PC_CLB, PC_PS, PC_GQA, PC_GKV = 0, 6, 68, 70, 72, 74, 76, 78
PC_N = 79


class Slot:

    def __init__(self, ap, sem=None):
        self.ap, self.sem, self.n = ap, sem, 0
        self.full, self.free = [], []


class Ring:
    def __init__(self, slots):
        self.slots, self.i = slots, 0

    def next(self):
        s = self.slots[self.i % len(self.slots)]
        self.i += 1
        return s


class Prog:

    def __init__(self, nc):
        self.nc = nc
        self.eng = {"pe": nc.tensor, "dve": nc.vector, "act": nc.scalar, "pool": nc.gpsimd, "sp": nc.sync}
        self.nphase = 0
        self.open()

    def open(self):
        self.sem = {e: self.nc.alloc_semaphore(f"s{self.nphase}_{e}") for e in ("pe", "dve", "act", "pool")}
        self.cnt = {e: 0 for e in self.sem}
        self.seen = {}
        self.dmas = []
        self.nphase += 1

    def inc(self, e, ins):
        ins.then_inc(self.sem[e], 1)
        self.cnt[e] += 1
        return (self.sem[e], self.cnt[e])

    def wait(self, e, *toks):
        for sem, n in toks:
            key = (e, sem.name)
            if self.seen.get(key, 0) < n:
                self.eng[e].wait_ge(sem, n)
                self.seen[key] = n

    def slot_sem(self, name):
        return self.nc.alloc_semaphore(name)

    def dma(self, e, slot, out, in_, **kw):
        self.eng[e].dma_start(out, in_, **kw).then_inc(slot.sem, 16)
        slot.n += 16
        t = (slot.sem, slot.n)
        self.dmas.append(t)
        return t

    def close(self):
        last = {}
        for sem, n in self.dmas:
            last[sem.name] = (sem, n)
        ends = list(last.values()) + [(self.sem[e], self.cnt[e]) for e in self.sem if self.cnt[e]]
        for e in self.eng:
            self.wait(e, *ends)
        self.open()


def bcast(ap1d, n):
    return ap1d.rearrange("(o n) -> o n", o=1).broadcast_to([128, n])


def layer_norm(p, x, n, rows, st, mv, sd, rs, eps_t, out, g, b, ready, out_free, eng2="dve"):
    nc = p.nc
    k = max(1, n // 512)
    w = n // k
    p.wait("dve", *ready)
    for i in range(k):
        t = p.inc("dve", nc.vector.bn_stats(st[:rows, i * 6:(i + 1) * 6], x[:rows, i * w:(i + 1) * w]))
    p.wait("dve", t)
    t = p.inc("dve", nc.vector.bn_aggr(mv[:rows, :], st[:rows, 0:6 * k]))
    p.wait("act", t)
    t = p.inc("act", nc.scalar.activation(sd[:rows, :], mv[:rows, 1:2], ACT.Sqrt, bias=eps_t[:rows, :], scale=1.0))
    p.wait("dve", t)
    t = p.inc("dve", nc.vector.reciprocal(rs[:rows, :], sd[:rows, :]))
    p.wait("dve", t, *out_free)
    t = p.inc("dve", nc.vector.tensor_scalar(out[:rows, :n], x[:rows, :n], mv[:rows, 0:1], rs[:rows, 0:1],
                                             ALU.subtract, ALU.mult))
    p.wait(eng2, t)
    t = p.inc(eng2, p.eng[eng2].tensor_tensor(out[:rows, :n], out[:rows, :n], g[:rows, :n], ALU.mult))
    p.wait(eng2, t)
    return p.inc(eng2, p.eng[eng2].tensor_tensor(out[:rows, :n], out[:rows, :n], b[:rows, :n], ALU.add))


def phase_mixer(p, A, h0d, ident, eps_ln):
    nc = p.nc
    with ExitStack() as ctx:
        def sb(name, shape, dt=F32):
            return ctx.enter_context(nc.sbuf_tensor("m_" + name, shape, dt))

        banks = [ctx.enter_context(nc.psum_tensor(f"m_ps{i}", [128, 512], F32)) for i in range(8)]
        PR = Ring([Slot(b) for b in banks[0:3]])
        MS = Ring([Slot(b) for b in banks[3:8]])

        xT = sb("xT", [128, 2, 8, CH])
        xTs = [Slot(xT[:, i], p.slot_sem(f"m_xT{i}")) for i in range(2)]
        NW = 4
        wt = sb("wt", [128, NW, 8, 256])
        W = Ring([Slot(wt[:, i], p.slot_sem(f"m_w{i}")) for i in range(NW)])
        wo = sb("wo", [128, 10, 1024])
        yT = sb("yT", [128, 10, CH])
        pc = sb("pc", [128, PC_N])
        wsg = sb("wsg", [128, 4, 128])
        tri = sb("tri", [128, 128])
        sgb = sb("sgb", [128, 2, 128])
        poolw = sb("poolw", [128, 2, 128])
        pw = sb("pw", [128, 2, 256])
        prc = sb("prc", [128, 2, 17])
        onm = sb("onm", [128, 128])
        lngb = sb("lngb", [128, 2, 256])
        LN = sb("LN", [128, 4, 1024])
        kT = sb("kT", [128, 2, 256])
        vm = sb("vm", [128, 2, 256])
        At = sb("At", [128, 2, 2 + CH])
        Dt = sb("Dt", [128, 2, 30 + CH])
        Ct = sb("Ct", [128, 2, 15 + CH])
        qT = sb("qT", [128, 2, CH])
        acc = sb("acc", [128, 2, CH])
        tmp = sb("tmp", [128, 2, CH])
        tmp2 = sb("tmp2", [128, 2, 15 + CH])
        gvn = sb("gvn", [128, 4, 256])
        pe_ = sb("pe_", [128, 4, 256])
        pT = sb("pT", [128, 8, 128])
        st = sb("st", [128, 64])
        xr = sb("xr", [128, 2, 1024])
        h0 = sb("h0", [128, 1, 1024])

        cs = p.slot_sem("m_const")
        cslot = Slot(None, cs)

        def const(dst, src, e="sp"):
            cslot.full.append(p.dma(e, cslot, dst, src))

        const(pc[:], A["pc"], "act")
        memT = xT[:, 1, 0:4, :].rearrange("p a b -> p (a b)").rearrange("p (k m) -> p k m", k=8)
        wkv = wt[:, 2:4].rearrange("p a k n -> p (a k n)").rearrange("p (k n) -> p k n", k=8)
        const(memT, A["memT"])
        const(wkv, A["wkv"])
        xTs[0].full = [p.dma("sp", xTs[0], xTs[0].ap, A["xT"][:, :, 0:CH])]
        const(onm[:], A["onm"], "act")
        const(wsg[:], A["sgw"], "act")
        const(tri[:], A["tri"], "act")
        const(sgb[:], A["sgb"], "act")
        const(poolw[:], A["poolw"], "act")
        const(pw[:], A["pw"], "act")
        const(prc[:], A["prc"], "act")
        const(lngb[:, 0, :], bcast(A["sg_ln_g"], 256), "act")
        const(lngb[:, 1, :], bcast(A["sg_ln_b"], 256), "act")
        for i, n in enumerate(("ln_g", "ln_b", "ln_emb_g_2", "ln_emb_b_2")):
            const(LN[:, i, :], bcast(A[n], 1024), "act")
        consts = [cslot.full[-1]]
        for e in ("pe", "dve", "act", "pool"):
            p.wait(e, *consts)
        t = p.inc("pool", nc.gpsimd.memset(At[:, :, 0:2], 0.0))
        t = p.inc("pool", nc.gpsimd.memset(Dt[:, :, 0:30], 0.0))
        halo0 = p.inc("pool", nc.gpsimd.memset(Ct[:, :, 0:15], 0.0))
        halo = {"A": [halo0], "D": [halo0], "C": [halo0]}
        t = [p.inc("pool", nc.gpsimd.tensor_tensor(wsg[:, h, :], wsg[:, h, :], tri[:], ALU.mult)) for h in range(4)]
        wsg_ok = t[-1]
        s = MS.next()
        for j in range(2):
            for k in range(8):
                t = nc.tensor.matmul(s.ap[:, j * 256:(j + 1) * 256], wkv[:, k, j * 128:(j + 1) * 128], memT[:, k, :],
                                     start=(k == 0), stop=(k == 7))
        t = p.inc("pe", t)
        p.wait("act", t)
        kv_ok = p.inc("act", nc.scalar.copy(kT[:].rearrange("p a b -> p (a b)"), s.ap[:, :]))
        s.free = [kv_ok]
        s = MS.next()
        for j in range(2):
            for k in range(8):
                t = nc.tensor.matmul(s.ap[:, j * 256:(j + 1) * 256], memT[:, k, j * 128:(j + 1) * 128], wkv[:, k, 256:512],
                                     start=(k == 0), stop=(k == 7))
        kvpe = p.inc("pe", t)
        p.wait("act", kvpe)
        kv_ok = p.inc("act", nc.scalar.copy(vm[:].rearrange("p a b -> p (a b)"), s.ap[:, :]))
        s.free = [kv_ok]
        W.slots[2].free = W.slots[3].free = [kvpe]
        xTs[1].free = [kvpe]

        order = [7, 6, 8, 5, 0, 2, 1, 4, 3, 9, 10, 11, 12, 13]
        loads = [(c, g) for c in range(4) for g in order]
        issued = {}

        def issue(n):
            if n >= len(loads):
                return
            c, g = loads[n]
            s = W.next()
            p.wait("sp", *s.free)
            s.full = [p.dma("sp", s, s.ap, A["w1"][g])]
            issued[(c, g)] = s

        for n in range(NW):
            issue(n)
        wos = Slot(wo[:], p.slot_sem("m_wo"))
        wos.full = [p.dma("sp", wos, wo[:], A["wout"])]
        nl = [NW]

        xrs = Ring([Slot(xr[:, i], p.slot_sem(f"m_xr{i}")) for i in range(2)])
        h0s = Ring([Slot(h0[:, 0], p.slot_sem("m_h00"))])

        def proj(c, g, each):
            w = issued[(c, g)]
            x = xTs[c % 2]
            p.wait("pe", *w.full, *x.full)
            for j in range(2):
                s = PR.next()
                p.wait("pe", *s.free)
                for k in range(8):
                    t = nc.tensor.matmul(s.ap[:, :], w.ap[:, k, j * 128:(j + 1) * 128], x.ap[:, k, :],
                                         start=(k == 0), stop=(k == 7))
                t = p.inc("pe", t)
                s.free = [each(j, s.ap, t)]
            w.free = [t]
            x.free = [t]
            issue(nl[0])
            nl[0] += 1

        sgq = {}
        Y = {}
        free = {}

        def fr(name):
            return free.get(name, [])

        for c in range(4):
            def e_dg(j, ps, t):
                p.wait("act", t, *fr("tmp"))
                sgq[j] = p.inc("act", nc.scalar.activation(tmp[:, j, :], ps[:, :], ACT.Sigmoid))
                return sgq[j]

            proj(c, 7, e_dg)
            dok = {}

            def e_da(j, ps, t):
                p.wait("dve", t, sgq[j], *fr("D"))
                dok[j] = p.inc("dve", nc.vector.tensor_tensor(Dt[:, j, 30:], ps[:, :], tmp[:, j, :], ALU.mult))
                return dok[j]

            proj(c, 6, e_da)
            free["tmp"] = [dok[1]]

            def e_q(j, ps, t):
                p.wait("act", t, *fr("q"))
                sgq["q"] = p.inc("act", nc.scalar.copy(qT[:, j, :], ps[:, :]))
                return sgq["q"]

            proj(c, 8, e_q)
            q_ok = sgq["q"]

            t2 = {}
            for j in range(2):
                p.wait("dve", dok[j], *halo["D"], *fr("acc"))
                t2[j] = p.inc("dve", nc.vector.tensor_scalar(acc[:, j, :], Dt[:, j, 0:CH], pc[:, PC_DW + j:PC_DW + j + 1],
                                                             pc[:, PC_DWB + j:PC_DWB + j + 1], ALU.mult, ALU.add))
            for k in range(1, 31):
                for j in range(2):
                    p.wait("dve", t2[j])
                    t2[j] = p.inc("dve", nc.vector.scalar_tensor_tensor(
                        out=acc[:, j, :], in0=Dt[:, j, k:k + CH], scalar=pc[:, PC_DW + 2 * k + j:PC_DW + 2 * k + j + 1],
                        in1=acc[:, j, :], op0=ALU.mult, op1=ALU.add))
            conv_ok = t2[1]
            p.wait("dve", conv_ok)
            t = p.inc("dve", nc.vector.tensor_copy(Dt[:, :, 0:30], Dt[:, :, CH:CH + 30]))
            halo["D"] = [t]
            free["D"] = [t]

            def cross(m):
                sc = []
                for pr in range(2):
                    s = MS.next()
                    p.wait("pe", *s.free, q_ok, kv_ok)
                    lo = 64 * pr
                    for hh in range(2):
                        t = nc.tensor.matmul(s.ap[:, hh * 256:(hh + 1) * 256], qT[lo:lo + 64, hh, m * 128:(m + 1) * 128],
                                             kT[lo:lo + 64, hh, :], start=True, stop=True)
                    sc.append((s, p.inc("pe", t)))
                free["q"] = [sc[1][1]]
                mx, nb, sm, rc = st[:, 0:4], st[:, 4:8], st[:, 8:12], st[:, 12:16]
                for pr, (s, t) in enumerate(sc):
                    p.wait("dve", t, *fr("nb"))
                    t = p.inc("dve", nc.vector.tensor_reduce(mx[:, pr:4:2],
                                                             s.ap[:, :].rearrange("p (a b) -> p a b", a=2), AX, ALU.max))
                p.wait("dve", t)
                t = p.inc("dve", nc.vector.tensor_scalar(nb, mx, -0.125, None, ALU.mult))
                p.wait("act", t, *fr("pe_"))
                for h in range(4):
                    s = sc[h % 2][0]
                    t = p.inc("act", nc.scalar.activation(pe_[:, h, :], s.ap[:, (h // 2) * 256:(h // 2 + 1) * 256], ACT.Exp,
                                                          bias=nb[:, h:h + 1], scale=0.125, accum_out=sm[:, h:h + 1]))
                    s.free = [t]
                free["nb"] = [t]
                p.wait("dve", t)
                t = p.inc("dve", nc.vector.reciprocal(rc, sm))
                p.wait("dve", t)
                for h in range(4):
                    t = p.inc("dve", nc.vector.tensor_scalar(pe_[:, h, :], pe_[:, h, :], rc[:, h:h + 1], None, ALU.mult))
                pt = []
                for pr in range(2):
                    s = MS.next()
                    p.wait("pe", t, *s.free)
                    for i in range(4):
                        h, j = 2 * pr + i // 2, i % 2
                        u = nc.tensor.transpose(s.ap[:, i * 128:(i + 1) * 128], pe_[:, h, j * 128:(j + 1) * 128], ident[:])
                    u = p.inc("pe", u)
                    p.wait("act", u, *fr("pT"))
                    v = p.inc("act", nc.scalar.copy(pT[:, 4 * pr:4 * pr + 4, :].rearrange("p a b -> p (a b)"), s.ap[:, :]))
                    s.free = [v]
                    pt.append(v)
                free["pe_"] = [u]
                s = MS.next()
                p.wait("pe", *pt, *s.free)
                for h in range(4):
                    lo = 64 * (h % 2)
                    for j in range(2):
                        t = nc.tensor.matmul(s.ap[lo:lo + 64, (h // 2) * 128:(h // 2 + 1) * 128],
                                             vm[:, j, h * 64:(h + 1) * 64], pT[:, 2 * h + j, :],
                                             start=(j == 0), stop=(j == 1), skip_group_check=True)
                t = p.inc("pe", t)
                free["pT"] = [t]
                p.wait("act", t, *fr("yT"))
                t = p.inc("act", nc.scalar.copy(yT[:, 8:10, m * 128:(m + 1) * 128],
                                                s.ap[:, 0:256].rearrange("p (a b) -> p a b", a=2)))
                s.free = [t]
                Y[8] = Y[9] = t

            cok = {}

            def e_xc(j, ps, t):
                p.wait("act", t, *fr("C"))
                cok[j] = p.inc("act", nc.scalar.copy(Ct[:, j, 15:], ps[:, :]))
                return cok[j]

            proj(c, 5, e_xc)
            cross(0)
            N = 15 + CH
            for j in range(2):
                src, off = Ct[:, j, :], 0
                p.wait("pool", cok[j], *halo["C"], *fr("tmp2"))
                w, b = 1, 0
                res = {}
                steps = 2 if j == 0 else 4
                for i in range(steps):
                    lo = 2 * w - 1
                    t = p.inc("pool", nc.gpsimd.tensor_tensor(tmp2[:, b, lo:N], src[:, lo:N], src[:, lo - w:N - w], ALU.add))
                    p.wait("pool", t)
                    src = tmp2[:, b, :]
                    res[2 * w] = (src, t)
                    w *= 2
                    b = 1 - b
                a, z = (2, 4) if j == 0 else (8, 16)
                p.wait("dve", res[z][1], *fr("tmp"))
                for lo, win in ((0, a), (64, z)):
                    src = res[win][0]
                    if c == 0:
                        t = p.inc("dve", nc.vector.tensor_tensor(tmp[lo:lo + 64, j, 0:16], src[lo:lo + 64, 15:31],
                                                                 prc[lo:lo + 64, j, 0:16], ALU.mult))
                        p.wait("dve", t)
                        t = p.inc("dve", nc.vector.tensor_tensor(tmp[lo:lo + 64, j, 0:16], tmp[lo:lo + 64, j, 0:16],
                                                                 Ct[lo:lo + 64, j, 15:31], ALU.subtract))
                    o = 16 if c == 0 else 0
                    t = p.inc("dve", nc.vector.scalar_tensor_tensor(
                        out=tmp[lo:lo + 64, j, o:CH], in0=src[lo:lo + 64, 15 + o:N], scalar=prc[lo:lo + 64, j, 16:17],
                        in1=Ct[lo:lo + 64, j, 15 + o:N], op0=ALU.mult, op1=ALU.subtract))
                free["tmp2"] = [t]
                s = MS.next()
                p.wait("pe", t, *s.free)
                u = p.inc("pe", nc.tensor.matmul(s.ap[:, :], poolw[:, j, :], tmp[:, j, :], start=True, stop=True))
                p.wait("act", u, *fr("yT"))
                Y[4 + j] = p.inc("act", nc.scalar.activation(yT[:, 4 + j, :], s.ap[:, :], ACT.Copy,
                                                             scale=pc[:, PC_PS + j:PC_PS + j + 1]))
                s.free = [Y[4 + j]]
                free["tmp"] = [u]
            p.wait("pool", t)
            t = p.inc("pool", nc.gpsimd.tensor_copy(Ct[:, :, 0:15], Ct[:, :, CH:CH + 15]))
            halo["C"] = [t]
            free["C"] = [t]

            s = MS.next()
            p.wait("pe", conv_ok, *s.free)
            for j in range(2):
                t = nc.tensor.matmul(s.ap[:, :], onm[:], acc[:, j, :], start=(j == 0), stop=(j == 1))
            t = p.inc("pe", t)
            p.wait("dve", t, *fr("D2"))
            for j in range(2):
                t = p.inc("dve", nc.vector.tensor_tensor(acc[:, j, :], acc[:, j, :], s.ap[:, :], ALU.subtract))
            s.free = [t]
            p.wait("act", t, *free["tmp"])
            for j in range(2):
                t = p.inc("act", nc.scalar.activation(tmp[:, j, :], acc[:, j, :], ACT.Square))
            s = MS.next()
            p.wait("pe", t, *s.free)
            for j in range(2):
                t = nc.tensor.matmul(s.ap[:, :], onm[:], tmp[:, j, :], start=(j == 0), stop=(j == 1))
            t = p.inc("pe", t)
            p.wait("act", t)
            t = p.inc("act", nc.scalar.activation(tmp[:, 0, :], s.ap[:, :], ACT.Sqrt, bias=eps_ln[:], scale=1.0))
            s.free = [t]
            p.wait("dve", t)
            t = p.inc("dve", nc.vector.reciprocal(tmp[:, 1, :], tmp[:, 0, :]))
            p.wait("dve", t)
            for j in range(2):
                t = p.inc("dve", nc.vector.tensor_tensor(acc[:, j, :], acc[:, j, :], tmp[:, 1, :], ALU.mult))
            free["tmp"] = [t]
            p.wait("act", t)
            for j in range(2):
                t = p.inc("act", nc.scalar.activation(acc[:, j, :], acc[:, j, :], ACT.Silu,
                                                      bias=pc[:, PC_CLB + j:PC_CLB + j + 1],
                                                      scale=pc[:, PC_CLG + j:PC_CLG + j + 1]))
            cn_ok = t

            xa_ok = {}

            def e_xa(j, ps, t):
                p.wait("act", t, *free["tmp"])
                xa_ok[j] = p.inc("act", nc.scalar.copy(tmp[:, j, :], ps[:, :]))
                return xa_ok[j]

            proj(c, 0, e_xa)
            cross(1)
            ca_ok = {}

            def e_ca(j, ps, t):
                p.wait("dve", t, xa_ok[j], *halo["A"], *fr("A"))
                ca_ok[j] = p.inc("dve", nc.vector.tensor_tensor(At[:, j, 2:], ps[:, :], tmp[:, j, :], ALU.mult))
                return ca_ok[j]

            proj(c, 2, e_ca)
            for j in range(2):
                p.wait("dve", ca_ok[j])
                t = p.inc("dve", nc.vector.tensor_scalar(tmp[:, j, :], At[:, j, 0:CH], pc[:, j:j + 1], None, ALU.mult))
                for k in range(1, 3):
                    p.wait("dve", t)
                    t = p.inc("dve", nc.vector.scalar_tensor_tensor(
                        out=tmp[:, j, :], in0=At[:, j, k:k + CH], scalar=pc[:, 2 * k + j:2 * k + j + 1],
                        in1=tmp[:, j, :], op0=ALU.mult, op1=ALU.add))
            p.wait("dve", t)
            ha = p.inc("dve", nc.vector.tensor_copy(At[:, :, 0:2], At[:, :, CH:CH + 2]))
            halo["A"] = [ha]

            def e_ba(j, ps, t):
                p.wait("dve", t, ha, *fr("yT"))
                Y[j] = p.inc("dve", nc.vector.tensor_tensor(yT[:, j, :], ps[:, :], tmp[:, j, :], ALU.mult))
                return Y[j]

            for j in range(2):
                s = MS.next()
                p.wait("pe", cn_ok, *s.free)
                for i in range(2):
                    t = nc.tensor.matmul(s.ap[:, :], pw[:, i, j * 128:(j + 1) * 128], acc[:, i, :],
                                         start=(i == 0), stop=(i == 1))
                t = p.inc("pe", t)
                p.wait("act", t, *fr("yT"))
                Y[6 + j] = p.inc("act", nc.scalar.copy(yT[:, 6 + j, :], s.ap[:, :]))
                s.free = [Y[6 + j]]
            free["acc"] = [t]
            proj(c, 1, e_ba)
            free["tmp"] = [Y[1]]
            cross(2)

            w, x = issued[(c, 4)], xTs[c % 2]
            p.wait("pe", *w.full)
            vb = []
            for pr in range(2):
                s = PR.next()
                p.wait("pe", *s.free)
                for m in range(2):
                    for k in range(8):
                        t = nc.tensor.matmul(s.ap[:, m * 256:(m + 1) * 256],
                                             x.ap[:, k, (2 * pr + m) * 128:(2 * pr + m + 1) * 128], w.ap[:, k, :],
                                             start=(k == 0), stop=(k == 7))
                t = p.inc("pe", t)
                p.wait("act", t, *fr("gvn"))
                u = p.inc("act", nc.scalar.activation(gvn[:, 2 * pr:2 * pr + 2, :].rearrange("p a b -> p (a b)"),
                                                      s.ap[:, :], ACT.Gelu_apprx_tanh))
                s.free = [u]
                vb.append(u)
            w.free = [t]
            issue(nl[0])
            nl[0] += 1
            gu_ok = {}

            def e_u(j, ps, t):
                p.wait("act", t, *free["tmp"])
                gu_ok[j] = p.inc("act", nc.scalar.activation(tmp[:, j, :], ps[:, :], ACT.Gelu_apprx_tanh))
                return gu_ok[j]

            proj(c, 3, e_u)
            p.wait("dve", *vb)
            for m in range(4):
                t = p.inc("dve", nc.vector.bn_stats(st[:, 16 + 6 * m:22 + 6 * m], gvn[:, m, :]))
            p.wait("dve", t)
            for m in range(4):
                t = p.inc("dve", nc.vector.bn_aggr(st[:, 40 + 2 * m:42 + 2 * m], st[:, 16 + 6 * m:22 + 6 * m]))
            p.wait("act", t)
            t = p.inc("act", nc.scalar.activation(st[:, 48:52], st[:, 41:48:2], ACT.Sqrt, bias=eps_ln[:], scale=1.0))
            p.wait("dve", t)
            t = p.inc("dve", nc.vector.reciprocal(st[:, 52:56], st[:, 48:52]))
            p.wait("dve", t)
            for m in range(4):
                t = p.inc("dve", nc.vector.tensor_scalar(gvn[:, m, :], gvn[:, m, :], st[:, 40 + 2 * m:41 + 2 * m],
                                                         st[:, 52 + m:53 + m], ALU.subtract, ALU.mult))
                p.wait("pool", t)
                t = p.inc("pool", nc.gpsimd.tensor_tensor(gvn[:, m, :], gvn[:, m, :], lngb[:, 0, :], ALU.mult))
                p.wait("pool", t)
                vn_ok = p.inc("pool", nc.gpsimd.tensor_tensor(gvn[:, m, :], gvn[:, m, :], lngb[:, 1, :], ALU.add))
            cross(3)

            def gate(g, ys):
                def e_g(j, ps, t):
                    y = ys[j]
                    p.wait("act", t, *fr("tmp2"))
                    u = p.inc("act", nc.scalar.activation(tmp2[:, j, 0:CH], ps[:, :], ACT.Silu))
                    p.wait("dve", u, Y[y])
                    Y[y] = p.inc("dve", nc.vector.tensor_tensor(yT[:, y, :], yT[:, y, :], tmp2[:, j, 0:CH], ALU.mult))
                    free["tmp2"] = [Y[y]]
                    return u
                proj(c, g, e_g)

            gate(9, [0, 1])
            for m in range(4):
                s = MS.next()
                p.wait("pe", vn_ok, wsg_ok, *s.free)
                for h in range(4):
                    lo = 64 * (h % 2)
                    t = nc.tensor.matmul(s.ap[lo:lo + 64, (h // 2) * 128:(h // 2 + 1) * 128],
                                         gvn[:, m, h * 64:(h + 1) * 64], wsg[:, h, :], start=True, stop=True,
                                         skip_group_check=True)
                t = p.inc("pe", t)
                p.wait("dve", t, *fr("yT"))
                u = p.inc("dve", nc.vector.tensor_tensor(yT[:, 2:4, m * 128:(m + 1) * 128],
                                                         s.ap[:, 0:256].rearrange("p (a b) -> p a b", a=2),
                                                         sgb[:], ALU.add))
                s.free = [u]
            free["gvn"] = [t]
            p.wait("dve", gu_ok[0], gu_ok[1], u)
            for j in range(2):
                Y[2 + j] = p.inc("dve", nc.vector.tensor_tensor(yT[:, 2 + j, :], yT[:, 2 + j, :], tmp[:, j, :], ALU.mult))
            free["tmp"] = [Y[3]]
            if c < 3:
                x = xTs[(c + 1) % 2]
                p.wait("sp", *x.free)
                x.full = [p.dma("sp", x, x.ap, A["xT"][:, :, (c + 1) * CH:(c + 2) * CH])]
            for g in range(10, 14):
                gate(g, [2 * (g - 9), 2 * (g - 9) + 1])

            for m in range(4):
                xs = xrs.next()
                tok = (4 * c + m) * 128
                p.wait("sp", *xs.free)
                xs.full = [p.dma("sp", xs, xs.ap, A["x"][tok:tok + 128, :])]
                hs = h0s.next()
                for n in range(2):
                    s = MS.next()
                    p.wait("pe", *s.free, *[Y[i] for i in range(10)], *wos.full)
                    for k in range(10):
                        t = nc.tensor.matmul(s.ap[:, :], yT[:, k, m * 128:(m + 1) * 128], wo[:, k, n * 512:(n + 1) * 512],
                                             start=(k == 0), stop=(k == 9))
                    t = p.inc("pe", t)
                    p.wait("dve", t, *xs.full)
                    u = p.inc("dve", nc.vector.scalar_tensor_tensor(
                        out=xs.ap[:, n * 512:(n + 1) * 512], in0=xs.ap[:, n * 512:(n + 1) * 512], scalar=ALPHA,
                        in1=s.ap[:, :], op0=ALU.mult, op1=ALU.add))
                    s.free = [u]
                free["yT"] = [t]
                t = layer_norm(p, xs.ap, 1024, 128, st[:, 16:28], st[:, 56:58], st[:, 58:59], st[:, 59:60], eps_ln,
                               xs.ap, LN[:, 0, :], LN[:, 1, :], [u], [], "pool")
                t = layer_norm(p, xs.ap, 1024, 128, st[:, 28:40], st[:, 60:62], st[:, 62:63], st[:, 63:64], eps_ln,
                               hs.ap, LN[:, 2, :], LN[:, 3, :], [t], hs.free, "pool")
                xs.free = [t]
                p.wait("sp", t)
                hs.free = [p.dma("sp", hs, h0d[tok:tok + 128, :], hs.ap)]
        xs, hs = xrs.next(), h0s.next()
        p.wait("sp", *xs.free)
        xs.full = [p.dma("sp", xs, xs.ap[0:NM, :], A["meta"])]
        t = layer_norm(p, xs.ap, 1024, NM, st[:, 16:28], st[:, 56:58], st[:, 58:59], st[:, 59:60], eps_ln,
                       hs.ap, LN[:, 2, :], LN[:, 3, :], xs.full, hs.free, "pool")
        p.wait("sp", t)
        hs.free = [p.dma("sp", hs, h0d[S:L, :], hs.ap[0:NM, :])]
        p.close()


NT = 17


class KV:
    pass


def alloc_kv(nc, ctx):
    kv = KV()

    def sb(name, shape):
        return ctx.enter_context(nc.sbuf_tensor("kv_" + name, shape, F32))

    kv.kn = sb("kn", [128, 4, L])
    kv.kr = sb("kr", [128, L])
    kv.v = sb("v", [128, NT, 512])
    kv.kg = sb("kg", [128, 2, L])
    kv.vg = sb("vg", [128, NT, 256])
    return kv


def phase_project(p, A, h0d, qTd, kv, ident, eps_rms):
    nc = p.nc
    with ExitStack() as ctx:
        def sb(name, shape, dt=F32):
            return ctx.enter_context(nc.sbuf_tensor("p_" + name, shape, dt))

        banks = [ctx.enter_context(nc.psum_tensor(f"p_ps{i}", [128, 512], F32)) for i in range(8)]
        B = Ring([Slot(b) for b in banks])
        w2 = sb("w2", [128, 8, 1472])
        wqb = sb("wqb", [128, 2, 768])
        wkvb = sb("wkvb", [128, 1024])
        pc = sb("pc", [128, 3])
        gg = sb("gg", [128, 2, 128])
        ht = sb("ht", [128, 1, 1024])
        hT = sb("hT", [128, 8, 128])
        rp = sb("rp", [128, 384])
        an = sb("an", [128, 384])
        aT = sb("aT", [128, 3, 128])
        ra = sb("ra", [128, 1024])
        rb = sb("rb", [128, 1024])
        qt = sb("qt", [128, 10, 128])
        sq = sb("sq", [128, 256])
        st = sb("st", [128, 32])

        cslot = Slot(None, p.slot_sem("p_const"))
        for dst, src in ((pc[:], A["pc"][:, PC_GQA:PC_N]), (gg[:, 0, :], bcast(A["g_q_gqa_2"], 128)),
                         (gg[:, 1, :], bcast(A["g_k_gqa_2"], 128)), (wqb[:], A["wqb"]), (wkvb[:], A["wkvb"])):
            cok = p.dma("act", cslot, dst, src)
        w2s = [Slot(None, p.slot_sem(f"p_w2{i}")) for i in range(2)]
        hts = Ring([Slot(ht[:, 0], p.slot_sem("p_ht0"))])
        rps = Slot(rp[:], p.slot_sem("p_rp"))
        qts = Slot(qt[:], p.slot_sem("p_qt"))

        def load(i):
            n = 128 if i < 16 else NM
            s = hts.next()
            p.wait("sp", *s.free)
            s.full = [p.dma("sp", s, s.ap[0:n, :], h0d[i * 128:i * 128 + n, :])]
            return s

        cur = load(0)
        for i in range(2):
            w2s[i].full = [p.dma("sp", w2s[i], w2[:, 4 * i:4 * i + 4, :], A["w2"][:, 4 * i:4 * i + 4, :])]
        for e in ("pe", "dve", "act", "pool"):
            p.wait(e, cok)
        free = {}

        def fr(n):
            return free.get(n, [])

        def evac(e, dst, src, *toks):
            p.wait(e, *toks)
            if e == "act":
                return p.inc("act", nc.scalar.copy(dst, src))
            return p.inc("dve", nc.vector.tensor_copy(dst, src))

        for i in range(NT):
            n = 128 if i < 16 else NM
            p.wait("sp", *rps.free)
            rps.full = [p.dma("sp", rps, rp[:], A["rope"][i])]
            tt = []
            for hf in range(2):
                s = B.next()
                p.wait("pe", *cur.full, *s.free)
                for k in range(4):
                    t = nc.tensor.transpose(s.ap[:, k * 128:k * 128 + n],
                                            cur.ap[0:n, (4 * hf + k) * 128:(4 * hf + k + 1) * 128], ident[0:n, 0:n])
                t = p.inc("pe", t)
                e = ("act", "dve")[hf]
                s.free = [evac(e, hT[:, 4 * hf:4 * hf + 4, 0:n],
                               s.ap[:, :].rearrange("p (a b) -> p a b", a=4)[:, :, 0:n], t, *fr("hT"))]
                tt += s.free
            cur.free = [t]
            if i + 1 < NT:
                cur = load(i + 1)
            zs = []
            for lo, w in ((0, 448), (448, 512), (960, 512)):
                s = B.next()
                p.wait("pe", *tt, *w2s[0].full, *w2s[1].full, *s.free)
                for k in range(8):
                    t = nc.tensor.matmul(s.ap[0:n, 0:w], hT[:, k, 0:n], w2[:, k, lo:lo + w], start=(k == 0), stop=(k == 7))
                zs.append((s, p.inc("pe", t)))
            free["hT"] = [zs[-1][1]]
            (z0, t0), (z1, t1), (z2, t2) = zs
            p.wait("act", t0, *fr("st"))
            parts = [(z0, 0, 256), (z0, 256, 128)] + [(z1, 128 * h, 128) for h in range(4)] + [(z2, 128 * h, 128) for h in range(2)]
            for m, (z, lo, w) in enumerate(parts):
                if m == 2:
                    p.wait("act", t1)
                if m == 6:
                    p.wait("act", t2)
                if m:
                    p.wait("act", u)
                u = p.inc("act", nc.scalar.activation(sq[0:n, 0:w], z.ap[0:n, lo:lo + w], ACT.Square, accum_out=st[0:n, m:m + 1]))
            u = p.inc("act", nc.scalar.copy(kv.vg[0:n, i, :], z2.ap[0:n, 256:512]))
            p.wait("act", u)
            p.inc("act", nc.scalar.activation(st[0:n, 8:9], st[0:n, 0:1], ACT.Sqrt, bias=eps_rms[0:n, :], scale=1.0 / 256))
            u = p.inc("act", nc.scalar.activation(st[0:n, 9:16], st[0:n, 1:8], ACT.Sqrt, bias=eps_rms[0:n, :], scale=1.0 / 128))
            p.wait("dve", u)
            r = p.inc("dve", nc.vector.reciprocal(st[0:n, 16:24], st[0:n, 8:16]))
            p.wait("act", r, *fr("an"))
            p.inc("act", nc.scalar.activation(an[0:n, 0:256], z0.ap[0:n, 0:256], ACT.Copy, scale=st[0:n, 16:17]))
            ua = p.inc("act", nc.scalar.activation(an[0:n, 256:384], z0.ap[0:n, 256:384], ACT.Copy, scale=st[0:n, 17:18]))
            p.wait("dve", *rps.full)

            def rot(dst, tmp, src, heads, w, c0, s0, e, toks):
                p.wait(e, *toks)
                eng = p.eng[e]
                h_ = w // 64
                cb = rp[0:n, c0:c0 + w].unsqueeze(1).to_broadcast([n, heads, w])
                t = p.inc(e, eng.tensor_tensor(dst, src, cb, ALU.mult))
                s4 = src.rearrange("p h (f two c) -> p h f two c", f=h_, two=2)
                t4 = tmp.rearrange("p h (f two c) -> p h f two c", f=h_, two=2)
                sv = rp[0:n, s0:s0 + w].rearrange("p (f two c) -> p f two c", f=h_, two=2)
                for a in range(2):
                    for f in range(h_):
                        sb_ = sv[:, f, a, :].unsqueeze(1).to_broadcast([n, heads, 32])
                        t = p.inc(e, eng.tensor_tensor(t4[:, :, f, a, :], s4[:, :, f, 1 - a, :], sb_, ALU.mult))
                p.wait(e, t)
                return p.inc(e, eng.tensor_tensor(dst, dst, tmp, ALU.add))

            kr3 = ra[0:n, 0:64].rearrange("p (h w) -> p h w", h=1)
            t = rot(kr3, rb[0:n, 0:64].rearrange("p (h w) -> p h w", h=1),
                    z0.ap[0:n, 384:448].rearrange("p (h w) -> p h w", h=1), 1, 64, 0, 64, "dve", [ua, *fr("ra")])
            p.wait("dve", t)
            krt = p.inc("dve", nc.vector.tensor_copy(ra[0:n, 64:128], ra[0:n, 0:64]))
            z0.free = [krt, ua]
            rq = st[0:n, 18:22].unsqueeze(2).to_broadcast([n, 4, 128])
            rk = st[0:n, 22:24].unsqueeze(2).to_broadcast([n, 2, 128])
            xg = ra[0:n, 256:1024].rearrange("p (h w) -> p h w", h=6)
            p.wait("dve", *fr("xg"))
            a1 = p.inc("dve", nc.vector.tensor_tensor(xg[:, 0:4, :], z1.ap[0:n, :].rearrange("p (h w) -> p h w", h=4), rq, ALU.mult))
            a2 = p.inc("dve", nc.vector.tensor_tensor(xg[:, 4:6, :], z2.ap[0:n, 0:256].rearrange("p (h w) -> p h w", h=2), rk, ALU.mult))
            z1.free = [a1]
            z2.free = [a2]
            p.wait("pool", a2)
            p.inc("pool", nc.gpsimd.tensor_tensor(xg[:, 0:4, :], xg[:, 0:4, :], gg[0:n, 0:1, :].to_broadcast([n, 4, 128]), ALU.mult))
            a2 = p.inc("pool", nc.gpsimd.tensor_tensor(xg[:, 4:6, :], xg[:, 4:6, :], gg[0:n, 1:2, :].to_broadcast([n, 2, 128]), ALU.mult))
            yg = rb[0:n, 256:1024].rearrange("p (h w) -> p h w", h=6)
            yq = rot2(p, yg, xg, rp, n, [a2, *rps.full], fr("yg"))
            free["xg"] = [yq]
            s = B.next()
            p.wait("pe", ua, *s.free)
            for k in range(3):
                t = nc.tensor.transpose(s.ap[:, k * 128:k * 128 + n], an[0:n, k * 128:(k + 1) * 128], ident[0:n, 0:n])
            t = p.inc("pe", t)
            free["an"] = [t]
            p.wait("act", t, *fr("aT"))
            for k in range(3):
                a_ok = p.inc("act", nc.scalar.activation(aT[:, k, 0:n], s.ap[:, k * 128:k * 128 + n], ACT.Copy, scale=pc[:, k:k + 1]))
            s.free = [a_ok]
            s = B.next()
            p.wait("pe", a_ok, *s.free)
            for h in range(4):
                t = nc.tensor.matmul(s.ap[:, h * 128:h * 128 + n], wkvb[:, h * 256:h * 256 + 128], aT[:, 2, 0:n], start=True, stop=True)
            t = p.inc("pe", t)
            s.free = [evac("dve", kv.kn[:, :, i * 128:i * 128 + n],
                           s.ap[:, :].rearrange("p (a b) -> p a b", a=4)[:, :, 0:n], t)]
            s = B.next()
            p.wait("pe", *s.free)
            for h in range(4):
                t = nc.tensor.matmul(s.ap[0:n, h * 128:(h + 1) * 128], aT[:, 2, 0:n], wkvb[:, h * 256 + 128:(h + 1) * 256], start=True, stop=True)
            t = p.inc("pe", t)
            s.free = [evac("act", kv.v[0:n, i, :], s.ap[0:n, :], t)]
            if i < 16:
                s = B.next()
                p.wait("pe", *s.free)
                for h in range(4):
                    for k in range(2):
                        t = nc.tensor.matmul(s.ap[:, h * 128:(h + 1) * 128], wqb[:, k, h * 192:h * 192 + 128], aT[:, k, :],
                                             start=(k == 0), stop=(k == 1))
                t = p.inc("pe", t)
                s.free = [evac("act", qt[:, 0:4, :].rearrange("p a b -> p (a b)"), s.ap[:, :], t, *qts.free)]
                s = B.next()
                p.wait("pe", *s.free)
                for h in range(4):
                    for k in range(2):
                        t = nc.tensor.matmul(s.ap[:, h * 64:(h + 1) * 64], aT[:, k, :], wqb[:, k, h * 192 + 128:(h + 1) * 192],
                                             start=(k == 0), stop=(k == 1))
                t = p.inc("pe", t)
                qr = an[:, 0:256].rearrange("p (h w) -> p h w", h=4)
                qu = rot(qr, rb[:, 0:256].rearrange("p (h w) -> p h w", h=4),
                         s.ap[:, 0:256].rearrange("p (h w) -> p h w", h=4), 4, 64, 0, 64, "dve", [t, krt, *free["an"]])
                s.free = [qu]
            free["aT"] = [t]
            s = B.next()
            p.wait("pe", krt, *s.free)
            t = nc.tensor.transpose(s.ap[:, 0:n], ra[0:n, 0:128], ident[0:n, 0:n])
            if i < 16:
                p.wait("pe", qu)
                for k in range(2):
                    t = nc.tensor.transpose(s.ap[:, 128 + k * 128:256 + k * 128], an[:, k * 128:(k + 1) * 128], ident[:])
            t = p.inc("pe", t)
            free["ra"] = [t]
            free["an"] = [t]
            s.free = [evac("act", kv.kr[:, i * 128:i * 128 + n], s.ap[:, 0:n], t)]
            if i < 16:
                s.free = [evac("act", qt[:, 4:6, :].rearrange("p a b -> p (a b)"), s.ap[:, 128:384], t, *qts.free)]
            s = B.next()
            p.wait("pe", yq, *s.free)
            for k in range(2):
                t = nc.tensor.transpose(s.ap[:, k * 128:k * 128 + n], rb[0:n, 768 + k * 128:896 + k * 128], ident[0:n, 0:n])
            t = p.inc("pe", t)
            s.free = [evac("dve", kv.kg[:, :, i * 128:i * 128 + n],
                           s.ap[:, 0:256].rearrange("p (a b) -> p a b", a=2)[:, :, 0:n], t)]
            if i < 16:
                s = B.next()
                p.wait("pe", *s.free)
                for k in range(4):
                    t = nc.tensor.transpose(s.ap[:, k * 128:(k + 1) * 128], rb[:, 256 + k * 128:384 + k * 128], ident[:])
                t = p.inc("pe", t)
                s.free = [evac("act", qt[:, 6:10, :].rearrange("p a b -> p (a b)"), s.ap[:, :], t)]
                p.wait("sp", *s.free)
                qts.free = [p.dma("sp", qts, qTd[i], qt[:].rearrange("p a b -> p (a b)"))]
            free["yg"] = [t]
            rps.free = [yq, krt] + ([qu] if i < 16 else [])
        p.close()


def rot2(p, out, x, rp, n, toks, out_free):
    eng = p.nc.gpsimd
    p.wait("pool", *toks, *out_free)
    x5 = x.rearrange("p h (f two c) -> p h f two c", f=2, two=2)
    o5 = out.rearrange("p h (f two c) -> p h f two c", f=2, two=2)
    sv = rp[0:n, 256:384].rearrange("p (f two c) -> p f two c", f=2, two=2)
    for a in range(2):
        for f in range(2):
            t = p.inc("pool", eng.tensor_tensor(o5[:, :, f, a, :], x5[:, :, f, 1 - a, :],
                                                sv[:, f, a, :].unsqueeze(1).to_broadcast([n, 6, 32]), ALU.mult))
    p.wait("pool", t)
    t = p.inc("pool", eng.tensor_tensor(x, x, rp[0:n, 128:256].unsqueeze(1).to_broadcast([n, 6, 128]), ALU.mult))
    p.wait("pool", t)
    return p.inc("pool", eng.tensor_tensor(out, out, x, ALU.add))


def phase_attend(p, qTd, od, yd, kv, ident):
    nc = p.nc
    with ExitStack() as ctx:
        def sb(name, shape, dt=F32):
            return ctx.enter_context(nc.sbuf_tensor("a_" + name, shape, dt))

        banks = [ctx.enter_context(nc.psum_tensor(f"a_ps{i}", [128, 512], F32)) for i in range(8)]
        SB = [Slot(b) for b in banks[0:4]]
        X = Slot(banks[4][:, 0:16])
        TB = Ring([Slot(banks[5]), Slot(banks[6])])
        OB = Slot(banks[7])
        P = sb("P", [128, 2, L])
        Ps = [Slot(P[:, i]) for i in range(2)]
        PT = sb("PT", [128, 2, NT * 128])
        PTs = [Slot(PT[:, i]) for i in range(2)]
        q = sb("q", [128, 2, 10, 128])
        qs = [Slot(q[:, i], p.slot_sem(f"a_q{i}")) for i in range(2)]
        o = sb("o", [128, 2, 1024])
        os_ = [Slot(o[:, i], p.slot_sem(f"a_o{i}")) for i in range(2)]
        sc = sb("sc", [128, 2, 32])
        scs = [Slot(sc[:, i]) for i in range(2)]

        def load(i):
            s = qs[i % 2]
            p.wait("sp", *s.free)
            s.full = [p.dma("sp", s, s.ap.rearrange("p a b -> p (a b)"), qTd[i])]

        load(0)
        load(1)
        zt = sb("zt", [128, 4096])
        zs = Slot(None, p.slot_sem("a_zt"))
        zok = p.inc("pool", nc.gpsimd.memset(zt[:], 0.0))
        p.wait("sp", zok)
        for b in range(64, YB, 4):
            p.dma("sp", zs, yd[b * 128:(b + 4) * 128, :].rearrange("(p a) n -> p (a n)", a=4), zt[:])
        steps = [(i, h) for i in range(16) for h in range(8)]

        def scores(m):
            i, h = steps[m]
            s = qs[i % 2]
            p.wait("pe", *s.full)
            toks = []
            for c in range(5):
                b = SB[c] if c < 4 else X
                lo, w = c * 512, (512 if c < 4 else NM)
                p.wait("pe", *b.free)
                if h < 4:
                    r = 64 * (h % 2)
                    nc.tensor.matmul(b.ap[:, 0:w], s.ap[:, h, :], kv.kn[:, h, lo:lo + w], start=True, stop=False)
                    t = nc.tensor.matmul(b.ap[:, 0:w], s.ap[r:r + 64, 4 + h // 2, :], kv.kr[r:r + 64, lo:lo + w],
                                         start=False, stop=True)
                else:
                    t = nc.tensor.matmul(b.ap[:, 0:w], s.ap[:, 2 + h, :], kv.kg[:, (h - 4) // 2, lo:lo + w], start=True, stop=True)
                toks.append(p.inc("pe", t))
            if h == 7:
                s.free = [toks[-1]]
                if i + 2 < 16:
                    load(i + 2)
            return toks

        def softmax(m, toks):
            i, h = steps[m]
            scale = SQK_M if h < 4 else SQK_G
            z, P_ = scs[m % 2], Ps[m % 2]
            p.wait("dve", *z.free)
            for c in range(5):
                b = SB[c] if c < 4 else X
                w = 512 if c < 4 else NM
                p.wait("dve", toks[c])
                t = p.inc("dve", nc.vector.tensor_reduce(z.ap[:, c:c + 1], b.ap[:, 0:w], AX, ALU.max))
            p.wait("dve", t)
            t = p.inc("dve", nc.vector.tensor_reduce(z.ap[:, 5:6], z.ap[:, 0:5], AX, ALU.max))
            p.wait("dve", t)
            t = p.inc("dve", nc.vector.tensor_scalar(z.ap[:, 6:7], z.ap[:, 5:6], -scale, None, ALU.mult))
            p.wait("act", t, *P_.free)
            P_.full = []
            for c in range(5):
                b = SB[c] if c < 4 else X
                w = 512 if c < 4 else NM
                u = p.inc("act", nc.scalar.activation(P_.ap[:, c * 512:c * 512 + w], b.ap[:, 0:w], ACT.Exp, bias=z.ap[:, 6:7],
                                                      scale=scale, accum_out=z.ap[:, 8 + c:9 + c]))
                b.free = [u]
                P_.full.append(u)
            z.full = [u]

        def turn(m):
            P_, T = Ps[m % 2], PTs[m % 2]
            T.full = []
            for c in range(5):
                s = TB.next()
                k = 4 if c < 4 else 1
                n = 128 if c < 4 else NM
                p.wait("pe", P_.full[c], *s.free)
                for a in range(k):
                    t = nc.tensor.transpose(s.ap[0:n, a * 128:(a + 1) * 128], P_.ap[:, c * 512 + a * 128:c * 512 + a * 128 + n], ident[:])
                t = p.inc("pe", t)
                e = ("act", "dve")[c % 2] if c < 4 else "dve"
                p.wait(e, t, *T.free)
                dst, src = T.ap[0:n, c * 512:c * 512 + k * 128], s.ap[0:n, 0:k * 128]
                u = p.inc(e, nc.scalar.copy(dst, src) if e == "act" else nc.vector.tensor_copy(dst, src))
                s.free = [u]
                T.full.append(u)
            P_.free = [t]

        def values(m):
            i, h = steps[m]
            T, z, O = PTs[m % 2], scs[m % 2], os_[i % 2]
            p.wait("pe", *OB.free)
            for j in range(NT):
                n = 128 if j < 16 else NM
                p.wait("pe", T.full[j // 4])
                v = kv.v[0:n, j, h * 128:(h + 1) * 128] if h < 4 else kv.vg[0:n, j, (h - 4) // 2 * 128:((h - 4) // 2 + 1) * 128]
                t = nc.tensor.matmul(OB.ap[:, 0:128], T.ap[0:n, j * 128:(j + 1) * 128], v, start=(j == 0), stop=(j == NT - 1))
            t = p.inc("pe", t)
            T.free = [t]
            p.wait("dve", *z.full)
            u = p.inc("dve", nc.vector.tensor_reduce(z.ap[:, 14:15], z.ap[:, 8:13], AX, ALU.add))
            p.wait("dve", u)
            u = p.inc("dve", nc.vector.reciprocal(z.ap[:, 15:16], z.ap[:, 14:15]))
            p.wait("dve", u, t, *O.free)
            u = p.inc("dve", nc.vector.tensor_scalar(O.ap[:, h * 128:(h + 1) * 128], OB.ap[:, 0:128], z.ap[:, 15:16], None, ALU.mult))
            OB.free = [u]
            z.free = [u]
            if h == 7:
                p.wait("sp", u)
                O.free = [p.dma("sp", O, od[i * 128:(i + 1) * 128, :], O.ap)]

        t = scores(0)
        softmax(0, t)
        for m in range(1, len(steps)):
            t = scores(m)
            turn(m - 1)
            softmax(m, t)
            values(m - 1)
        turn(len(steps) - 1)
        values(len(steps) - 1)
        p.close()


class Route:
    pass


def alloc_route(nc):
    r = Route()
    r.slot = nc.alloc_sbuf_tensor("r_slot", [128, 16, 4], U32)
    r.pos = nc.alloc_sbuf_tensor("r_pos", [128, 16, 4], F32)
    r.idf = nc.alloc_sbuf_tensor("r_idf", [128, 16, 4], F32)
    r.base = nc.alloc_sbuf_tensor("r_base", [128, 32], F32)
    r.gate = nc.alloc_sbuf_tensor("r_gate", [128, 16, 4], F32)
    r.nb = nc.alloc_sbuf_tensor("r_nb", [1, NE], I32)
    r.tot = nc.alloc_sbuf_tensor("r_tot", [1, 1], I32)
    r.cum = nc.alloc_sbuf_tensor("r_cum", [1, NE], I32)
    return r


def phase_route(p, A, h0d, od, h1d, tabd, R, ident, eps_ln, eps_rms, lgd=None):
    nc = p.nc
    with ExitStack() as ctx:
        def sb(name, shape, dt=F32):
            return ctx.enter_context(nc.sbuf_tensor("o_" + name, shape, dt))

        banks = [ctx.enter_context(nc.psum_tensor(f"o_ps{i}", [128, 512], F32)) for i in range(8)]
        B = Ring([Slot(b) for b in banks])
        wo = sb("wo", [128, 8, 1024])
        wr = sb("wr", [128, 8, 32])
        go = sb("go", [128, 1024])
        LN = sb("LN", [128, 2, 1024])
        br = sb("br", [128, 32])
        erow = sb("erow", [128, 32])
        before = sb("before", [128, 128])
        ones = sb("ones", [128, 128])
        tokid = sb("tokid", [128, 16], I32)
        thr = sb("thr", [128, 15])
        zt = sb("zt", [128, NE * CAP // 128], I32)
        ob = sb("ob", [128, 2, 1024])
        hb = sb("hb", [128, 2, 1024])
        h1 = sb("h1", [128, 2, 1024])
        oT = sb("oT", [128, 2, 8, 128])
        sq = sb("sq", [128, 512])
        st = sb("st", [128, 64])
        lg = sb("lg", [128, 2, 32])
        m8 = sb("m8", [128, 8])
        i8 = sb("i8", [128, 8], U32)
        ex = sb("ex", [128, 8])
        oh = sb("oh", [128, 4, 32])
        pr = sb("pr", [128, 4, 32])
        M = sb("M", [128, 32])
        Macc = sb("Macc", [128, 32])
        C = sb("C", [128, 32])
        sf = sb("sf", [128, 4])
        cnt = sb("cnt", [128, 4, 32])
        tb = sb("tb", [128, 32, 15])

        cslot = Slot(None, p.slot_sem("o_const"))
        for dst, src in ((go[:], bcast(A["g_o"], 1024)), (LN[:, 0, :], bcast(A["ln1_g_2"], 1024)),
                         (LN[:, 1, :], bcast(A["ln1_b_2"], 1024)), (br[:], bcast(A["b_router_2"], 32)),
                         (erow[:], A["erow"]), (before[:], A["before"]),
                         (tokid[:], A["tokid"]), (thr[:], A["thr"]), (wr[:], A["wr"]), (wo[:], A["wo2"])):
            cok = p.dma("act", cslot, dst, src)
        z = p.inc("dve", nc.vector.memset(zt[:], 0))
        p.inc("dve", nc.vector.memset(ones[:], 1.0))
        m0 = p.inc("dve", nc.vector.memset(Macc[:], 0.0))
        zs = Slot(None, p.slot_sem("o_zt"))
        p.wait("sp", z)
        tab_ok = p.dma("sp", zs, tabd.rearrange("(p n) o -> p (n o)", p=128), zt[:])
        obs = Ring([Slot(ob[:, i], p.slot_sem(f"o_ob{i}")) for i in range(2)])
        hbs = Ring([Slot(hb[:, i], p.slot_sem(f"o_hb{i}")) for i in range(2)])
        h1s = Ring([Slot(h1[:, i], p.slot_sem(f"o_h1{i}")) for i in range(2)])
        oTs = Ring([Slot(oT[:, i]) for i in range(2)])
        scs = Slot(None, p.slot_sem("o_scatter"))

        def load(i):
            a, b = obs.next(), hbs.next()
            p.wait("sp", *a.free)
            a.full = [p.dma("sp", a, a.ap, od[i * 128:(i + 1) * 128, :])]
            p.wait("sp", *b.free)
            b.full = [p.dma("sp", b, b.ap, h0d[i * 128:(i + 1) * 128, :])]
            return a, b

        def turn(src, ready):
            dst = oTs.next()
            dst.full = []
            for hf in range(2):
                s = B.next()
                p.wait("pe", *ready, *s.free)
                for k in range(4):
                    t = nc.tensor.transpose(s.ap[:, k * 128:(k + 1) * 128], src[:, (4 * hf + k) * 128:(4 * hf + k + 1) * 128], ident[:])
                t = p.inc("pe", t)
                e = ("act", "dve")[hf]
                p.wait(e, t, *dst.free)
                o_ = dst.ap[:, 4 * hf:4 * hf + 4, :].rearrange("p a b -> p (a b)")
                s.free = [p.inc(e, nc.scalar.copy(o_, s.ap[:, :]) if e == "act" else nc.vector.tensor_copy(o_, s.ap[:, :]))]
                dst.full += s.free
            return dst, t

        for e in ("pe", "dve", "act", "pool"):
            p.wait(e, cok, m0)
        free = {}

        def fr(n):
            return free.get(n, [])

        cur = load(0)
        nxt = load(1)
        carry = {"oh": [], "M": [m0]}

        def first(i, a, b):
            p.wait("act", *a.full)
            for hf in range(2):
                if hf:
                    p.wait("act", u)
                u = p.inc("act", nc.scalar.activation(sq[:], a.ap[:, hf * 512:(hf + 1) * 512], ACT.Square, accum_out=st[:, hf:hf + 1]))
            p.wait("act", u)
            u = p.inc("act", nc.scalar.activation(st[:, 2:4], st[:, 0:2], ACT.Sqrt, bias=eps_rms[:], scale=1.0 / 512))
            p.wait("dve", u)
            u = p.inc("dve", nc.vector.reciprocal(st[:, 4:6], st[:, 2:4]))
            p.wait("dve", u)
            for hf in range(2):
                v = a.ap[:, hf * 512:(hf + 1) * 512]
                u = p.inc("dve", nc.vector.scalar_tensor_tensor(out=v, in0=v, scalar=st[:, 4 + hf:5 + hf],
                                                                in1=go[:, hf * 512:(hf + 1) * 512], op0=ALU.mult, op1=ALU.mult))
            T, t = turn(a.ap, [u])
            a.free = [t]
            h = h1s.next()
            for n in range(2):
                s = B.next()
                p.wait("pe", *T.full, *s.free)
                for k in range(8):
                    t = nc.tensor.matmul(s.ap[:, :], T.ap[:, k, :], wo[:, k, n * 512:(n + 1) * 512], start=(k == 0), stop=(k == 7))
                t = p.inc("pe", t)
                p.wait("dve", t, *b.full)
                u = p.inc("dve", nc.vector.scalar_tensor_tensor(
                    out=b.ap[:, n * 512:(n + 1) * 512], in0=b.ap[:, n * 512:(n + 1) * 512], scalar=ALPHA,
                    in1=s.ap[:, :], op0=ALU.mult, op1=ALU.add))
                s.free = [u]
            T.free = [t]
            t = layer_norm(p, b.ap, 1024, 128, st[:, 16:28], st[:, 8:10], st[:, 10:11], st[:, 11:12], eps_ln,
                           h.ap, LN[:, 0, :], LN[:, 1, :], [u], h.free, "pool")
            b.free = [t]
            p.wait("sp", t)
            h.free = [p.dma("sp", h, h1d[i * 128:(i + 1) * 128, :], h.ap)]
            return h, t

        def second(i, h, ok):
            T, t = turn(h.ap, [ok])
            h.free = h.free + [t]
            s = B.next()
            p.wait("pe", *T.full, *s.free)
            for k in range(8):
                t = nc.tensor.matmul(s.ap[:, 0:32], T.ap[:, k, :], wr[:, k, :], start=(k == 0), stop=(k == 7))
            t = p.inc("pe", t)
            T.free = [t]
            l = lg[:, i % 2, :]
            p.wait("dve", t)

            def v(ins):
                tok = p.inc("dve", ins)
                p.wait("dve", tok)
                return tok

            s.free = [v(nc.vector.tensor_tensor(l, s.ap[:, 0:32], br[:], ALU.add))]
            v(nc.vector.max(m8[:], l))
            v(nc.vector.max_index(i8[:], m8[:], l))
            v(nc.vector.tensor_copy(R.idf[:, i, :], i8[:, 0:4]))
            p.wait("dve", *fr("ex"))
            t = v(nc.vector.tensor_scalar(ex[:, 4:5], m8[:, 0:1], -1.0, None, ALU.mult))
            p.wait("act", t)
            g = p.inc("act", nc.scalar.activation(ex[:, 0:4], m8[:, 0:4], ACT.Exp, bias=ex[:, 4:5], scale=1.0, accum_out=ex[:, 5:6]))
            v(nc.vector.tensor_tensor(oh[:], erow[:].unsqueeze(1).to_broadcast([128, 4, 32]),
                                      R.idf[:, i, :].unsqueeze(2).to_broadcast([128, 4, 32]), ALU.is_equal))
            p.wait("dve", *fr("M"))
            t = v(nc.vector.tensor_reduce(M[:], oh[:].rearrange("p k e -> p e k"), AX, ALU.add))
            s = B.next()
            p.wait("pe", t, *s.free, *carry["M"])
            nc.tensor.matmul(s.ap[:, 0:32], before[:], M[:], start=True, stop=False)
            t = p.inc("pe", nc.tensor.matmul(s.ap[:, 0:32], ones[:], Macc[:], start=False, stop=True))
            free["M"] = [t]
            p.wait("dve", t)
            s.free = [v(nc.vector.tensor_copy(C[:], s.ap[:, 0:32]))]
            carry["M"] = [v(nc.vector.tensor_tensor(Macc[:], Macc[:], M[:], ALU.add))]
            v(nc.vector.tensor_tensor(pr[:], oh[:], C[:].unsqueeze(1).to_broadcast([128, 4, 32]), ALU.mult))
            v(nc.vector.tensor_reduce(R.pos[:, i, :], pr[:], AX, ALU.add))
            v(nc.vector.scalar_tensor_tensor(out=sf[:], in0=R.idf[:, i, :], scalar=float(CAP), in1=R.pos[:, i, :],
                                             op0=ALU.mult, op1=ALU.add))
            sl = v(nc.vector.tensor_copy(R.slot[:, i, :], sf[:]))
            p.wait("dve", g)
            v(nc.vector.reciprocal(ex[:, 6:7], ex[:, 5:6]))
            free["ex"] = [v(nc.vector.tensor_scalar(R.gate[:, i, :], ex[:, 0:4], ex[:, 6:7], None, ALU.mult))]
            p.wait("pool", sl, tab_ok)
            for k in range(4):
                nc.gpsimd.indirect_dma_start(
                    out=tabd, out_offset=bass.IndirectOffsetOnAxis(ap=R.slot[:, i, k:k + 1], axis=0),
                    in_=tokid[:, i:i + 1], in_offset=None).then_inc(scs.sem, 16)
                scs.n += 16
                p.dmas.append((scs.sem, scs.n))

        prev = None
        for i in range(16):
            h, ok = first(i, *cur)
            cur = nxt
            if i + 2 < 16:
                nxt = load(i + 2)
            if prev:
                second(*prev)
            prev = (i, h, ok)
        second(*prev)
        s = B.next()
        p.wait("pe", *carry["M"], *s.free)
        t = p.inc("pe", nc.tensor.matmul(s.ap[:, 0:32], ones[:], Macc[:], start=True, stop=True))
        p.wait("dve", t)

        def v(ins):
            tok = p.inc("dve", ins)
            p.wait("dve", tok)

        v(nc.vector.tensor_copy(cnt[:, 0, :], s.ap[:, 0:32]))
        v(nc.vector.tensor_tensor(tb[:], cnt[:, 0, :].unsqueeze(2).to_broadcast([128, 32, 15]),
                                  thr[:].unsqueeze(1).to_broadcast([128, 32, 15]), ALU.is_gt))
        v(nc.vector.tensor_reduce(cnt[:, 1, :], tb[:], AX, ALU.add))
        v(nc.vector.tensor_scalar(cnt[:, 1, :], cnt[:, 1, :], 1.0, None, ALU.add))
        v(nc.vector.tensor_copy(R.nb[:], cnt[0:1, 1, :]))
        v(nc.vector.tensor_tensor_scan(cnt[:, 2, :], ones[:, 0:32], cnt[:, 1, :], 1.0, ALU.mult, ALU.add))
        v(nc.vector.tensor_copy(R.tot[:], cnt[0:1, 2, 31:32]))
        v(nc.vector.tensor_tensor(cnt[:, 3, :], cnt[:, 2, :], cnt[:, 1, :], ALU.subtract))
        v(nc.vector.tensor_copy(R.cum[:], cnt[0:1, 3, :]))
        v(nc.vector.tensor_scalar(R.base[:], cnt[:, 3, :], 128.0, -128.0, ALU.mult, ALU.add))
        p.close()


def phase_experts(p, A, h1d, tabd, yd, R, ident):
    nc = p.nc
    with ExitStack() as ctx:
        def sb(name, shape, dt=F32):
            return ctx.enter_context(nc.sbuf_tensor("e_" + name, shape, dt))

        def sem(name):
            return nc.alloc_semaphore("e_" + name)

        banks = [ctx.enter_context(nc.psum_tensor(f"e_ps{i}", [128, 512], F32)) for i in range(8)]
        G, Yb, Tb = banks[0:4], banks[4:6], banks[6:8]
        w = sb("w", [128, 6, 8, 512])
        bg = sb("bg", [128, 2048])
        bd = sb("bd", [128, 1024])
        idx = sb("idx", [128, 1], I32)
        hx = sb("hx", [128, 1024])
        hT = sb("hT", [128, 8, 128])
        tt = sb("tt", [128, 512])
        gg = sb("gg", [128, 256])
        uu = sb("uu", [128, 256])
        sg = sb("sg", [128, 256])
        act = sb("act", [128, 1024])
        aT = sb("aT", [128, 8, 128])
        Y = sb("Y", [128, 1024])
        junk = sb("junk", [1, 8])

        w_full = [sem(f"w_full{c}") for c in range(6)]
        w_used = [sem(f"w_used{c}") for c in range(6)]
        bg_full, bd_full = sem("bg_full"), sem("bd_full")
        bg_used, bd_used = sem("bg_used"), sem("bd_used")
        idx_seen = sem("idx_seen")
        idx_full = sem("idx_full")
        hx_full, hx_free = sem("hx_full"), sem("hx_free")
        t_full = [sem("t_full0"), sem("t_full1")]
        t_free = [sem("t_free0"), sem("t_free1")]
        hT_full = sem("hT_full")
        g_full = [sem(f"g_full{n}") for n in range(4)]
        g_free = [sem(f"g_free{n}") for n in range(4)]
        glu, sig = sem("glu"), sem("sig")
        act_full = [sem("act_full0"), sem("act_full1")]
        aT_full = sem("aT_full")
        y_full = [sem("y_full0"), sem("y_full1")]
        y_free = [sem("y_free0"), sem("y_free1")]
        out_full, out_free = sem("out_full"), sem("out_free")
        dv = sem("dv")

        def take(eng, s, n=1):
            eng.wait_ge(s, n)
            eng.sem_inc(s, -n)

        sp, pe, dve, act_e, pool = nc.sync, nc.tensor, nc.vector, nc.scalar, nc.gpsimd
        for n in range(4):
            dve.sem_inc(g_free[n], 1)
        for n in range(2):
            dve.sem_inc(y_free[n], 1)
            act_e.sem_inc(t_free[n], 1)
        for c in range(5):
            pe.sem_inc(w_used[c], 1)
        dve.sem_inc(bg_used, 1)
        dve.sem_inc(bd_used, 1)
        act_e.sem_inc(out_free, 16)
        pe.sem_inc(hx_free, 1)

        with sp.Fori(0, NE) as e:
            cum = sp.value_load(R.cum[0:1, bass.ds(e, 1)], min_val=1, max_val=1 + 16 * NE)
            for c in range(6):
                src = A["wgu"][bass.ds(e, 1), c] if c < 4 else A["wdn"][bass.ds(e, 1), c - 4]
                sp.wait_ge(w_used[c], cum)
                sp.dma_start(w[:, c].rearrange("p k n -> p (k n)"), src.rearrange("o p n -> p (o n)")).then_inc(w_full[c], 16)
                if c == 0:
                    sp.wait_ge(bg_used, cum)
                    sp.dma_start(bg[:], A["bgu"][bass.ds(e, 1), :].broadcast_to([128, 2048])).then_inc(bg_full, 16)
                if c == 4:
                    sp.wait_ge(bd_used, cum)
                    sp.dma_start(bd[:], A["bdn"][bass.ds(e, 1), :].broadcast_to([128, 1024])).then_inc(bd_full, 16)

        def gather(at, blocks):
            take(pool, hx_free)
            pool.dma_start(idx[:], tabd[at, :]).then_inc(idx_full, 16)
            pool.wait_ge(idx_full, blocks * 16)
            pool.sem_inc(idx_seen, 1)
            pool.indirect_dma_start(out=hx[:], out_offset=None, in_=h1d,
                                    in_offset=bass.IndirectOffsetOnAxis(ap=idx[:, 0:1], axis=0)).then_inc(hx_full, 16)

        with pool.Fori(0, NE) as e:
            nb = pool.value_load(R.nb[0:1, bass.ds(e, 1)], min_val=1, max_val=16)
            cum = pool.value_load(R.cum[0:1, bass.ds(e, 1)], min_val=1, max_val=1 + 16 * NE)
            with pool.Fori(0, nb) as b:
                gather(bass.ds(e * CAP + b * 128, 128), cum + b)
        gather(slice(0, 128), pool.value_load(R.tot[0:1, 0:1], min_val=1, max_val=2 + 16 * NE))

        def turn_hx(blocks, first=None):
            pe.wait_ge(hx_full, blocks * 16)
            for hf in range(2):
                take(pe, t_free[hf])
                for k in range(4):
                    t = pe.transpose(Tb[hf][:, k * 128:(k + 1) * 128], hx[:, (4 * hf + k) * 128:(4 * hf + k + 1) * 128], ident[:])
                    if hf == 0 and k == 0 and first is not None:
                        t.then_inc(first, 1)
                t.then_inc(t_full[hf], 1)

        turn_hx(1)
        with pe.Fori(0, NE) as e:
            nb = pe.value_load(R.nb[0:1, bass.ds(e, 1)], min_val=1, max_val=16)
            cum = pe.value_load(R.cum[0:1, bass.ds(e, 1)], min_val=1, max_val=1 + 16 * NE)
            with pe.Fori(0, nb) as b:
                take(pe, hT_full)
                for n in range(4):
                    pe.wait_ge(w_full[n], 16)
                    take(pe, g_free[n])
                    for k in range(8):
                        t = pe.matmul(G[n][:, :], hT[:, k, :], w[:, n, k, :], start=(k == 0), stop=(k == 7))
                        if k == 0:
                            t.then_inc(w_used[(n - 1) % 6], 1)
                        if n == 0 and k == 1:
                            t.then_inc(hx_free, 1)
                    t.then_inc(g_full[n], 1)
                turn_hx(cum + b + 1, w_used[3])
                for hf in range(2):
                    take(pe, act_full[hf])
                    take(pe, t_free[hf])
                    for k in range(4):
                        t = pe.transpose(Tb[hf][:, k * 128:(k + 1) * 128], act[:, (4 * hf + k) * 128:(4 * hf + k + 1) * 128], ident[:])
                    t.then_inc(t_full[hf], 1)
                take(pe, aT_full)
                for n in range(2):
                    pe.wait_ge(w_full[4 + n], 16)
                    take(pe, y_free[n])
                    for k in range(8):
                        t = pe.matmul(Yb[n][:, :], aT[:, k, :], w[:, 4 + n, k, :], start=(k == 0), stop=(k == 7))
                        if k == 0 and n == 1:
                            t.then_inc(w_used[4], 1)
                    t.then_inc(y_full[n], 1)
            for c in range(6):
                pe.sem_inc(w_full[c], -16)

        def move_T(dst, done):
            for hf in range(2):
                take(act_e, t_full[hf])
                act_e.copy(dst[:, 4 * hf:4 * hf + 4, :].rearrange("p a b -> p (a b)"), Tb[hf][:, :]).then_inc(t_free[hf], 1)

        def ping(s, cell):
            act_e.copy(junk[0:1, cell:cell + 1], ident[0:1, 0:1]).then_inc(s, 1)

        move_T(hT, None)
        ping(hT_full, 5)
        with act_e.Fori(0, NE) as e:
            nb = act_e.value_load(R.nb[0:1, bass.ds(e, 1)], min_val=1, max_val=16)
            cum = act_e.value_load(R.cum[0:1, bass.ds(e, 1)], min_val=1, max_val=YB)
            with act_e.Fori(0, nb) as b:
                for n in range(4):
                    if n == 3:
                        move_T(hT, None)
                        ping(hT_full, 5)
                    take(act_e, glu)
                    act_e.activation(sg[:], gg[:], ACT.Sigmoid, scale=1.702).then_inc(sig, 1)
                move_T(aT, None)
                ping(aT_full, 6)
                take(act_e, out_full)
                act_e.dma_start(yd[bass.ds((cum + b - 1) * 128, 128), :], Y[:]).then_inc(out_free, 16)

        def link(ins):
            ins.then_inc(dv, 1)
            take(dve, dv)

        def tell(s, cell):
            dve.memset(junk[0:1, cell:cell + 1], 0.0).then_inc(s, 1)

        with dve.Fori(0, NE) as e:
            nb = dve.value_load(R.nb[0:1, bass.ds(e, 1)], min_val=1, max_val=16)
            with dve.Fori(0, nb) as b:
                dve.wait_ge(bg_full, 16)
                for n in range(4):
                    take(dve, g_full[n])
                    dve.tensor_tensor(tt[:], G[n][:, :], bg[:, n * 512:(n + 1) * 512], ALU.add).then_inc(g_free[n], 1)
                    link(dve.memset(junk[0:1, 3:4], 0.0))
                    dve.tensor_scalar(gg[:], tt[:, 0:256], 7.0, None, ALU.min).then_inc(glu, 1)
                    link(dve.tensor_scalar(uu[:], tt[:, 256:512], 7.0, -7.0, ALU.min, ALU.max))
                    link(dve.scalar_tensor_tensor(out=uu[:], in0=uu[:], scalar=1.0, in1=gg[:], op0=ALU.add, op1=ALU.mult))
                    take(dve, sig)
                    t = dve.tensor_tensor(act[:, n * 256:(n + 1) * 256], uu[:], sg[:], ALU.mult)
                    if n % 2:
                        t.then_inc(act_full[n // 2], 1)
                tell(bg_used, 0)
                dve.wait_ge(bd_full, 16)
                take(dve, out_free, 16)
                for n in range(2):
                    take(dve, y_full[n])
                    dve.tensor_tensor(Y[:, n * 512:(n + 1) * 512], Yb[n][:, :], bd[:, n * 512:(n + 1) * 512], ALU.add).then_inc(y_free[n], 1)
                tell(out_full, 1)
                tell(bd_used, 2)
            dve.sem_inc(bg_full, -16)
            dve.sem_inc(bd_full, -16)
        dve.wait_ge(out_free, 16)
        dve.wait_ge(hT_full, 1)
        p.inc("dve", dve.memset(junk[0:1, 4:5], 0.0))
        p.close()


def phase_combine(p, A, h1d, yd, R, out, eps_ln):
    nc = p.nc
    with ExitStack() as ctx:
        def sb(name, shape, dt=F32):
            return ctx.enter_context(nc.sbuf_tensor("c_" + name, shape, dt))

        LN = sb("LN", [128, 2, 1024])
        y = sb("y", [128, 8, 1024])
        h = sb("h", [128, 3, 1024])
        o = sb("o", [128, 2, 1024])
        st = sb("st", [128, 2, 32])
        cslot = Slot(None, p.slot_sem("c_const"))
        p.dma("act", cslot, LN[:, 0, :], bcast(A["ln2_g_2"], 1024))
        cok = p.dma("act", cslot, LN[:, 1, :], bcast(A["ln2_b_2"], 1024))
        for e in ("dve", "pool"):
            p.wait(e, cok)
        ys = Ring([Slot(y[:, i], p.slot_sem(f"c_y{i}")) for i in range(8)])
        hs = Ring([Slot(h[:, i], p.slot_sem(f"c_h{i}")) for i in range(3)])
        os_ = Ring([Slot(o[:, i], p.slot_sem(f"c_o{i}")) for i in range(2)])
        erow = sb("erow", [128, 32])
        eq = sb("eq", [128, 64, 32])
        eok = p.dma("act", cslot, erow[:], A["erow"])
        p.wait("dve", eok)

        def v(ins):
            tok = p.inc("dve", ins)
            p.wait("dve", tok)
            return tok

        v(nc.vector.tensor_tensor(eq[:], erow[:].unsqueeze(1).to_broadcast([128, 64, 32]),
                                  R.idf[:].rearrange("p a b -> p (a b)").unsqueeze(2).to_broadcast([128, 64, 32]), ALU.is_equal))
        v(nc.vector.tensor_tensor(eq[:], eq[:], R.base[:].unsqueeze(1).to_broadcast([128, 64, 32]), ALU.mult))
        sf = sb("sf", [128, 64])
        v(nc.vector.tensor_reduce(sf[:], eq[:], AX, ALU.add))
        v(nc.vector.tensor_tensor(sf[:], sf[:], R.pos[:].rearrange("p a b -> p (a b)"), ALU.add))
        sl = v(nc.vector.tensor_copy(R.slot[:].rearrange("p a b -> p (a b)"), sf[:]))
        p.wait("pool", sl)
        loaded = {}

        def load(i):
            a = hs.next()
            p.wait("sp", *a.free)
            a.full = [p.dma("sp", a, a.ap, h1d[i * 128:(i + 1) * 128, :])]
            g = []
            for k in range(4):
                s = ys.next()
                p.wait("pool", *s.free)
                nc.gpsimd.indirect_dma_start(out=s.ap, out_offset=None, in_=yd[0:YB * 128, :],
                                             in_offset=bass.IndirectOffsetOnAxis(ap=R.slot[:, i, k:k + 1], axis=0)).then_inc(s.sem, 16)
                s.n += 16
                s.full = [(s.sem, s.n)]
                p.dmas.append((s.sem, s.n))
                g.append(s)
            loaded[i] = (a, g)

        load(0)
        load(1)
        for i in range(16):
            a, g = loaded[i]
            p.wait("dve", *a.full)
            t = p.inc("dve", nc.vector.tensor_scalar(a.ap, a.ap, ALPHA, None, ALU.mult))
            for k, s in enumerate(g):
                p.wait("dve", t, *s.full)
                t = p.inc("dve", nc.vector.scalar_tensor_tensor(out=a.ap, in0=s.ap, scalar=R.gate[:, i, k:k + 1], in1=a.ap,
                                                                op0=ALU.mult, op1=ALU.add))
                s.free = [t]
            if i + 2 < 16:
                load(i + 2)
            q = os_.next()
            z = st[:, i % 2, :]
            t = layer_norm(p, a.ap, 1024, 128, z[:, 0:12], z[:, 12:14], z[:, 14:15], z[:, 15:16], eps_ln,
                           q.ap, LN[:, 0, :], LN[:, 1, :], [t], q.free, "dve")
            a.free = [t]
            p.wait("sp", t)
            q.free = [p.dma("sp", q, out[i * 128:(i + 1) * 128, :], q.ap)]
        p.close()


def build(nc, A, out, stop=9, dbg=None):
    p = Prog(nc)
    ident = nc.alloc_sbuf_tensor("ident", [128, 128], F32)
    eps_ln = nc.alloc_sbuf_tensor("eps_ln", [128, 1], F32)
    eps_rms = nc.alloc_sbuf_tensor("eps_rms", [128, 1], F32)
    h0d = nc.dram_tensor("h0d", (L, D), F32).ap()
    isl = Slot(None, p.slot_sem("ident_in"))
    t = p.dma("sp", isl, ident[:], A["ident"])
    a = p.inc("dve", nc.vector.memset(eps_ln[:], LN_EPS))
    b = p.inc("dve", nc.vector.memset(eps_rms[:], RMS_EPS))
    for e in ("pe", "dve", "act", "pool"):
        p.wait(e, t, a, b)
    phase_mixer(p, A, h0d, ident, eps_ln)
    if stop == 1:
        return h0d
    yd = nc.dram_tensor("yd", ((YB + 16) * 128, D), F32).ap()
    qTd = nc.dram_tensor("qTd", (16, 128, 1280), F32).ap()
    od = nc.dram_tensor("od", (S, D), F32).ap()
    with ExitStack() as ctx:
        kv = alloc_kv(nc, ctx)
        phase_project(p, A, h0d, qTd, kv, ident, eps_rms)
        phase_attend(p, qTd, od, yd, kv, ident)
    if stop == 2:
        return
    h1d = nc.dram_tensor("h1d", (S, D), F32).ap()
    tabd = nc.dram_tensor("tabd", (NE * CAP, 1), I32).ap()
    R = alloc_route(nc)
    phase_route(p, A, h0d, od, h1d, tabd, R, ident, eps_ln, eps_rms)
    if stop == 3:
        return
    phase_experts(p, A, h1d, tabd, yd, R, ident)
    if stop == 4:
        return
    phase_combine(p, A, h1d, yd, R, out, eps_ln)


def host_arrays(x, mem, w_in, conv_a_w, sg_ln_g, sg_ln_b, sg_w, sg_b, pool_w, pool_scale, cc_dw_w, cc_dw_b,
                cc_ln_g, cc_ln_b, cc_pw_w, w_kv, w_out, ln_g, ln_b, meta_tokens_2, ln_emb_g_2, ln_emb_b_2,
                w_in_2, g_q_a_2, w_q_b_2, g_kv_a_2, w_kv_b_2, g_q_gqa_2, g_k_gqa_2, g_o_mla_2, g_o_gqa_2,
                w_o_2, ln1_g_2, ln1_b_2, w_router_2, b_router_2, w_gate_up_2, b_gate_up_2, w_down_2,
                b_down_2, ln2_g_2, ln2_b_2):
    def kp(w):
        k = w.shape[0] // 128
        return np.ascontiguousarray(w.reshape(k, 128, -1).transpose(1, 0, 2))

    def cols(v):
        return v.reshape(-1, 128).T

    A = {}
    A["x"] = x[0]
    A["xT"] = kp(x[0].T)
    A["memT"] = kp(mem[0].T)
    A["w1"] = np.ascontiguousarray(w_in[0].reshape(8, 128, 14, 256).transpose(2, 1, 0, 3))
    A["wkv"] = kp(w_kv[0])
    A["wout"] = kp(w_out[0])
    A["sgw"] = np.ascontiguousarray(sg_w[0].transpose(2, 0, 1))
    A["sgb"] = np.ascontiguousarray(np.repeat(sg_b[0], 64, axis=0).reshape(2, 128, 128).transpose(1, 0, 2))
    bd = np.zeros((128, 2, 128), pool_w.dtype)
    for g in range(4):
        lo = 64 * (g % 2)
        bd[lo:lo + 64, g // 2, lo:lo + 64] = pool_w[0, g]
    A["poolw"] = bd
    A["pw"] = kp(cc_pw_w[0])
    A["pc"] = np.ascontiguousarray(np.concatenate(
        [cols(conv_a_w[0]), cols(cc_dw_w[0]), cols(cc_dw_b[0]), cols(cc_ln_g[0]), cols(cc_ln_b[0]),
         cols(pool_scale[0]), cols(g_q_a_2[0]), cols(g_kv_a_2[0])], axis=1))
    for n, v in (("sg_ln_g", sg_ln_g), ("sg_ln_b", sg_ln_b), ("ln_g", ln_g), ("ln_b", ln_b),
                 ("g_q_gqa_2", g_q_gqa_2), ("g_k_gqa_2", g_k_gqa_2), ("ln1_g_2", ln1_g_2), ("ln1_b_2", ln1_b_2),
                 ("ln2_g_2", ln2_g_2), ("ln2_b_2", ln2_b_2), ("b_router_2", b_router_2)):
        A[n] = v[0]
    A["g_o"] = np.concatenate([g_o_mla_2[0], g_o_gqa_2[0]])
    A["ln_emb_g_2"], A["ln_emb_b_2"] = ln_emb_g_2, ln_emb_b_2
    A["meta"] = meta_tokens_2
    A["w2"] = kp(w_in_2[0])
    A["wqb"] = kp(w_q_b_2[0])
    A["wkvb"] = w_kv_b_2[0]
    A["wo2"] = kp(w_o_2[0])
    A["wr"] = kp(w_router_2[0])
    gu = w_gate_up_2[0].reshape(32, 8, 128, 4, 256, 2)
    A["wgu"] = np.ascontiguousarray(gu.transpose(0, 3, 2, 1, 5, 4)).reshape(32, 4, 128, 4096)
    A["bgu"] = np.ascontiguousarray(b_gate_up_2[0].reshape(32, 4, 256, 2).transpose(0, 1, 3, 2)).reshape(32, 2048)
    A["wdn"] = np.ascontiguousarray(w_down_2[0].reshape(32, 8, 128, 2, 512).transpose(0, 3, 2, 1, 4)).reshape(32, 2, 128, 4096)
    A["bdn"] = b_down_2[0]
    return A


def shape_constants():
    C = {}
    f = np.float32
    C["onm"] = np.full((128, 128), 1.0 / 256, f)
    i = np.arange(128)
    C["tri"] = (i[:, None] <= i[None, :]).astype(f)
    C["ident"] = np.eye(128, dtype=f)
    C["before"] = (i[:, None] < i[None, :]).astype(f)
    prc = np.zeros((128, 2, 17), f)
    for g, w in enumerate((2, 4, 8, 16)):
        lo = 64 * (g % 2)
        prc[lo:lo + 64, g // 2, 0:16] = f(1) / np.minimum(np.arange(16) + 1, w).astype(f)
        prc[lo:lo + 64, g // 2, 16] = 1.0 / w
    C["prc"] = prc
    t = np.arange(S)
    pos = np.concatenate([t + NM, np.arange(NM)])
    row = np.concatenate([t // 64, np.full(NM, -1)])
    col = np.concatenate([t % 64, np.arange(NM)])

    def rope(p_, dim):
        inv = f(10000.0) ** (-np.arange(0, dim, 2, dtype=f) / f(dim))
        ang = p_.astype(f)[:, None] * inv[None, :].astype(f)
        return np.cos(ang).astype(f), np.sin(ang).astype(f)

    c1, s1 = rope(pos, 64)
    cr, sr = rope(row, 64)
    cc, sc = rope(col, 64)
    R = np.concatenate([c1, c1, -s1, s1, cr, cr, cc, cc, -sr, sr, -sc, sc], axis=1)
    pad = np.zeros((17 * 128 - L, R.shape[1]), f)
    C["rope"] = np.ascontiguousarray(np.concatenate([R, pad]).reshape(17, 128, 384))
    C["erow"] = np.broadcast_to(np.arange(32, dtype=f), (128, 32)).copy()
    C["thr"] = np.broadcast_to(np.arange(1, 16, dtype=f) * 128, (128, 15)).copy()
    C["tokid"] = np.ascontiguousarray(np.arange(S, dtype=np.int32).reshape(16, 128).T)
    return C


def kernel(**inputs):
    import numpy as _np
    import concourse.bacc as _bacc
    from concourse import mybir as _mybir
    from concourse.bass_utils import run_bass_kernel_spmd as _run

    nc = _bacc.Bacc("TRN2", target_bir_lowering=False, num_devices=1)
    arrays = host_arrays(**{k: _np.asarray(v) for k, v in inputs.items()})
    arrays.update(shape_constants())
    arrays = {"in_" + k: _np.ascontiguousarray(v) for k, v in arrays.items()}
    A = {k[3:]: nc.dram_tensor(k, v.shape, _mybir.dt.from_np(v.dtype), kind="ExternalInput").ap()
         for k, v in arrays.items()}
    out = nc.dram_tensor("out_0", (S, D), _mybir.dt.float32, kind="ExternalOutput").ap()
    build(nc, A, out)
    r = _run(nc, [arrays], core_ids=[0])
    return r.results[0]["out_0"].reshape(1, S, D)
```

```python
from contextlib import ExitStack

import numpy as np

import concourse.bass as bass
from concourse import mybir

ALU = mybir.AluOpType
ACT = mybir.ActivationFunctionType
AX = mybir.AxisListType.X
F32 = mybir.dt.float32
I32 = mybir.dt.int32
U32 = mybir.dt.uint32

S = 2048
D = 1024
NM = 16
L = S + NM
NE = 32
CAP = 2048
GT = 49
YB = 96
ALPHA = 2.0 ** 0.25
LN_EPS = 1e-5
RMS_EPS = 1e-6
CH = 512
SQK_M = 192 ** -0.5
SQK_G = 128 ** -0.5

PC_CONVA, PC_DW, PC_DWB, PC_CLG, PC_CLB, PC_PS, PC_GQA, PC_GKV = 0, 6, 68, 70, 72, 74, 76, 78
PC_N = 79


class Slot:

    def __init__(self, ap, sem=None):
        self.ap, self.sem, self.n = ap, sem, 0
        self.full, self.free = [], []


class Ring:
    def __init__(self, slots):
        self.slots, self.i = slots, 0

    def next(self):
        s = self.slots[self.i % len(self.slots)]
        self.i += 1
        return s


class Prog:

    def __init__(self, nc):
        self.nc = nc
        self.eng = {"pe": nc.tensor, "dve": nc.vector, "act": nc.scalar, "pool": nc.gpsimd, "sp": nc.sync}
        self.nphase = 0
        self.open()

    def open(self):
        self.sem = {e: self.nc.alloc_semaphore(f"s{self.nphase}_{e}") for e in ("pe", "dve", "act", "pool")}
        self.cnt = {e: 0 for e in self.sem}
        self.seen = {}
        self.dmas = []
        self.nphase += 1

    def inc(self, e, ins):
        ins.then_inc(self.sem[e], 1)
        self.cnt[e] += 1
        return (self.sem[e], self.cnt[e])

    def wait(self, e, *toks):
        for sem, n in toks:
            key = (e, sem.name)
            if self.seen.get(key, 0) < n:
                self.eng[e].wait_ge(sem, n)
                self.seen[key] = n

    def slot_sem(self, name):
        return self.nc.alloc_semaphore(name)

    def dma(self, e, slot, out, in_, **kw):
        self.eng[e].dma_start(out, in_, **kw).then_inc(slot.sem, 16)
        slot.n += 16
        t = (slot.sem, slot.n)
        self.dmas.append(t)
        return t

    def close(self):
        last = {}
        for sem, n in self.dmas:
            last[sem.name] = (sem, n)
        ends = list(last.values()) + [(self.sem[e], self.cnt[e]) for e in self.sem if self.cnt[e]]
        for e in self.eng:
            self.wait(e, *ends)
        self.open()


def bcast(ap1d, n):
    return ap1d.rearrange("(o n) -> o n", o=1).broadcast_to([128, n])


def layer_norm(p, x, n, rows, st, mv, sd, rs, eps_t, out, g, b, ready, out_free, eng2="dve"):
    nc = p.nc
    k = max(1, n // 512)
    w = n // k
    p.wait("dve", *ready)
    for i in range(k):
        t = p.inc("dve", nc.vector.bn_stats(st[:rows, i * 6:(i + 1) * 6], x[:rows, i * w:(i + 1) * w]))
    p.wait("dve", t)
    t = p.inc("dve", nc.vector.bn_aggr(mv[:rows, :], st[:rows, 0:6 * k]))
    p.wait("act", t)
    t = p.inc("act", nc.scalar.activation(sd[:rows, :], mv[:rows, 1:2], ACT.Sqrt, bias=eps_t[:rows, :], scale=1.0))
    p.wait("dve", t)
    t = p.inc("dve", nc.vector.reciprocal(rs[:rows, :], sd[:rows, :]))
    p.wait("dve", t, *out_free)
    t = p.inc("dve", nc.vector.tensor_scalar(out[:rows, :n], x[:rows, :n], mv[:rows, 0:1], rs[:rows, 0:1],
                                             ALU.subtract, ALU.mult))
    p.wait(eng2, t)
    t = p.inc(eng2, p.eng[eng2].tensor_tensor(out[:rows, :n], out[:rows, :n], g[:rows, :n], ALU.mult))
    p.wait(eng2, t)
    return p.inc(eng2, p.eng[eng2].tensor_tensor(out[:rows, :n], out[:rows, :n], b[:rows, :n], ALU.add))


def phase_mixer(p, A, h0d, ident, eps_ln):
    nc = p.nc
    with ExitStack() as ctx:
        def sb(name, shape, dt=F32):
            return ctx.enter_context(nc.sbuf_tensor("m_" + name, shape, dt))

        banks = [ctx.enter_context(nc.psum_tensor(f"m_ps{i}", [128, 512], F32)) for i in range(8)]
        PR = Ring([Slot(b) for b in banks[0:3]])
        MS = Ring([Slot(b) for b in banks[3:8]])

        xT = sb("xT", [128, 2, 8, CH])
        xTs = [Slot(xT[:, i], p.slot_sem(f"m_xT{i}")) for i in range(2)]
        NW = 4
        wt = sb("wt", [128, NW, 8, 256])
        W = Ring([Slot(wt[:, i], p.slot_sem(f"m_w{i}")) for i in range(NW)])
        wo = sb("wo", [128, 10, 1024])
        yT = sb("yT", [128, 10, CH])
        pc = sb("pc", [128, PC_N])
        wsg = sb("wsg", [128, 4, 128])
        tri = sb("tri", [128, 128])
        sgb = sb("sgb", [128, 2, 128])
        poolw = sb("poolw", [128, 2, 128])
        pw = sb("pw", [128, 2, 256])
        prc = sb("prc", [128, 2, 17])
        onm = sb("onm", [128, 128])
        lngb = sb("lngb", [128, 2, 256])
        LN = sb("LN", [128, 4, 1024])
        kT = sb("kT", [128, 2, 256])
        vm = sb("vm", [128, 2, 256])
        At = sb("At", [128, 2, 2 + CH])
        Dt = sb("Dt", [128, 2, 30 + CH])
        Ct = sb("Ct", [128, 2, 15 + CH])
        qT = sb("qT", [128, 2, CH])
        acc = sb("acc", [128, 2, CH])
        tmp = sb("tmp", [128, 2, CH])
        tmp2 = sb("tmp2", [128, 2, 15 + CH])
        gvn = sb("gvn", [128, 4, 256])
        pe_ = sb("pe_", [128, 4, 256])
        pT = sb("pT", [128, 8, 128])
        st = sb("st", [128, 64])
        xr = sb("xr", [128, 2, 1024])
        h0 = sb("h0", [128, 1, 1024])

        cs = p.slot_sem("m_const")
        cslot = Slot(None, cs)

        def const(dst, src, e="sp"):
            cslot.full.append(p.dma(e, cslot, dst, src))

        const(pc[:], A["pc"], "act")
        memT = xT[:, 1, 0:4, :].rearrange("p a b -> p (a b)").rearrange("p (k m) -> p k m", k=8)
        wkv = wt[:, 2:4].rearrange("p a k n -> p (a k n)").rearrange("p (k n) -> p k n", k=8)
        const(memT, A["memT"])
        const(wkv, A["wkv"])
        xTs[0].full = [p.dma("sp", xTs[0], xTs[0].ap, A["xT"][:, :, 0:CH])]
        const(onm[:], A["onm"], "act")
        const(wsg[:], A["sgw"], "act")
        const(tri[:], A["tri"], "act")
        const(sgb[:], A["sgb"], "act")
        const(poolw[:], A["poolw"], "act")
        const(pw[:], A["pw"], "act")
        const(prc[:], A["prc"], "act")
        const(lngb[:, 0, :], bcast(A["sg_ln_g"], 256), "act")
        const(lngb[:, 1, :], bcast(A["sg_ln_b"], 256), "act")
        for i, n in enumerate(("ln_g", "ln_b", "ln_emb_g_2", "ln_emb_b_2")):
            const(LN[:, i, :], bcast(A[n], 1024), "act")
        consts = [cslot.full[-1]]
        for e in ("pe", "dve", "act", "pool"):
            p.wait(e, *consts)
        t = p.inc("pool", nc.gpsimd.memset(At[:, :, 0:2], 0.0))
        t = p.inc("pool", nc.gpsimd.memset(Dt[:, :, 0:30], 0.0))
        halo0 = p.inc("pool", nc.gpsimd.memset(Ct[:, :, 0:15], 0.0))
        halo = {"A": [halo0], "D": [halo0], "C": [halo0]}
        t = [p.inc("pool", nc.gpsimd.tensor_tensor(wsg[:, h, :], wsg[:, h, :], tri[:], ALU.mult)) for h in range(4)]
        wsg_ok = t[-1]
        s = MS.next()
        for j in range(2):
            for k in range(8):
                t = nc.tensor.matmul(s.ap[:, j * 256:(j + 1) * 256], wkv[:, k, j * 128:(j + 1) * 128], memT[:, k, :],
                                     start=(k == 0), stop=(k == 7))
        t = p.inc("pe", t)
        p.wait("act", t)
        kv_ok = p.inc("act", nc.scalar.copy(kT[:].rearrange("p a b -> p (a b)"), s.ap[:, :]))
        s.free = [kv_ok]
        s = MS.next()
        for j in range(2):
            for k in range(8):
                t = nc.tensor.matmul(s.ap[:, j * 256:(j + 1) * 256], memT[:, k, j * 128:(j + 1) * 128], wkv[:, k, 256:512],
                                     start=(k == 0), stop=(k == 7))
        kvpe = p.inc("pe", t)
        p.wait("act", kvpe)
        kv_ok = p.inc("act", nc.scalar.copy(vm[:].rearrange("p a b -> p (a b)"), s.ap[:, :]))
        s.free = [kv_ok]
        W.slots[2].free = W.slots[3].free = [kvpe]
        xTs[1].free = [kvpe]

        order = [7, 6, 8, 5, 0, 2, 1, 4, 3, 9, 10, 11, 12, 13]
        loads = [(c, g) for c in range(4) for g in order]
        issued = {}

        def issue(n):
            if n >= len(loads):
                return
            c, g = loads[n]
            s = W.next()
            p.wait("sp", *s.free)
            s.full = [p.dma("sp", s, s.ap, A["w1"][g])]
            issued[(c, g)] = s

        for n in range(NW):
            issue(n)
        wos = Slot(wo[:], p.slot_sem("m_wo"))
        wos.full = [p.dma("sp", wos, wo[:], A["wout"])]
        nl = [NW]

        xrs = Ring([Slot(xr[:, i], p.slot_sem(f"m_xr{i}")) for i in range(2)])
        h0s = Ring([Slot(h0[:, 0], p.slot_sem("m_h00"))])

        def proj(c, g, each):
            w = issued[(c, g)]
            x = xTs[c % 2]
            p.wait("pe", *w.full, *x.full)
            for j in range(2):
                s = PR.next()
                p.wait("pe", *s.free)
                for k in range(8):
                    t = nc.tensor.matmul(s.ap[:, :], w.ap[:, k, j * 128:(j + 1) * 128], x.ap[:, k, :],
                                         start=(k == 0), stop=(k == 7))
                t = p.inc("pe", t)
                s.free = [each(j, s.ap, t)]
            w.free = [t]
            x.free = [t]
            issue(nl[0])
            nl[0] += 1

        sgq = {}
        Y = {}
        free = {}

        def fr(name):
            return free.get(name, [])

        for c in range(4):
            def e_dg(j, ps, t):
                p.wait("act", t, *fr("tmp"))
                sgq[j] = p.inc("act", nc.scalar.activation(tmp[:, j, :], ps[:, :], ACT.Sigmoid))
                return sgq[j]

            proj(c, 7, e_dg)
            dok = {}

            def e_da(j, ps, t):
                p.wait("dve", t, sgq[j], *fr("D"))
                dok[j] = p.inc("dve", nc.vector.tensor_tensor(Dt[:, j, 30:], ps[:, :], tmp[:, j, :], ALU.mult))
                return dok[j]

            proj(c, 6, e_da)
            free["tmp"] = [dok[1]]

            def e_q(j, ps, t):
                p.wait("act", t, *fr("q"))
                sgq["q"] = p.inc("act", nc.scalar.copy(qT[:, j, :], ps[:, :]))
                return sgq["q"]

            proj(c, 8, e_q)
            q_ok = sgq["q"]

            t2 = {}
            for j in range(2):
                p.wait("dve", dok[j], *halo["D"], *fr("acc"))
                t2[j] = p.inc("dve", nc.vector.tensor_scalar(acc[:, j, :], Dt[:, j, 0:CH], pc[:, PC_DW + j:PC_DW + j + 1],
                                                             pc[:, PC_DWB + j:PC_DWB + j + 1], ALU.mult, ALU.add))
            for k in range(1, 31):
                for j in range(2):
                    p.wait("dve", t2[j])
                    t2[j] = p.inc("dve", nc.vector.scalar_tensor_tensor(
                        out=acc[:, j, :], in0=Dt[:, j, k:k + CH], scalar=pc[:, PC_DW + 2 * k + j:PC_DW + 2 * k + j + 1],
                        in1=acc[:, j, :], op0=ALU.mult, op1=ALU.add))
            conv_ok = t2[1]
            p.wait("dve", conv_ok)
            t = p.inc("dve", nc.vector.tensor_copy(Dt[:, :, 0:30], Dt[:, :, CH:CH + 30]))
            halo["D"] = [t]
            free["D"] = [t]

            def cross(m):
                sc = []
                for pr in range(2):
                    s = MS.next()
                    p.wait("pe", *s.free, q_ok, kv_ok)
                    lo = 64 * pr
                    for hh in range(2):
                        t = nc.tensor.matmul(s.ap[:, hh * 256:(hh + 1) * 256], qT[lo:lo + 64, hh, m * 128:(m + 1) * 128],
                                             kT[lo:lo + 64, hh, :], start=True, stop=True)
                    sc.append((s, p.inc("pe", t)))
                free["q"] = [sc[1][1]]
                mx, nb, sm, rc = st[:, 0:4], st[:, 4:8], st[:, 8:12], st[:, 12:16]
                for pr, (s, t) in enumerate(sc):
                    p.wait("dve", t, *fr("nb"))
                    t = p.inc("dve", nc.vector.tensor_reduce(mx[:, pr:4:2],
                                                             s.ap[:, :].rearrange("p (a b) -> p a b", a=2), AX, ALU.max))
                p.wait("dve", t)
                t = p.inc("dve", nc.vector.tensor_scalar(nb, mx, -0.125, None, ALU.mult))
                p.wait("act", t, *fr("pe_"))
                for h in range(4):
                    s = sc[h % 2][0]
                    t = p.inc("act", nc.scalar.activation(pe_[:, h, :], s.ap[:, (h // 2) * 256:(h // 2 + 1) * 256], ACT.Exp,
                                                          bias=nb[:, h:h + 1], scale=0.125, accum_out=sm[:, h:h + 1]))
                    s.free = [t]
                free["nb"] = [t]
                p.wait("dve", t)
                t = p.inc("dve", nc.vector.reciprocal(rc, sm))
                p.wait("dve", t)
                for h in range(4):
                    t = p.inc("dve", nc.vector.tensor_scalar(pe_[:, h, :], pe_[:, h, :], rc[:, h:h + 1], None, ALU.mult))
                pt = []
                for pr in range(2):
                    s = MS.next()
                    p.wait("pe", t, *s.free)
                    for i in range(4):
                        h, j = 2 * pr + i // 2, i % 2
                        u = nc.tensor.transpose(s.ap[:, i * 128:(i + 1) * 128], pe_[:, h, j * 128:(j + 1) * 128], ident[:])
                    u = p.inc("pe", u)
                    p.wait("act", u, *fr("pT"))
                    v = p.inc("act", nc.scalar.copy(pT[:, 4 * pr:4 * pr + 4, :].rearrange("p a b -> p (a b)"), s.ap[:, :]))
                    s.free = [v]
                    pt.append(v)
                free["pe_"] = [u]
                s = MS.next()
                p.wait("pe", *pt, *s.free)
                for h in range(4):
                    lo = 64 * (h % 2)
                    for j in range(2):
                        t = nc.tensor.matmul(s.ap[lo:lo + 64, (h // 2) * 128:(h // 2 + 1) * 128],
                                             vm[:, j, h * 64:(h + 1) * 64], pT[:, 2 * h + j, :],
                                             start=(j == 0), stop=(j == 1), skip_group_check=True)
                t = p.inc("pe", t)
                free["pT"] = [t]
                p.wait("act", t, *fr("yT"))
                t = p.inc("act", nc.scalar.copy(yT[:, 8:10, m * 128:(m + 1) * 128],
                                                s.ap[:, 0:256].rearrange("p (a b) -> p a b", a=2)))
                s.free = [t]
                Y[8] = Y[9] = t

            cok = {}

            def e_xc(j, ps, t):
                p.wait("act", t, *fr("C"))
                cok[j] = p.inc("act", nc.scalar.copy(Ct[:, j, 15:], ps[:, :]))
                return cok[j]

            proj(c, 5, e_xc)
            cross(0)
            N = 15 + CH
            for j in range(2):
                src, off = Ct[:, j, :], 0
                p.wait("pool", cok[j], *halo["C"], *fr("tmp2"))
                w, b = 1, 0
                res = {}
                steps = 2 if j == 0 else 4
                for i in range(steps):
                    lo = 2 * w - 1
                    t = p.inc("pool", nc.gpsimd.tensor_tensor(tmp2[:, b, lo:N], src[:, lo:N], src[:, lo - w:N - w], ALU.add))
                    p.wait("pool", t)
                    src = tmp2[:, b, :]
                    res[2 * w] = (src, t)
                    w *= 2
                    b = 1 - b
                a, z = (2, 4) if j == 0 else (8, 16)
                p.wait("dve", res[z][1], *fr("tmp"))
                for lo, win in ((0, a), (64, z)):
                    src = res[win][0]
                    if c == 0:
                        t = p.inc("dve", nc.vector.tensor_tensor(tmp[lo:lo + 64, j, 0:16], src[lo:lo + 64, 15:31],
                                                                 prc[lo:lo + 64, j, 0:16], ALU.mult))
                        p.wait("dve", t)
                        t = p.inc("dve", nc.vector.tensor_tensor(tmp[lo:lo + 64, j, 0:16], tmp[lo:lo + 64, j, 0:16],
                                                                 Ct[lo:lo + 64, j, 15:31], ALU.subtract))
                    o = 16 if c == 0 else 0
                    t = p.inc("dve", nc.vector.scalar_tensor_tensor(
                        out=tmp[lo:lo + 64, j, o:CH], in0=src[lo:lo + 64, 15 + o:N], scalar=prc[lo:lo + 64, j, 16:17],
                        in1=Ct[lo:lo + 64, j, 15 + o:N], op0=ALU.mult, op1=ALU.subtract))
                free["tmp2"] = [t]
                s = MS.next()
                p.wait("pe", t, *s.free)
                u = p.inc("pe", nc.tensor.matmul(s.ap[:, :], poolw[:, j, :], tmp[:, j, :], start=True, stop=True))
                p.wait("act", u, *fr("yT"))
                Y[4 + j] = p.inc("act", nc.scalar.activation(yT[:, 4 + j, :], s.ap[:, :], ACT.Copy,
                                                             scale=pc[:, PC_PS + j:PC_PS + j + 1]))
                s.free = [Y[4 + j]]
                free["tmp"] = [u]
            p.wait("pool", t)
            t = p.inc("pool", nc.gpsimd.tensor_copy(Ct[:, :, 0:15], Ct[:, :, CH:CH + 15]))
            halo["C"] = [t]
            free["C"] = [t]

            s = MS.next()
            p.wait("pe", conv_ok, *s.free)
            for j in range(2):
                t = nc.tensor.matmul(s.ap[:, :], onm[:], acc[:, j, :], start=(j == 0), stop=(j == 1))
            t = p.inc("pe", t)
            p.wait("dve", t, *fr("D2"))
            for j in range(2):
                t = p.inc("dve", nc.vector.tensor_tensor(acc[:, j, :], acc[:, j, :], s.ap[:, :], ALU.subtract))
            s.free = [t]
            p.wait("act", t, *free["tmp"])
            for j in range(2):
                t = p.inc("act", nc.scalar.activation(tmp[:, j, :], acc[:, j, :], ACT.Square))
            s = MS.next()
            p.wait("pe", t, *s.free)
            for j in range(2):
                t = nc.tensor.matmul(s.ap[:, :], onm[:], tmp[:, j, :], start=(j == 0), stop=(j == 1))
            t = p.inc("pe", t)
            p.wait("act", t)
            t = p.inc("act", nc.scalar.activation(tmp[:, 0, :], s.ap[:, :], ACT.Sqrt, bias=eps_ln[:], scale=1.0))
            s.free = [t]
            p.wait("dve", t)
            t = p.inc("dve", nc.vector.reciprocal(tmp[:, 1, :], tmp[:, 0, :]))
            p.wait("dve", t)
            for j in range(2):
                t = p.inc("dve", nc.vector.tensor_tensor(acc[:, j, :], acc[:, j, :], tmp[:, 1, :], ALU.mult))
            free["tmp"] = [t]
            p.wait("act", t)
            for j in range(2):
                t = p.inc("act", nc.scalar.activation(acc[:, j, :], acc[:, j, :], ACT.Silu,
                                                      bias=pc[:, PC_CLB + j:PC_CLB + j + 1],
                                                      scale=pc[:, PC_CLG + j:PC_CLG + j + 1]))
            cn_ok = t

            xa_ok = {}

            def e_xa(j, ps, t):
                p.wait("act", t, *free["tmp"])
                xa_ok[j] = p.inc("act", nc.scalar.copy(tmp[:, j, :], ps[:, :]))
                return xa_ok[j]

            proj(c, 0, e_xa)
            cross(1)
            ca_ok = {}

            def e_ca(j, ps, t):
                p.wait("dve", t, xa_ok[j], *halo["A"], *fr("A"))
                ca_ok[j] = p.inc("dve", nc.vector.tensor_tensor(At[:, j, 2:], ps[:, :], tmp[:, j, :], ALU.mult))
                return ca_ok[j]

            proj(c, 2, e_ca)
            for j in range(2):
                p.wait("dve", ca_ok[j])
                t = p.inc("dve", nc.vector.tensor_scalar(tmp[:, j, :], At[:, j, 0:CH], pc[:, j:j + 1], None, ALU.mult))
                for k in range(1, 3):
                    p.wait("dve", t)
                    t = p.inc("dve", nc.vector.scalar_tensor_tensor(
                        out=tmp[:, j, :], in0=At[:, j, k:k + CH], scalar=pc[:, 2 * k + j:2 * k + j + 1],
                        in1=tmp[:, j, :], op0=ALU.mult, op1=ALU.add))
            p.wait("dve", t)
            ha = p.inc("dve", nc.vector.tensor_copy(At[:, :, 0:2], At[:, :, CH:CH + 2]))
            halo["A"] = [ha]

            def e_ba(j, ps, t):
                p.wait("dve", t, ha, *fr("yT"))
                Y[j] = p.inc("dve", nc.vector.tensor_tensor(yT[:, j, :], ps[:, :], tmp[:, j, :], ALU.mult))
                return Y[j]

            for j in range(2):
                s = MS.next()
                p.wait("pe", cn_ok, *s.free)
                for i in range(2):
                    t = nc.tensor.matmul(s.ap[:, :], pw[:, i, j * 128:(j + 1) * 128], acc[:, i, :],
                                         start=(i == 0), stop=(i == 1))
                t = p.inc("pe", t)
                p.wait("act", t, *fr("yT"))
                Y[6 + j] = p.inc("act", nc.scalar.copy(yT[:, 6 + j, :], s.ap[:, :]))
                s.free = [Y[6 + j]]
            free["acc"] = [t]
            proj(c, 1, e_ba)
            free["tmp"] = [Y[1]]
            cross(2)

            w, x = issued[(c, 4)], xTs[c % 2]
            p.wait("pe", *w.full)
            vb = []
            for pr in range(2):
                s = PR.next()
                p.wait("pe", *s.free)
                for m in range(2):
                    for k in range(8):
                        t = nc.tensor.matmul(s.ap[:, m * 256:(m + 1) * 256],
                                             x.ap[:, k, (2 * pr + m) * 128:(2 * pr + m + 1) * 128], w.ap[:, k, :],
                                             start=(k == 0), stop=(k == 7))
                t = p.inc("pe", t)
                p.wait("act", t, *fr("gvn"))
                u = p.inc("act", nc.scalar.activation(gvn[:, 2 * pr:2 * pr + 2, :].rearrange("p a b -> p (a b)"),
                                                      s.ap[:, :], ACT.Gelu_apprx_tanh))
                s.free = [u]
                vb.append(u)
            w.free = [t]
            issue(nl[0])
            nl[0] += 1
            gu_ok = {}

            def e_u(j, ps, t):
                p.wait("act", t, *free["tmp"])
                gu_ok[j] = p.inc("act", nc.scalar.activation(tmp[:, j, :], ps[:, :], ACT.Gelu_apprx_tanh))
                return gu_ok[j]

            proj(c, 3, e_u)
            p.wait("dve", *vb)
            for m in range(4):
                t = p.inc("dve", nc.vector.bn_stats(st[:, 16 + 6 * m:22 + 6 * m], gvn[:, m, :]))
            p.wait("dve", t)
            for m in range(4):
                t = p.inc("dve", nc.vector.bn_aggr(st[:, 40 + 2 * m:42 + 2 * m], st[:, 16 + 6 * m:22 + 6 * m]))
            p.wait("act", t)
            t = p.inc("act", nc.scalar.activation(st[:, 48:52], st[:, 41:48:2], ACT.Sqrt, bias=eps_ln[:], scale=1.0))
            p.wait("dve", t)
            t = p.inc("dve", nc.vector.reciprocal(st[:, 52:56], st[:, 48:52]))
            p.wait("dve", t)
            for m in range(4):
                t = p.inc("dve", nc.vector.tensor_scalar(gvn[:, m, :], gvn[:, m, :], st[:, 40 + 2 * m:41 + 2 * m],
                                                         st[:, 52 + m:53 + m], ALU.subtract, ALU.mult))
                p.wait("pool", t)
                t = p.inc("pool", nc.gpsimd.tensor_tensor(gvn[:, m, :], gvn[:, m, :], lngb[:, 0, :], ALU.mult))
                p.wait("pool", t)
                vn_ok = p.inc("pool", nc.gpsimd.tensor_tensor(gvn[:, m, :], gvn[:, m, :], lngb[:, 1, :], ALU.add))
            cross(3)

            def gate(g, ys):
                def e_g(j, ps, t):
                    y = ys[j]
                    p.wait("act", t, *fr("tmp2"))
                    u = p.inc("act", nc.scalar.activation(tmp2[:, j, 0:CH], ps[:, :], ACT.Silu))
                    p.wait("dve", u, Y[y])
                    Y[y] = p.inc("dve", nc.vector.tensor_tensor(yT[:, y, :], yT[:, y, :], tmp2[:, j, 0:CH], ALU.mult))
                    free["tmp2"] = [Y[y]]
                    return u
                proj(c, g, e_g)

            gate(9, [0, 1])
            for m in range(4):
                s = MS.next()
                p.wait("pe", vn_ok, wsg_ok, *s.free)
                for h in range(4):
                    lo = 64 * (h % 2)
                    t = nc.tensor.matmul(s.ap[lo:lo + 64, (h // 2) * 128:(h // 2 + 1) * 128],
                                         gvn[:, m, h * 64:(h + 1) * 64], wsg[:, h, :], start=True, stop=True,
                                         skip_group_check=True)
                t = p.inc("pe", t)
                p.wait("dve", t, *fr("yT"))
                u = p.inc("dve", nc.vector.tensor_tensor(yT[:, 2:4, m * 128:(m + 1) * 128],
                                                         s.ap[:, 0:256].rearrange("p (a b) -> p a b", a=2),
                                                         sgb[:], ALU.add))
                s.free = [u]
            free["gvn"] = [t]
            p.wait("dve", gu_ok[0], gu_ok[1], u)
            for j in range(2):
                Y[2 + j] = p.inc("dve", nc.vector.tensor_tensor(yT[:, 2 + j, :], yT[:, 2 + j, :], tmp[:, j, :], ALU.mult))
            free["tmp"] = [Y[3]]
            if c < 3:
                x = xTs[(c + 1) % 2]
                p.wait("sp", *x.free)
                x.full = [p.dma("sp", x, x.ap, A["xT"][:, :, (c + 1) * CH:(c + 2) * CH])]
            for g in range(10, 14):
                gate(g, [2 * (g - 9), 2 * (g - 9) + 1])

            for m in range(4):
                xs = xrs.next()
                tok = (4 * c + m) * 128
                p.wait("sp", *xs.free)
                xs.full = [p.dma("sp", xs, xs.ap, A["x"][tok:tok + 128, :])]
                hs = h0s.next()
                for n in range(2):
                    s = MS.next()
                    p.wait("pe", *s.free, *[Y[i] for i in range(10)], *wos.full)
                    for k in range(10):
                        t = nc.tensor.matmul(s.ap[:, :], yT[:, k, m * 128:(m + 1) * 128], wo[:, k, n * 512:(n + 1) * 512],
                                             start=(k == 0), stop=(k == 9))
                    t = p.inc("pe", t)
                    p.wait("dve", t, *xs.full)
                    u = p.inc("dve", nc.vector.scalar_tensor_tensor(
                        out=xs.ap[:, n * 512:(n + 1) * 512], in0=xs.ap[:, n * 512:(n + 1) * 512], scalar=ALPHA,
                        in1=s.ap[:, :], op0=ALU.mult, op1=ALU.add))
                    s.free = [u]
                free["yT"] = [t]
                t = layer_norm(p, xs.ap, 1024, 128, st[:, 16:28], st[:, 56:58], st[:, 58:59], st[:, 59:60], eps_ln,
                               xs.ap, LN[:, 0, :], LN[:, 1, :], [u], [], "pool")
                t = layer_norm(p, xs.ap, 1024, 128, st[:, 28:40], st[:, 60:62], st[:, 62:63], st[:, 63:64], eps_ln,
                               hs.ap, LN[:, 2, :], LN[:, 3, :], [t], hs.free, "pool")
                xs.free = [t]
                p.wait("sp", t)
                hs.free = [p.dma("sp", hs, h0d[tok:tok + 128, :], hs.ap)]
        xs, hs = xrs.next(), h0s.next()
        p.wait("sp", *xs.free)
        xs.full = [p.dma("sp", xs, xs.ap[0:NM, :], A["meta"])]
        t = layer_norm(p, xs.ap, 1024, NM, st[:, 16:28], st[:, 56:58], st[:, 58:59], st[:, 59:60], eps_ln,
                       hs.ap, LN[:, 2, :], LN[:, 3, :], xs.full, hs.free, "pool")
        p.wait("sp", t)
        hs.free = [p.dma("sp", hs, h0d[S:L, :], hs.ap[0:NM, :])]
        p.close()


NT = 17


F32R = mybir.dt.float32r


def phase_project(p, A, h0d, qTd, kTd, vd, ident, eps_rms):
    nc = p.nc
    with ExitStack() as ctx:
        def sb(name, shape, dt=F32):
            return ctx.enter_context(nc.sbuf_tensor("p_" + name, shape, dt))

        banks = [ctx.enter_context(nc.psum_tensor(f"p_ps{i}", [128, 512], F32)) for i in range(8)]
        B = Ring([Slot(b) for b in banks])
        w2r = sb("w2r", [128, 2, 1472])
        w2h = sb("w2h", [128, 8, 1472], F32R)
        w2l = sb("w2l", [128, 8, 1472], F32R)
        wqb = sb("wqb", [128, 2, 768])
        wkvb = sb("wkvb", [128, 1024])
        pc = sb("pc", [128, 3])
        gg = sb("gg", [128, 2, 128])
        ht = sb("ht", [128, 2, 1024])
        hTh = sb("hTh", [128, 8, 128], F32R)
        hTl = sb("hTl", [128, 8, 128], F32R)
        rp = sb("rp", [128, 384])
        an = sb("an", [128, 384])
        aT = sb("aT", [128, 3, 128])
        ra = sb("ra", [128, 1024])
        rb = sb("rb", [128, 1024])
        qt = sb("qt", [128, 2, 10, 128], F32R)
        kt = sb("kt", [128, 2, 7, 128], F32R)
        vt = sb("vt", [128, 6, 128])
        sq = sb("sq", [128, 256])
        st = sb("st", [128, 32])

        cslot = Slot(None, p.slot_sem("p_const"))
        for dst, src in ((pc[:], A["pc"][:, PC_GQA:PC_N]), (gg[:, 0, :], bcast(A["g_q_gqa_2"], 128)),
                         (gg[:, 1, :], bcast(A["g_k_gqa_2"], 128)), (wqb[:], A["wqb"]), (wkvb[:], A["wkvb"])):
            cok = p.dma("act", cslot, dst, src)
        w2s = Ring([Slot(w2r[:, i], p.slot_sem(f"p_w2{i}")) for i in range(2)])
        hts = Ring([Slot(ht[:, i], p.slot_sem(f"p_ht{i}")) for i in range(2)])
        kts = Slot(kt[:], p.slot_sem("p_kt"))
        vts = Slot(vt[:], p.slot_sem("p_vt"))
        rps = Slot(rp[:], p.slot_sem("p_rp"))
        qts = Slot(qt[:], p.slot_sem("p_qt"))

        def load(i):
            n = 128 if i < 16 else NM
            s = hts.next()
            p.wait("sp", *s.free)
            s.full = [p.dma("sp", s, s.ap[0:n, :], h0d[i * 128:i * 128 + n, :])]
            return s

        cur = load(0)
        w2_ok = []
        for k in range(8):
            s = w2s.next()
            p.wait("sp", *s.free)
            t = p.dma("sp", s, s.ap, A["w2"][:, k, :])
            p.wait("act", t)
            u = p.inc("act", nc.scalar.copy(w2h[:, k, :], s.ap))
            p.wait("dve", u)
            u = p.inc("dve", nc.vector.tensor_tensor(w2l[:, k, :], s.ap, w2h[:, k, :].bitcast(F32), ALU.subtract))
            s.free = [u]
            w2_ok.append(u)
        for e in ("pe", "dve", "act", "pool"):
            p.wait(e, cok)
        free = {}

        def fr(n):
            return free.get(n, [])

        def evac(e, dst, src, *toks):
            p.wait(e, *toks)
            if e == "act":
                return p.inc("act", nc.scalar.copy(dst, src))
            return p.inc("dve", nc.vector.tensor_copy(dst, src))

        def split(hi, lo, src, *toks):
            p.wait("act", *toks)
            u = p.inc("act", nc.scalar.copy(hi, src))
            p.wait("dve", u)
            return p.inc("dve", nc.vector.tensor_tensor(lo, src, hi.bitcast(F32), ALU.subtract))

        for i in range(NT):
            n = 128 if i < 16 else NM
            p.wait("sp", *rps.free)
            rps.full = [p.dma("sp", rps, rp[:], A["rope"][i])]
            tt = []
            for hf in range(2):
                s = B.next()
                p.wait("pe", *cur.full, *s.free)
                for k in range(4):
                    t = nc.tensor.transpose(s.ap[:, k * 128:k * 128 + n],
                                            cur.ap[0:n, (4 * hf + k) * 128:(4 * hf + k + 1) * 128], ident[0:n, 0:n])
                t = p.inc("pe", t)
                ks = slice(4 * hf, 4 * hf + 4)
                s.free = [split(hTh[:, ks, 0:n], hTl[:, ks, 0:n], s.ap[:, :].rearrange("p (a b) -> p a b", a=4)[:, :, 0:n],
                                t, *fr("hT"))]
                tt += s.free
            cur.free = [t]
            if i + 1 < NT:
                cur = load(i + 1)
            zs = []
            for lo, w in ((0, 448), (448, 512), (960, 512)):
                s = B.next()
                p.wait("pe", *tt, *s.free)
                for k in range(8):
                    p.wait("pe", w2_ok[k])
                    for m, (x, y) in enumerate(((hTh, w2h), (hTh, w2l), (hTl, w2h))):
                        t = nc.tensor.matmul(s.ap[0:n, 0:w], x[:, k, 0:n], y[:, k, lo:lo + w],
                                             start=(k == 0 and m == 0), stop=(k == 7 and m == 2))
                zs.append((s, p.inc("pe", t)))
            free["hT"] = [zs[-1][1]]
            (z0, t0), (z1, t1), (z2, t2) = zs
            p.wait("act", t0, *fr("st"))
            parts = [(z0, 0, 256), (z0, 256, 128)] + [(z1, 128 * h, 128) for h in range(4)] + [(z2, 128 * h, 128) for h in range(2)]
            for m, (z, lo, w) in enumerate(parts):
                if m == 2:
                    p.wait("act", t1)
                if m == 6:
                    p.wait("act", t2)
                if m:
                    p.wait("act", u)
                u = p.inc("act", nc.scalar.activation(sq[0:n, 0:w], z.ap[0:n, lo:lo + w], ACT.Square, accum_out=st[0:n, m:m + 1]))
            p.wait("act", *vts.free)
            u = p.inc("act", nc.scalar.copy(vt[0:n, 4:6, :].rearrange("p a b -> p (a b)"), z2.ap[0:n, 256:512]))
            p.wait("act", u)
            p.inc("act", nc.scalar.activation(st[0:n, 8:9], st[0:n, 0:1], ACT.Sqrt, bias=eps_rms[0:n, :], scale=1.0 / 256))
            u = p.inc("act", nc.scalar.activation(st[0:n, 9:16], st[0:n, 1:8], ACT.Sqrt, bias=eps_rms[0:n, :], scale=1.0 / 128))
            p.wait("dve", u)
            r = p.inc("dve", nc.vector.reciprocal(st[0:n, 16:24], st[0:n, 8:16]))
            p.wait("act", r, *fr("an"))
            p.inc("act", nc.scalar.activation(an[0:n, 0:256], z0.ap[0:n, 0:256], ACT.Copy, scale=st[0:n, 16:17]))
            ua = p.inc("act", nc.scalar.activation(an[0:n, 256:384], z0.ap[0:n, 256:384], ACT.Copy, scale=st[0:n, 17:18]))
            p.wait("dve", *rps.full)

            def rot(dst, tmp, src, heads, w, c0, s0, e, toks):
                p.wait(e, *toks)
                eng = p.eng[e]
                h_ = w // 64
                cb = rp[0:n, c0:c0 + w].unsqueeze(1).to_broadcast([n, heads, w])
                t = p.inc(e, eng.tensor_tensor(dst, src, cb, ALU.mult))
                s4 = src.rearrange("p h (f two c) -> p h f two c", f=h_, two=2)
                t4 = tmp.rearrange("p h (f two c) -> p h f two c", f=h_, two=2)
                sv = rp[0:n, s0:s0 + w].rearrange("p (f two c) -> p f two c", f=h_, two=2)
                for a in range(2):
                    for f in range(h_):
                        sb_ = sv[:, f, a, :].unsqueeze(1).to_broadcast([n, heads, 32])
                        t = p.inc(e, eng.tensor_tensor(t4[:, :, f, a, :], s4[:, :, f, 1 - a, :], sb_, ALU.mult))
                p.wait(e, t)
                return p.inc(e, eng.tensor_tensor(dst, dst, tmp, ALU.add))

            kr3 = ra[0:n, 0:64].rearrange("p (h w) -> p h w", h=1)
            t = rot(kr3, rb[0:n, 0:64].rearrange("p (h w) -> p h w", h=1),
                    z0.ap[0:n, 384:448].rearrange("p (h w) -> p h w", h=1), 1, 64, 0, 64, "dve", [ua, *fr("ra")])
            p.wait("dve", t)
            krt = p.inc("dve", nc.vector.tensor_copy(ra[0:n, 64:128], ra[0:n, 0:64]))
            z0.free = [krt, ua]
            rq = st[0:n, 18:22].unsqueeze(2).to_broadcast([n, 4, 128])
            rk = st[0:n, 22:24].unsqueeze(2).to_broadcast([n, 2, 128])
            xg = ra[0:n, 256:1024].rearrange("p (h w) -> p h w", h=6)
            p.wait("dve", *fr("xg"))
            a1 = p.inc("dve", nc.vector.tensor_tensor(xg[:, 0:4, :], z1.ap[0:n, :].rearrange("p (h w) -> p h w", h=4), rq, ALU.mult))
            a2 = p.inc("dve", nc.vector.tensor_tensor(xg[:, 4:6, :], z2.ap[0:n, 0:256].rearrange("p (h w) -> p h w", h=2), rk, ALU.mult))
            z1.free = [a1]
            z2.free = [a2]
            p.wait("pool", a2)
            p.inc("pool", nc.gpsimd.tensor_tensor(xg[:, 0:4, :], xg[:, 0:4, :], gg[0:n, 0:1, :].to_broadcast([n, 4, 128]), ALU.mult))
            a2 = p.inc("pool", nc.gpsimd.tensor_tensor(xg[:, 4:6, :], xg[:, 4:6, :], gg[0:n, 1:2, :].to_broadcast([n, 2, 128]), ALU.mult))
            yg = rb[0:n, 256:1024].rearrange("p (h w) -> p h w", h=6)
            yq = rot2(p, yg, xg, rp, n, [a2, *rps.full], fr("yg"))
            free["xg"] = [yq]
            s = B.next()
            p.wait("pe", ua, *s.free)
            for k in range(3):
                t = nc.tensor.transpose(s.ap[:, k * 128:k * 128 + n], an[0:n, k * 128:(k + 1) * 128], ident[0:n, 0:n])
            t = p.inc("pe", t)
            free["an"] = [t]
            p.wait("act", t, *fr("aT"))
            for k in range(3):
                a_ok = p.inc("act", nc.scalar.activation(aT[:, k, 0:n], s.ap[:, k * 128:k * 128 + n], ACT.Copy, scale=pc[:, k:k + 1]))
            s.free = [a_ok]
            s = B.next()
            p.wait("pe", a_ok, *s.free)
            for h in range(4):
                t = nc.tensor.matmul(s.ap[:, h * 128:h * 128 + n], wkvb[:, h * 256:h * 256 + 128], aT[:, 2, 0:n], start=True, stop=True)
            t = p.inc("pe", t)
            s.free = [split(kt[:, 0, 0:4, 0:n], kt[:, 1, 0:4, 0:n],
                            s.ap[:, :].rearrange("p (a b) -> p a b", a=4)[:, :, 0:n], t, *kts.free)]
            s = B.next()
            p.wait("pe", *s.free)
            for h in range(4):
                t = nc.tensor.matmul(s.ap[0:n, h * 128:(h + 1) * 128], aT[:, 2, 0:n], wkvb[:, h * 256 + 128:(h + 1) * 256], start=True, stop=True)
            t = p.inc("pe", t)
            s.free = [evac("act", vt[0:n, 0:4, :].rearrange("p a b -> p (a b)"), s.ap[0:n, :], t)]
            p.wait("sp", *s.free)
            vts.free = [p.dma("sp", vts, vd[:, 0:n, i, :].rearrange("h p d -> p h d"), vt[0:n])]
            if i < 16:
                s = B.next()
                p.wait("pe", *s.free)
                for h in range(4):
                    for k in range(2):
                        t = nc.tensor.matmul(s.ap[:, h * 128:(h + 1) * 128], wqb[:, k, h * 192:h * 192 + 128], aT[:, k, :],
                                             start=(k == 0), stop=(k == 1))
                t = p.inc("pe", t)
                s.free = [split(qt[:, 0, 0:4, :].rearrange("p a b -> p (a b)"), qt[:, 1, 0:4, :].rearrange("p a b -> p (a b)"),
                                s.ap[:, :], t, *qts.free)]
                s = B.next()
                p.wait("pe", *s.free)
                for k in range(2):
                    t = nc.tensor.matmul(s.ap[:, 0:256], aT[:, k, :],
                                         wqb[:, k, :].rearrange("p (h w) -> p h w", h=4)[:, :, 128:192],
                                         start=(k == 0), stop=(k == 1))
                t = p.inc("pe", t)
                qr = an[:, 0:256].rearrange("p (h w) -> p h w", h=4)
                qu = rot(qr, rb[:, 0:256].rearrange("p (h w) -> p h w", h=4),
                         s.ap[:, 0:256].rearrange("p (h w) -> p h w", h=4), 4, 64, 0, 64, "dve", [t, krt, *free["an"]])
                s.free = [qu]
            free["aT"] = [t]
            s = B.next()
            p.wait("pe", krt, *s.free)
            t = nc.tensor.transpose(s.ap[:, 0:n], ra[0:n, 0:128], ident[0:n, 0:n])
            if i < 16:
                p.wait("pe", qu)
                for k in range(2):
                    t = nc.tensor.transpose(s.ap[:, 128 + k * 128:256 + k * 128], an[:, k * 128:(k + 1) * 128], ident[:])
            t = p.inc("pe", t)
            free["ra"] = [t]
            free["an"] = [t]
            s.free = [split(kt[:, 0, 4, 0:n], kt[:, 1, 4, 0:n], s.ap[:, 0:n], t)]
            if i < 16:
                s.free = [split(qt[:, 0, 4:6, :].rearrange("p a b -> p (a b)"), qt[:, 1, 4:6, :].rearrange("p a b -> p (a b)"),
                                s.ap[:, 128:384], t, *s.free)]
            s = B.next()
            p.wait("pe", yq, *s.free)
            for k in range(2):
                t = nc.tensor.transpose(s.ap[:, k * 128:k * 128 + n], rb[0:n, 768 + k * 128:896 + k * 128], ident[0:n, 0:n])
            t = p.inc("pe", t)
            s.free = [split(kt[:, 0, 5:7, 0:n], kt[:, 1, 5:7, 0:n],
                            s.ap[:, 0:256].rearrange("p (a b) -> p a b", a=2)[:, :, 0:n], t)]
            p.wait("sp", *s.free)
            kts.free = [p.dma("sp", kts, kTd[z, :, :, i * 128:i * 128 + n].rearrange("h p n -> p h n"),
                              kt[:, z, :, 0:n].bitcast(F32)) for z in range(2)]
            if i < 16:
                s = B.next()
                p.wait("pe", *s.free)
                for k in range(4):
                    t = nc.tensor.transpose(s.ap[:, k * 128:(k + 1) * 128], rb[:, 256 + k * 128:384 + k * 128], ident[:])
                t = p.inc("pe", t)
                s.free = [split(qt[:, 0, 6:10, :].rearrange("p a b -> p (a b)"), qt[:, 1, 6:10, :].rearrange("p a b -> p (a b)"),
                                s.ap[:, :], t)]
                p.wait("sp", *s.free)
                qts.free = [p.dma("sp", qts, qTd[z, :, :, i * 128:(i + 1) * 128].rearrange("h p n -> p h n"),
                                  qt[:, z].bitcast(F32)) for z in range(2)]
            free["yg"] = [t]
            rps.free = [yq, krt] + ([qu] if i < 16 else [])
        p.close()


def rot2(p, out, x, rp, n, toks, out_free):
    eng = p.nc.gpsimd
    p.wait("pool", *toks, *out_free)
    x5 = x.rearrange("p h (f two c) -> p h f two c", f=2, two=2)
    o5 = out.rearrange("p h (f two c) -> p h f two c", f=2, two=2)
    sv = rp[0:n, 256:384].rearrange("p (f two c) -> p f two c", f=2, two=2)
    for a in range(2):
        for f in range(2):
            t = p.inc("pool", eng.tensor_tensor(o5[:, :, f, a, :], x5[:, :, f, 1 - a, :],
                                                sv[:, f, a, :].unsqueeze(1).to_broadcast([n, 6, 32]), ALU.mult))
    p.wait("pool", t)
    t = p.inc("pool", eng.tensor_tensor(x, x, rp[0:n, 128:256].unsqueeze(1).to_broadcast([n, 6, 128]), ALU.mult))
    p.wait("pool", t)
    return p.inc("pool", eng.tensor_tensor(out, out, x, ALU.add))


SCW = [(416 * c, 416 if c < 4 else 400) for c in range(5)]


def phase_attend(p, qTd, kTd, vd, od, yd, ident):
    nc = p.nc
    with ExitStack() as ctx:
        def sb(name, shape, dt=F32):
            return ctx.enter_context(nc.sbuf_tensor("a_" + name, shape, dt))

        banks = [ctx.enter_context(nc.psum_tensor(f"a_ps{i}", [128, 512], F32)) for i in range(8)]
        SB = [Slot(b) for b in banks[0:5]]
        TB = Ring([Slot(banks[5]), Slot(banks[6])])
        OB = Slot(banks[7])
        K = sb("K", [128, 2, 2, L], F32R)
        Ks = Ring([Slot(K[:, i], p.slot_sem(f"a_K{i}")) for i in range(2)])
        KR = sb("KR", [128, 2, L], F32R)
        KRs = Slot(KR[:], p.slot_sem("a_KR"))
        V = sb("V", [128, 2, NT, 128])
        Vs = Ring([Slot(V[:, i], p.slot_sem(f"a_V{i}")) for i in range(2)])
        Q = sb("Q", [128, 2, 2, S], F32R)
        Qs = Ring([Slot(Q[:, i], p.slot_sem(f"a_Q{i}")) for i in range(2)])
        QR = sb("QR", [128, 2, 2, S], F32R)
        QRs = Ring([Slot(QR[:, i], p.slot_sem(f"a_QR{i}")) for i in range(2)])
        P = sb("P", [128, 2, L])
        Ps = [Slot(P[:, i]) for i in range(2)]
        PT = sb("PT", [128, 2, NT * 128])
        PTs = [Slot(PT[:, i]) for i in range(2)]
        o = sb("o", [128, 1, 16, 128])
        os_ = Ring([Slot(o[:, i], p.slot_sem(f"a_o{i}")) for i in range(1)])
        sc = sb("sc", [128, 2, 32])
        scs = [Slot(sc[:, i]) for i in range(2)]

        def fetch(slot, dst, src):
            slot.full = [p.dma("sp", slot, dst, src)]

        def parts(d, h):
            return d[:, h].rearrange("z p n -> p z n")

        heads = {}

        def load(h):
            prev = heads.get(h - 1)
            if h < 4:
                qr = prev["qr"] if h % 2 else QRs.next()
                if h % 2 == 0:
                    p.wait("sp", *qr.free)
                    fetch(qr, qr.ap.bitcast(F32), parts(qTd, 4 + h // 2))
            else:
                qr = None
            if h in (5, 7):
                k, v = prev["k"], prev["v"]
            else:
                kh = h if h < 4 else 5 + (h - 4) // 2
                vh = h if h < 4 else 4 + (h - 4) // 2
                k, v = Ks.next(), Vs.next()
                p.wait("sp", *k.free)
                fetch(k, k.ap.bitcast(F32), parts(kTd, kh))
                p.wait("sp", *v.free)
                p.dma("sp", v, v.ap[0:NM, 16, :], vd[vh, 0:NM, 16, :])
                fetch(v, v.ap[:, 0:16, :], vd[vh, :, 0:16, :])
            q = Qs.next()
            p.wait("sp", *q.free)
            fetch(q, q.ap.bitcast(F32), parts(qTd, h if h < 4 else 2 + h))
            heads[h] = {"qr": qr, "k": k, "v": v, "q": q, "o": os_.next()}

        load(0)
        fetch(KRs, KR[:].bitcast(F32), parts(kTd, 4))
        load(1)
        zt = sb("zt", [128, 1024])
        zs = Slot(None, p.slot_sem("a_zt"))
        zok = p.inc("pool", nc.gpsimd.memset(zt[:], 0.0))
        p.wait("sp", zok)
        for b in range(64, YB):
            p.dma("sp", zs, yd[b * 128:(b + 1) * 128, :], zt[:])
        steps = [(h, i) for h in range(8) for i in range(16)]

        def scores(m, c):
            h, i = steps[m]
            H = heads[h]
            b = SB[c]
            lo, w = SCW[c]
            qs = slice(i * 128, (i + 1) * 128)
            p.wait("pe", *H["q"].full, *H["k"].full, *b.free)
            todo = [(H["q"].ap[:, x, qs], H["k"].ap[:, y, lo:lo + w]) for x, y in ((0, 0), (0, 1), (1, 0))]
            if h < 4:
                r = 64 * (h % 2)
                p.wait("pe", *H["qr"].full, *KRs.full)
                todo += [(H["qr"].ap[r:r + 64, x, qs], KR[r:r + 64, y, lo:lo + w]) for x, y in ((0, 0), (0, 1), (1, 0))]
            for n, (x, y) in enumerate(todo):
                t = nc.tensor.matmul(b.ap[:, 0:w], x, y, start=(n == 0), stop=(n == len(todo) - 1))
            t = p.inc("pe", t)
            if i == 15:
                for n in ("q", "k", "qr"):
                    if H[n]:
                        H[n].free = [t]
            return t

        def maximum(m, c, t):
            z = scs[m % 2]
            p.wait("dve", t, *z.free)
            return p.inc("dve", nc.vector.tensor_reduce(z.ap[:, c:c + 1], SB[c].ap[:, 0:SCW[c][1]], AX, ALU.max))

        def weights(m, t):
            h, i = steps[m]
            scale = SQK_M if h < 4 else SQK_G
            z, P_ = scs[m % 2], Ps[m % 2]
            p.wait("dve", t)
            t = p.inc("dve", nc.vector.tensor_reduce(z.ap[:, 5:6], z.ap[:, 0:5], AX, ALU.max))
            p.wait("dve", t)
            t = p.inc("dve", nc.vector.tensor_scalar(z.ap[:, 6:7], z.ap[:, 5:6], -scale, None, ALU.mult))
            p.wait("act", t, *P_.free)
            P_.full = []
            for c in range(5):
                lo, w = SCW[c]
                u = p.inc("act", nc.scalar.activation(P_.ap[:, lo:lo + w], SB[c].ap[:, 0:w], ACT.Exp, bias=z.ap[:, 6:7],
                                                      scale=scale, accum_out=z.ap[:, 8 + c:9 + c]))
                SB[c].free = [u]
                P_.full.append(u)
            z.full = [u]

        def turn(m, c):
            P_, T = Ps[m % 2], PTs[m % 2]
            s = TB.next()
            k = 4 if c < 4 else 1
            n = 128 if c < 4 else NM
            p.wait("pe", P_.full[min(4, (c * 512 + 511) // 416)], *s.free)
            for a in range(k):
                t = nc.tensor.transpose(s.ap[0:n, a * 128:(a + 1) * 128], P_.ap[:, c * 512 + a * 128:c * 512 + a * 128 + n], ident[:])
            t = p.inc("pe", t)
            e = ("act", "dve", "act", "dve", "dve")[c]
            p.wait(e, t, *T.free)
            dst, src = T.ap[0:n, c * 512:c * 512 + k * 128], s.ap[0:n, 0:k * 128]
            u = p.inc(e, nc.scalar.copy(dst, src) if e == "act" else nc.vector.tensor_copy(dst, src))
            s.free = [u]
            T.full.append(u)
            if c == 4:
                P_.free = [t]

        def values(m):
            h, i = steps[m]
            H = heads[h]
            T, z, O = PTs[m % 2], scs[m % 2], H["o"]
            p.wait("pe", *OB.free, *H["v"].full)
            for j in range(NT):
                n = 128 if j < 16 else NM
                p.wait("pe", T.full[j // 4])
                t = nc.tensor.matmul(OB.ap[:, 0:128], T.ap[0:n, j * 128:(j + 1) * 128], H["v"].ap[0:n, j, :],
                                     start=(j == 0), stop=(j == NT - 1))
            t = p.inc("pe", t)
            T.free = [t]
            if i == 15:
                H["v"].free = [t]
            p.wait("dve", *z.full)
            u = p.inc("dve", nc.vector.tensor_reduce(z.ap[:, 14:15], z.ap[:, 8:13], AX, ALU.add))
            p.wait("dve", u)
            u = p.inc("dve", nc.vector.reciprocal(z.ap[:, 15:16], z.ap[:, 14:15]))
            p.wait("dve", u, t, *(O.free if i == 0 else []))
            u = p.inc("dve", nc.vector.tensor_scalar(O.ap[:, i, :], OB.ap[:, 0:128], z.ap[:, 15:16], None, ALU.mult))
            OB.free = [u]
            z.free = [u]
            if i % 8 == 7:
                g = slice(i - 7, i + 1)
                p.wait("sp", u)
                t = p.dma("sp", O, od[(i - 7) * 128:(i + 1) * 128, h * 128:(h + 1) * 128].rearrange("(i p) d -> p i d", p=128),
                          O.ap[:, g, :])
                O.free = [t]
                if i == 15 and h + 2 < 8:
                    load(h + 2)

        for m in range(len(steps)):
            for c in range(5):
                t = scores(m, c)
                if m:
                    if c == 0:
                        PTs[(m - 1) % 2].full = []
                    turn(m - 1, c)
                t = maximum(m, c, t)
            weights(m, t)
            if m:
                values(m - 1)
        m = len(steps) - 1
        PTs[m % 2].full = []
        for c in range(5):
            turn(m, c)
        values(m)
        p.close()


class Route:
    pass


def alloc_route(nc):
    r = Route()
    r.slot = nc.alloc_sbuf_tensor("r_slot", [128, 16, 4], U32)
    r.pos = nc.alloc_sbuf_tensor("r_pos", [128, 16, 4], F32)
    r.idf = nc.alloc_sbuf_tensor("r_idf", [128, 16, 4], F32)
    r.base = nc.alloc_sbuf_tensor("r_base", [128, 32], F32)
    r.gate = nc.alloc_sbuf_tensor("r_gate", [128, 16, 4], F32)
    r.ngr = nc.alloc_sbuf_tensor("r_ngr", [1, 1], I32)
    r.tab = nc.alloc_sbuf_tensor("r_tab", [4, GT], I32)
    return r


def phase_route(p, A, h0d, od, h1d, tabd, R, ident, eps_ln, eps_rms, lgd=None):
    nc = p.nc
    with ExitStack() as ctx:
        def sb(name, shape, dt=F32):
            return ctx.enter_context(nc.sbuf_tensor("o_" + name, shape, dt))

        banks = [ctx.enter_context(nc.psum_tensor(f"o_ps{i}", [128, 512], F32)) for i in range(8)]
        B = Ring([Slot(b) for b in banks])
        wo = sb("wo", [128, 8, 1024])
        wr = sb("wr", [128, 8, 32])
        go = sb("go", [128, 1024])
        LN = sb("LN", [128, 2, 1024])
        br = sb("br", [128, 32])
        erow = sb("erow", [128, 32])
        before = sb("before", [128, 128])
        ones = sb("ones", [128, 128])
        tokid = sb("tokid", [128, 16], I32)
        thr = sb("thr", [128, 15])
        zt = sb("zt", [128, NE * CAP // 128], I32)
        ob = sb("ob", [128, 2, 1024])
        hb = sb("hb", [128, 2, 1024])
        h1 = sb("h1", [128, 2, 1024])
        oT = sb("oT", [128, 2, 8, 128])
        sq = sb("sq", [128, 512])
        st = sb("st", [128, 64])
        lg = sb("lg", [128, 2, 32])
        m8 = sb("m8", [128, 8])
        i8 = sb("i8", [128, 8], U32)
        ex = sb("ex", [128, 8])
        oh = sb("oh", [128, 4, 32])
        pr = sb("pr", [128, 4, 32])
        M = sb("M", [128, 32])
        Macc = sb("Macc", [128, 32])
        C = sb("C", [128, 32])
        sf = sb("sf", [128, 4])
        cnt = sb("cnt", [128, 9, 32])
        gt = sb("gt", [128, 12])
        qcol = sb("qcol", [128, 1])
        tb = sb("tb", [128, 32, 15])

        cslot = Slot(None, p.slot_sem("o_const"))
        for dst, src in ((go[:], bcast(A["g_o"], 1024)), (LN[:, 0, :], bcast(A["ln1_g_2"], 1024)),
                         (LN[:, 1, :], bcast(A["ln1_b_2"], 1024)), (br[:], bcast(A["b_router_2"], 32)),
                         (erow[:], A["erow"]), (qcol[:], A["qcol"]), (before[:], A["before"]),
                         (tokid[:], A["tokid"]), (thr[:], A["thr"]), (wr[:], A["wr"]), (wo[:], A["wo2"])):
            cok = p.dma("act", cslot, dst, src)
        z = p.inc("dve", nc.vector.memset(zt[:], 0))
        p.inc("dve", nc.vector.memset(ones[:], 1.0))
        m0 = p.inc("dve", nc.vector.memset(Macc[:], 0.0))
        zs = Slot(None, p.slot_sem("o_zt"))
        p.wait("sp", z)
        tab_ok = p.dma("sp", zs, tabd.rearrange("(p n) o -> p (n o)", p=128), zt[:])
        obs = Ring([Slot(ob[:, i], p.slot_sem(f"o_ob{i}")) for i in range(2)])
        hbs = Ring([Slot(hb[:, i], p.slot_sem(f"o_hb{i}")) for i in range(2)])
        h1s = Ring([Slot(h1[:, i], p.slot_sem(f"o_h1{i}")) for i in range(2)])
        oTs = Ring([Slot(oT[:, i]) for i in range(2)])
        scs = Slot(None, p.slot_sem("o_scatter"))

        def load(i):
            a, b = obs.next(), hbs.next()
            p.wait("sp", *a.free)
            a.full = [p.dma("sp", a, a.ap, od[i * 128:(i + 1) * 128, :])]
            p.wait("sp", *b.free)
            b.full = [p.dma("sp", b, b.ap, h0d[i * 128:(i + 1) * 128, :])]
            return a, b

        def turn(src, ready):
            dst = oTs.next()
            dst.full = []
            for hf in range(2):
                s = B.next()
                p.wait("pe", *ready, *s.free)
                for k in range(4):
                    t = nc.tensor.transpose(s.ap[:, k * 128:(k + 1) * 128], src[:, (4 * hf + k) * 128:(4 * hf + k + 1) * 128], ident[:])
                t = p.inc("pe", t)
                e = ("act", "dve")[hf]
                p.wait(e, t, *dst.free)
                o_ = dst.ap[:, 4 * hf:4 * hf + 4, :].rearrange("p a b -> p (a b)")
                s.free = [p.inc(e, nc.scalar.copy(o_, s.ap[:, :]) if e == "act" else nc.vector.tensor_copy(o_, s.ap[:, :]))]
                dst.full += s.free
            return dst, t

        for e in ("pe", "dve", "act", "pool"):
            p.wait(e, cok, m0)
        free = {}

        def fr(n):
            return free.get(n, [])

        cur = load(0)
        nxt = load(1)
        carry = {"oh": [], "M": [m0]}

        def first(i, a, b):
            p.wait("act", *a.full)
            for hf in range(2):
                if hf:
                    p.wait("act", u)
                u = p.inc("act", nc.scalar.activation(sq[:], a.ap[:, hf * 512:(hf + 1) * 512], ACT.Square, accum_out=st[:, hf:hf + 1]))
            p.wait("act", u)
            u = p.inc("act", nc.scalar.activation(st[:, 2:4], st[:, 0:2], ACT.Sqrt, bias=eps_rms[:], scale=1.0 / 512))
            p.wait("dve", u)
            u = p.inc("dve", nc.vector.reciprocal(st[:, 4:6], st[:, 2:4]))
            p.wait("dve", u)
            for hf in range(2):
                v = a.ap[:, hf * 512:(hf + 1) * 512]
                u = p.inc("dve", nc.vector.scalar_tensor_tensor(out=v, in0=v, scalar=st[:, 4 + hf:5 + hf],
                                                                in1=go[:, hf * 512:(hf + 1) * 512], op0=ALU.mult, op1=ALU.mult))
            T, t = turn(a.ap, [u])
            a.free = [t]
            h = h1s.next()
            for n in range(2):
                s = B.next()
                p.wait("pe", *T.full, *s.free)
                for k in range(8):
                    t = nc.tensor.matmul(s.ap[:, :], T.ap[:, k, :], wo[:, k, n * 512:(n + 1) * 512], start=(k == 0), stop=(k == 7))
                t = p.inc("pe", t)
                p.wait("dve", t, *b.full)
                u = p.inc("dve", nc.vector.scalar_tensor_tensor(
                    out=b.ap[:, n * 512:(n + 1) * 512], in0=b.ap[:, n * 512:(n + 1) * 512], scalar=ALPHA,
                    in1=s.ap[:, :], op0=ALU.mult, op1=ALU.add))
                s.free = [u]
            T.free = [t]
            t = layer_norm(p, b.ap, 1024, 128, st[:, 16:28], st[:, 8:10], st[:, 10:11], st[:, 11:12], eps_ln,
                           h.ap, LN[:, 0, :], LN[:, 1, :], [u], h.free, "pool")
            b.free = [t]
            p.wait("sp", t)
            h.free = [p.dma("sp", h, h1d[i * 128:(i + 1) * 128, :], h.ap)]
            return h, t

        def second(i, h, ok):
            T, t = turn(h.ap, [ok])
            h.free = h.free + [t]
            s = B.next()
            p.wait("pe", *T.full, *s.free)
            for k in range(8):
                t = nc.tensor.matmul(s.ap[:, 0:32], T.ap[:, k, :], wr[:, k, :], start=(k == 0), stop=(k == 7))
            t = p.inc("pe", t)
            T.free = [t]
            l = lg[:, i % 2, :]
            p.wait("dve", t)

            def v(ins):
                tok = p.inc("dve", ins)
                p.wait("dve", tok)
                return tok

            s.free = [v(nc.vector.tensor_tensor(l, s.ap[:, 0:32], br[:], ALU.add))]
            v(nc.vector.max(m8[:], l))
            v(nc.vector.max_index(i8[:], m8[:], l))
            v(nc.vector.tensor_copy(R.idf[:, i, :], i8[:, 0:4]))
            p.wait("dve", *fr("ex"))
            t = v(nc.vector.tensor_scalar(ex[:, 4:5], m8[:, 0:1], -1.0, None, ALU.mult))
            p.wait("act", t)
            g = p.inc("act", nc.scalar.activation(ex[:, 0:4], m8[:, 0:4], ACT.Exp, bias=ex[:, 4:5], scale=1.0, accum_out=ex[:, 5:6]))
            v(nc.vector.tensor_tensor(oh[:], erow[:].unsqueeze(1).to_broadcast([128, 4, 32]),
                                      R.idf[:, i, :].unsqueeze(2).to_broadcast([128, 4, 32]), ALU.is_equal))
            p.wait("dve", *fr("M"))
            t = v(nc.vector.tensor_reduce(M[:], oh[:].rearrange("p k e -> p e k"), AX, ALU.add))
            s = B.next()
            p.wait("pe", t, *s.free, *carry["M"])
            nc.tensor.matmul(s.ap[:, 0:32], before[:], M[:], start=True, stop=False)
            t = p.inc("pe", nc.tensor.matmul(s.ap[:, 0:32], ones[:], Macc[:], start=False, stop=True))
            free["M"] = [t]
            p.wait("dve", t)
            s.free = [v(nc.vector.tensor_copy(C[:], s.ap[:, 0:32]))]
            carry["M"] = [v(nc.vector.tensor_tensor(Macc[:], Macc[:], M[:], ALU.add))]
            v(nc.vector.tensor_tensor(pr[:], oh[:], C[:].unsqueeze(1).to_broadcast([128, 4, 32]), ALU.mult))
            v(nc.vector.tensor_reduce(R.pos[:, i, :], pr[:], AX, ALU.add))
            v(nc.vector.scalar_tensor_tensor(out=sf[:], in0=R.idf[:, i, :], scalar=float(CAP), in1=R.pos[:, i, :],
                                             op0=ALU.mult, op1=ALU.add))
            sl = v(nc.vector.tensor_copy(R.slot[:, i, :], sf[:]))
            p.wait("dve", g)
            v(nc.vector.reciprocal(ex[:, 6:7], ex[:, 5:6]))
            free["ex"] = [v(nc.vector.tensor_scalar(R.gate[:, i, :], ex[:, 0:4], ex[:, 6:7], None, ALU.mult))]
            p.wait("pool", sl, tab_ok)
            for k in range(4):
                nc.gpsimd.indirect_dma_start(
                    out=tabd, out_offset=bass.IndirectOffsetOnAxis(ap=R.slot[:, i, k:k + 1], axis=0),
                    in_=tokid[:, i:i + 1], in_offset=None).then_inc(scs.sem, 16)
                scs.n += 16
                p.dmas.append((scs.sem, scs.n))

        prev = None
        for i in range(16):
            h, ok = first(i, *cur)
            cur = nxt
            if i + 2 < 16:
                nxt = load(i + 2)
            if prev:
                second(*prev)
            prev = (i, h, ok)
        second(*prev)
        s = B.next()
        p.wait("pe", *carry["M"], *s.free)
        t = p.inc("pe", nc.tensor.matmul(s.ap[:, 0:32], ones[:], Macc[:], start=True, stop=True))
        p.wait("dve", t)

        def v(ins):
            tok = p.inc("dve", ins)
            p.wait("dve", tok)

        v(nc.vector.tensor_copy(cnt[:, 0, :], s.ap[:, 0:32]))
        v(nc.vector.tensor_tensor(tb[:], cnt[:, 0, :].unsqueeze(2).to_broadcast([128, 32, 15]),
                                  thr[:].unsqueeze(1).to_broadcast([128, 32, 15]), ALU.is_gt))
        v(nc.vector.tensor_reduce(cnt[:, 1, :], tb[:], AX, ALU.add))
        v(nc.vector.tensor_scalar(cnt[:, 1, :], cnt[:, 1, :], 1.0, None, ALU.add))
        nb, inc, exc, grp, ginc, gexc = (cnt[:, j, :] for j in range(1, 7))
        v(nc.vector.tensor_tensor_scan(inc, ones[:, 0:32], nb, 0.0, ALU.mult, ALU.add))
        v(nc.vector.tensor_tensor(exc, inc, nb, ALU.subtract))
        v(nc.vector.tensor_scalar(R.base[:], exc, 128.0, None, ALU.mult))
        v(nc.vector.tensor_reduce(grp, tb[:, :, 3:12:4], AX, ALU.add))
        v(nc.vector.tensor_scalar(grp, grp, 1.0, None, ALU.add))
        v(nc.vector.tensor_tensor_scan(ginc, ones[:, 0:32], grp, 0.0, ALU.mult, ALU.add))
        v(nc.vector.tensor_tensor(gexc, ginc, grp, ALU.subtract))
        v(nc.vector.tensor_copy(R.ngr[:], cnt[0:1, 5, 31:32]))
        oh8, sel = cnt[:, 7, :], cnt[:, 8, :]
        v(nc.vector.tensor_scalar(oh8, gexc, qcol[:, 0:1], None, ALU.is_le))
        v(nc.vector.tensor_scalar(sel, ginc, qcol[:, 0:1], None, ALU.is_le))
        v(nc.vector.tensor_tensor(oh8, oh8, sel, ALU.subtract))
        for j, src in enumerate((erow[:], nb, gexc, exc)):
            v(nc.vector.tensor_tensor(sel, oh8, src, ALU.mult))
            v(nc.vector.tensor_reduce(gt[:, j:j + 1], sel, AX, ALU.add))
        e_, n_, gx, bx, s_ = (gt[:, j:j + 1] for j in range(5))
        o_ = gt[:, 8:12]
        v(nc.vector.tensor_tensor(s_, qcol[:], gx, ALU.subtract))
        v(nc.vector.tensor_copy(o_[:, 0:1], e_))
        v(nc.vector.scalar_tensor_tensor(out=o_[:, 1:2], in0=s_, scalar=-4.0, in1=n_, op0=ALU.mult, op1=ALU.add))
        v(nc.vector.tensor_scalar(o_[:, 1:2], o_[:, 1:2], 4.0, 0.0, ALU.min, ALU.max))
        v(nc.vector.tensor_scalar(gt[:, 5:6], s_, 512.0, None, ALU.mult))
        v(nc.vector.scalar_tensor_tensor(out=o_[:, 2:3], in0=e_, scalar=float(CAP), in1=gt[:, 5:6], op0=ALU.mult, op1=ALU.add))
        v(nc.vector.scalar_tensor_tensor(out=o_[:, 3:4], in0=s_, scalar=4.0, in1=bx, op0=ALU.mult, op1=ALU.add))
        s = B.next()
        p.wait("pe", (p.sem["dve"], p.cnt["dve"]), *s.free)
        t = p.inc("pe", nc.tensor.transpose(s.ap[0:4, 0:128], o_, ident[:]))
        p.wait("dve", t)
        v(nc.vector.tensor_copy(R.tab[:], s.ap[0:4, 0:GT]))
        p.close()


def phase_combine(p, A, h1d, yd, R, out, eps_ln):
    nc = p.nc
    with ExitStack() as ctx:
        def sb(name, shape, dt=F32):
            return ctx.enter_context(nc.sbuf_tensor("c_" + name, shape, dt))

        LN = sb("LN", [128, 2, 1024])
        y = sb("y", [128, 8, 1024])
        h = sb("h", [128, 3, 1024])
        o = sb("o", [128, 2, 1024])
        st = sb("st", [128, 2, 32])
        cslot = Slot(None, p.slot_sem("c_const"))
        p.dma("act", cslot, LN[:, 0, :], bcast(A["ln2_g_2"], 1024))
        cok = p.dma("act", cslot, LN[:, 1, :], bcast(A["ln2_b_2"], 1024))
        for e in ("dve", "pool"):
            p.wait(e, cok)
        ys = Ring([Slot(y[:, i], p.slot_sem(f"c_y{i}")) for i in range(8)])
        hs = Ring([Slot(h[:, i], p.slot_sem(f"c_h{i}")) for i in range(3)])
        os_ = Ring([Slot(o[:, i], p.slot_sem(f"c_o{i}")) for i in range(2)])
        erow = sb("erow", [128, 32])
        eq = sb("eq", [128, 64, 32])
        eok = p.dma("act", cslot, erow[:], A["erow"])
        p.wait("dve", eok)

        def v(ins):
            tok = p.inc("dve", ins)
            p.wait("dve", tok)
            return tok

        v(nc.vector.tensor_tensor(eq[:], erow[:].unsqueeze(1).to_broadcast([128, 64, 32]),
                                  R.idf[:].rearrange("p a b -> p (a b)").unsqueeze(2).to_broadcast([128, 64, 32]), ALU.is_equal))
        v(nc.vector.tensor_tensor(eq[:], eq[:], R.base[:].unsqueeze(1).to_broadcast([128, 64, 32]), ALU.mult))
        sf = sb("sf", [128, 64])
        v(nc.vector.tensor_reduce(sf[:], eq[:], AX, ALU.add))
        v(nc.vector.tensor_tensor(sf[:], sf[:], R.pos[:].rearrange("p a b -> p (a b)"), ALU.add))
        sl = v(nc.vector.tensor_copy(R.slot[:].rearrange("p a b -> p (a b)"), sf[:]))
        p.wait("pool", sl)
        loaded = {}

        def load(i):
            a = hs.next()
            p.wait("sp", *a.free)
            a.full = [p.dma("sp", a, a.ap, h1d[i * 128:(i + 1) * 128, :])]
            g = []
            for k in range(4):
                s = ys.next()
                p.wait("pool", *s.free)
                nc.gpsimd.indirect_dma_start(out=s.ap, out_offset=None, in_=yd[0:YB * 128, :],
                                             in_offset=bass.IndirectOffsetOnAxis(ap=R.slot[:, i, k:k + 1], axis=0)).then_inc(s.sem, 16)
                s.n += 16
                s.full = [(s.sem, s.n)]
                p.dmas.append((s.sem, s.n))
                g.append(s)
            loaded[i] = (a, g)

        load(0)
        load(1)
        for i in range(16):
            a, g = loaded[i]
            p.wait("dve", *a.full)
            t = p.inc("dve", nc.vector.tensor_scalar(a.ap, a.ap, ALPHA, None, ALU.mult))
            for k, s in enumerate(g):
                p.wait("dve", t, *s.full)
                t = p.inc("dve", nc.vector.scalar_tensor_tensor(out=a.ap, in0=s.ap, scalar=R.gate[:, i, k:k + 1], in1=a.ap,
                                                                op0=ALU.mult, op1=ALU.add))
                s.free = [t]
            if i + 2 < 16:
                load(i + 2)
            q = os_.next()
            z = st[:, i % 2, :]
            t = layer_norm(p, a.ap, 1024, 128, z[:, 0:12], z[:, 12:14], z[:, 14:15], z[:, 15:16], eps_ln,
                           q.ap, LN[:, 0, :], LN[:, 1, :], [t], q.free, "dve")
            a.free = [t]
            p.wait("sp", t)
            q.free = [p.dma("sp", q, out[i * 128:(i + 1) * 128, :], q.ap)]
        p.close()


F32R = mybir.dt.float32r


def phase_experts(p, A, h1d, tabd, yd, R, ident):
    nc = p.nc
    with ExitStack() as ctx:
        def sb(name, shape, dt=F32):
            return ctx.enter_context(nc.sbuf_tensor("e_" + name, shape, dt))

        def sem(name):
            return nc.alloc_semaphore("e_" + name)

        def sems(name, n):
            return [sem(f"{name}{i}") for i in range(n)]

        banks = [ctx.enter_context(nc.psum_tensor(f"e_ps{i}", [128, 512], F32)) for i in range(8)]
        G, TX, TA = banks[0:4], banks[4:6], banks[6:8]
        raw = sb("raw", [128, 2, 8, 512])
        wh = sb("wh", [128, 2, 8, 512], F32R)
        wl = sb("wl", [128, 2, 8, 512], F32R)
        bg = sb("bg", [128, 2048])
        bd = sb("bd", [128, 1024])
        idx = sb("idx", [128, 4], I32)
        hx = sb("hx", [128, 2, 1024])
        hTh = sb("hTh", [128, 4, 8, 128], F32R)
        hTl = sb("hTl", [128, 4, 8, 128], F32R)
        aTh = sb("aTh", [128, 4, 8, 128], F32R)
        aTl = sb("aTl", [128, 4, 8, 128], F32R)
        tt = sb("tt", [128, 512])
        gg = sb("gg", [128, 256])
        uu = sb("uu", [128, 256])
        sg = sb("sg", [128, 256])
        act = sb("act", [128, 4, 256])
        Y = sb("Y", [128, 4, 512])
        junk = sb("junk", [1, 8])

        raw_full, raw_free = sems("raw_full", 2), sems("raw_free", 2)
        hi_full = sem("hi_full")
        w_full, w_free = sem("w_full"), sem("w_free")
        bg_full, bg_free = sem("bg_full"), sem("bg_free")
        bd_full, bd_free = sem("bd_full"), sem("bd_free")
        idx_full, idx_seen = sem("idx_full"), sem("idx_seen")
        rows_in = sem("rows_in")
        hx_full, hx_free = sems("hx_full", 2), sems("hx_free", 2)
        x_full, x_hi, x_free = sems("x_full", 2), sems("x_hi", 2), sems("x_free", 2)
        hT_full = sems("hT_full", 4)
        a_full, a_hi, a_free = sems("a_full", 2), sems("a_hi", 2), sems("a_free", 2)
        aT_full = sems("aT_full", 4)
        g_full, g_free = sems("g_full", 4), sems("g_free", 4)
        glu, sig = sem("glu"), sem("sig")
        act_full = sems("act_full", 4)
        out_full, out_free = sems("out_full", 4), sems("out_free", 4)
        dv = sem("dv")

        def take(eng, s, n=1):
            eng.wait_ge(s, n)
            eng.sem_inc(s, -n)

        sp, pe, dve, act_e, pool = nc.sync, nc.tensor, nc.vector, nc.scalar, nc.gpsimd
        for s in g_free + a_free + x_free + [bg_free, bd_free] + raw_free:
            dve.sem_inc(s, 1)
        for s in hx_free:
            pe.sem_inc(s, 1)
        pe.sem_inc(w_free, 1)
        for s in out_free:
            act_e.sem_inc(s, 16)

        def bank(c, b):
            return (b + 2 * c) % 4

        def tab(eng, row, q, lo, hi):
            return eng.value_load(R.tab[row:row + 1, bass.ds(q, 1)], min_val=lo, max_val=hi)

        def groups(eng):
            return eng.Fori(0, eng.value_load(R.ngr[0:1, 0:1], min_val=1, max_val=GT - 1))

        def below(eng, b, r):
            return eng.If(r > b)

        def load_raw(c, src):
            take(sp, raw_free[c % 2])
            sp.dma_start(raw[:, c % 2].rearrange("p k n -> p (k n)"), src).then_inc(raw_full[c % 2], 16)

        with groups(sp) as q:
            e = tab(sp, 0, q, 0, NE - 1)
            for c in range(6):
                src = A["wgu"][bass.ds(e, 1), c] if c < 4 else A["wdn"][bass.ds(e, 1), c - 4]
                load_raw(c, src.rearrange("o p n -> p (o n)"))
                if c == 0:
                    take(sp, bg_free)
                    sp.dma_start(bg[:], A["bgu"][bass.ds(e, 1), :].broadcast_to([128, 2048])).then_inc(bg_full, 16)
                if c == 2:
                    take(sp, bd_free)
                    sp.dma_start(bd[:], A["bdn"][bass.ds(e, 1), :].broadcast_to([128, 1024])).then_inc(bd_full, 16)
        load_raw(0, A["wgu"][0, 0])

        with groups(pool) as q:
            r = tab(pool, 1, q, 1, 4)
            row = tab(pool, 2, q, 0, NE * CAP - 512)
            blk = tab(pool, 3, q, 0, YB)
            pool.dma_start(idx[:], tabd[bass.ds(row, 512), :].rearrange("(j p) o -> p (j o)", p=128),
                           allow_slow_non_contiguous=True).then_inc(idx_full, 16)
            pool.wait_ge(idx_full, q * 16 + 16)
            pool.sem_inc(idx_seen, 1)
            for b in range(4):
                with below(pool, b, r):
                    take(pool, hx_free[b % 2])
                    pool.indirect_dma_start(out=hx[:, b % 2, :], out_offset=None, in_=h1d,
                                            in_offset=bass.IndirectOffsetOnAxis(ap=idx[:, b:b + 1], axis=0)).then_inc(rows_in, 16)
                    pool.wait_ge(rows_in, blk * 16 + (16 * b + 16))
                    pool.sem_inc(hx_full[b % 2], 1)

        def pe_rows(b):
            take(pe, hx_full[b % 2])
            for hf in range(2):
                take(pe, x_free[hf])
                for k in range(4):
                    t = pe.transpose(TX[hf][:, k * 128:(k + 1) * 128],
                                     hx[:, b % 2, (4 * hf + k) * 128:(4 * hf + k + 1) * 128], ident[:])
                t.then_inc(x_full[hf], 1)

        def pe_product(c, b):
            ph, pl = (hTh, hTl) if c < 4 else (aTh, aTl)
            g = bank(c, b)
            take(pe, g_free[g])
            n = 0
            for k in range(8):
                if b == 0 and k % 2 == 0:
                    take(pe, w_full)
                for x, y in ((ph, wh), (ph, wl), (pl, wh)):
                    t = pe.matmul(G[g][:, :], x[:, b, k, :], y[:, c % 2, k, :], start=(n == 0), stop=(n == 23))
                    if n == 0 and b == 0:
                        t.then_inc(w_free, 1)
                    n += 1
            t.then_inc(g_full[g], 1)

        def pe_acts(c, b):
            take(pe, act_full[b])
            take(pe, a_free[b % 2])
            for k in range(2):
                t = pe.transpose(TA[b % 2][:, k * 128:(k + 1) * 128], act[:, b, k * 128:(k + 1) * 128], ident[:])
            t.then_inc(a_full[b % 2], 1)

        def act_hi(c):
            n = (c + 1) % 6
            take(act_e, raw_full[n % 2], 16)
            take(act_e, w_free)
            for i in range(4):
                act_e.copy(wh[:, n % 2, 2 * i:2 * i + 2, :].rearrange("p k n -> p (k n)"),
                           raw[:, n % 2, 2 * i:2 * i + 2, :].rearrange("p k n -> p (k n)")).then_inc(hi_full, 1)

        def act_rows(b):
            for hf in range(2):
                take(act_e, x_full[hf])
                act_e.copy(hTh[:, b, 4 * hf:4 * hf + 4, :].rearrange("p a b -> p (a b)"), TX[hf][:, :]).then_inc(x_hi[hf], 1)

        def act_acts(c, b):
            take(act_e, a_full[b % 2])
            act_e.copy(aTh[:, b, 2 * c:2 * c + 2, :].rearrange("p a b -> p (a b)"), TA[b % 2][:, 0:256]).then_inc(a_hi[b % 2], 1)

        def act_sig(b):
            take(act_e, glu)
            act_e.activation(sg[:], gg[:], ACT.Sigmoid, scale=1.702).then_inc(sig, 1)

        def act_store(c, b, blk):
            take(act_e, out_full[b])
            act_e.dma_start(yd[bass.ds((blk + b) * 128, 128), (c - 4) * 512:(c - 3) * 512], Y[:, b, :]).then_inc(out_free[b], 16)

        def link(ins):
            ins.then_inc(dv, 1)
            take(dve, dv)

        def tell(s, cell):
            link(dve.memset(junk[0:1, cell:cell + 1], 0.0))
            dve.sem_inc(s, 1)

        def f(ap):
            return ap.bitcast(F32)

        def dve_lo(c):
            n = (c + 1) % 6
            for i in range(4):
                take(dve, hi_full)
                dve.tensor_tensor(wl[:, n % 2, 2 * i:2 * i + 2, :].rearrange("p k n -> p (k n)"),
                                  raw[:, n % 2, 2 * i:2 * i + 2, :].rearrange("p k n -> p (k n)"),
                                  f(wh[:, n % 2, 2 * i:2 * i + 2, :].rearrange("p k n -> p (k n)")), ALU.subtract).then_inc(w_full, 1)
            tell(raw_free[n % 2], n % 2)

        def dve_rows(b):
            for hf in range(2):
                take(dve, x_hi[hf])
                dve.tensor_tensor(hTl[:, b, 4 * hf:4 * hf + 4, :].rearrange("p a b -> p (a b)"), TX[hf][:, :],
                                  f(hTh[:, b, 4 * hf:4 * hf + 4, :].rearrange("p a b -> p (a b)")), ALU.subtract).then_inc(x_free[hf], 1)
            link(dve.memset(junk[0:1, 2:3], 0.0))
            dve.sem_inc(hT_full[b], 1)
            dve.sem_inc(hx_free[b % 2], 1)

        def dve_acts(c, b):
            take(dve, a_hi[b % 2])
            dve.tensor_tensor(aTl[:, b, 2 * c:2 * c + 2, :].rearrange("p a b -> p (a b)"), TA[b % 2][:, 0:256],
                              f(aTh[:, b, 2 * c:2 * c + 2, :].rearrange("p a b -> p (a b)")), ALU.subtract).then_inc(a_free[b % 2], 1)
            if c == 3:
                link(dve.memset(junk[0:1, 2:3], 0.0))
                dve.sem_inc(aT_full[b], 1)

        def dve_item(c, b):
            g = bank(c, b)
            take(dve, g_full[g])
            dve.tensor_tensor(tt[:], G[g][:, :], bg[:, c * 512:(c + 1) * 512], ALU.add).then_inc(g_free[g], 1)
            link(dve.memset(junk[0:1, 3:4], 0.0))
            dve.tensor_scalar(gg[:], tt[:, 0:256], 7.0, None, ALU.min).then_inc(glu, 1)
            link(dve.tensor_scalar(uu[:], tt[:, 256:512], 7.0, -7.0, ALU.min, ALU.max))
            link(dve.scalar_tensor_tensor(out=uu[:], in0=uu[:], scalar=1.0, in1=gg[:], op0=ALU.add, op1=ALU.mult))
            take(dve, sig)
            dve.tensor_tensor(act[:, b, :], uu[:], sg[:], ALU.mult).then_inc(act_full[b], 1)

        def dve_out(c, b):
            g = bank(c, b)
            take(dve, g_full[g])
            take(dve, out_free[b], 16)
            dve.tensor_tensor(Y[:, b, :], G[g][:, :], bd[:, (c - 4) * 512:(c - 3) * 512], ALU.add).then_inc(out_full[b], 1)
            tell(g_free[g], 4)

        r0 = tab(pe, 1, 0, 1, 4)
        for b in range(4):
            with below(pe, b, r0):
                pe_rows(b)
        with groups(pe) as q:
            r = tab(pe, 1, q, 1, 4)
            rn = tab(pe, 1, q + 1, 0, 4)
            for c in range(6):
                for b in range(4):
                    with below(pe, b, r):
                        if c == 0:
                            take(pe, hT_full[b])
                        if 1 <= c <= 4:
                            pe_acts(c - 1, b)
                        if c == 4:
                            with below(pe, b, rn):
                                pe_rows(b)
                            take(pe, aT_full[b])
                        pe_product(c, b)
                if c == 4:
                    for b in range(1, 4):
                        with pe.If(r <= b):
                            with below(pe, b, rn):
                                pe_rows(b)

        ra = tab(act_e, 1, 0, 1, 4)
        act_hi(-1)
        for b in range(4):
            with below(act_e, b, ra):
                act_rows(b)
        with groups(act_e) as q:
            r = tab(act_e, 1, q, 1, 4)
            rn = tab(act_e, 1, q + 1, 0, 4)
            blk = tab(act_e, 3, q, 0, YB)
            for c in range(6):
                if c == 4:
                    act_acts(3, 0)
                    with below(act_e, 0, rn):
                        act_rows(0)
                if c == 5:
                    for b in range(4):
                        with below(act_e, b, r):
                            act_store(4, b, blk)
                act_hi(c)
                for b in range(4):
                    with below(act_e, b, r):
                        if c in (1, 2, 3) or (c == 4 and b > 0):
                            act_acts(c - 1, b)
                        if c == 4 and b > 0:
                            with below(act_e, b, rn):
                                act_rows(b)
                        if c < 4:
                            act_sig(b)
                        if c == 5:
                            act_store(5, b, blk)
                if c == 4:
                    for b in range(1, 4):
                        with act_e.If(r <= b):
                            with below(act_e, b, rn):
                                act_rows(b)

        rd = tab(dve, 1, 0, 1, 4)
        dve_lo(-1)
        for b in range(4):
            with below(dve, b, rd):
                dve_rows(b)
        with groups(dve) as q:
            r = tab(dve, 1, q, 1, 4)
            rn = tab(dve, 1, q + 1, 0, 4)
            for c in range(6):
                if c == 0:
                    take(dve, bg_full, 16)
                if c == 4:
                    dve_acts(3, 0)
                    with below(dve, 0, rn):
                        dve_rows(0)
                    take(dve, bd_full, 16)
                dve_lo(c)
                for b in range(4):
                    with below(dve, b, r):
                        if c in (1, 2, 3):
                            dve_acts(c - 1, b)
                        if c == 4 and b > 0:
                            dve_acts(3, b)
                            with below(dve, b, rn):
                                dve_rows(b)
                        if c < 4:
                            dve_item(c, b)
                        else:
                            dve_out(c, b)
                if c == 3:
                    tell(bg_free, 5)
                if c == 4:
                    for b in range(1, 4):
                        with dve.If(r <= b):
                            with below(dve, b, rn):
                                dve_rows(b)
                if c == 5:
                    tell(bd_free, 6)
        for s in out_free:
            dve.wait_ge(s, 16)
        p.inc("dve", dve.memset(junk[0:1, 7:8], 0.0))
        p.close()


def build(nc, A, out, stop=9, dbg=None):
    p = Prog(nc)
    ident = nc.alloc_sbuf_tensor("ident", [128, 128], F32)
    eps_ln = nc.alloc_sbuf_tensor("eps_ln", [128, 1], F32)
    eps_rms = nc.alloc_sbuf_tensor("eps_rms", [128, 1], F32)
    h0d = nc.dram_tensor("h0d", (L, D), F32).ap()
    isl = Slot(None, p.slot_sem("ident_in"))
    t = p.dma("sp", isl, ident[:], A["ident"])
    a = p.inc("dve", nc.vector.memset(eps_ln[:], LN_EPS))
    b = p.inc("dve", nc.vector.memset(eps_rms[:], RMS_EPS))
    for e in ("pe", "dve", "act", "pool"):
        p.wait(e, t, a, b)
    phase_mixer(p, A, h0d, ident, eps_ln)
    if stop == 1:
        return h0d
    yd = nc.dram_tensor("yd", ((YB + 16) * 128, D), F32).ap()
    qTd = nc.dram_tensor("qTd", (2, 10, 128, S), F32).ap()
    kTd = nc.dram_tensor("kTd", (2, 7, 128, L), F32).ap()
    vd = nc.dram_tensor("vd", (6, 128, NT, 128), F32).ap()
    od = nc.dram_tensor("od", (S, D), F32).ap()
    phase_project(p, A, h0d, qTd, kTd, vd, ident, eps_rms)
    phase_attend(p, qTd, kTd, vd, od, yd, ident)
    if stop == 2:
        return
    h1d = nc.dram_tensor("h1d", (S, D), F32).ap()
    tabd = nc.dram_tensor("tabd", (NE * CAP, 1), I32).ap()
    R = alloc_route(nc)
    phase_route(p, A, h0d, od, h1d, tabd, R, ident, eps_ln, eps_rms)
    if stop == 3:
        return
    phase_experts(p, A, h1d, tabd, yd, R, ident)
    if stop == 4:
        return
    phase_combine(p, A, h1d, yd, R, out, eps_ln)


def host_arrays(x, mem, w_in, conv_a_w, sg_ln_g, sg_ln_b, sg_w, sg_b, pool_w, pool_scale, cc_dw_w, cc_dw_b,
                cc_ln_g, cc_ln_b, cc_pw_w, w_kv, w_out, ln_g, ln_b, meta_tokens_2, ln_emb_g_2, ln_emb_b_2,
                w_in_2, g_q_a_2, w_q_b_2, g_kv_a_2, w_kv_b_2, g_q_gqa_2, g_k_gqa_2, g_o_mla_2, g_o_gqa_2,
                w_o_2, ln1_g_2, ln1_b_2, w_router_2, b_router_2, w_gate_up_2, b_gate_up_2, w_down_2,
                b_down_2, ln2_g_2, ln2_b_2):
    def kp(w):
        k = w.shape[0] // 128
        return np.ascontiguousarray(w.reshape(k, 128, -1).transpose(1, 0, 2))

    def cols(v):
        return v.reshape(-1, 128).T

    A = {}
    A["x"] = x[0]
    A["xT"] = kp(x[0].T)
    A["memT"] = kp(mem[0].T)
    A["w1"] = np.ascontiguousarray(w_in[0].reshape(8, 128, 14, 256).transpose(2, 1, 0, 3))
    A["wkv"] = kp(w_kv[0])
    A["wout"] = kp(w_out[0])
    A["sgw"] = np.ascontiguousarray(sg_w[0].transpose(2, 0, 1))
    A["sgb"] = np.ascontiguousarray(np.repeat(sg_b[0], 64, axis=0).reshape(2, 128, 128).transpose(1, 0, 2))
    bd = np.zeros((128, 2, 128), pool_w.dtype)
    for g in range(4):
        lo = 64 * (g % 2)
        bd[lo:lo + 64, g // 2, lo:lo + 64] = pool_w[0, g]
    A["poolw"] = bd
    A["pw"] = kp(cc_pw_w[0])
    A["pc"] = np.ascontiguousarray(np.concatenate(
        [cols(conv_a_w[0]), cols(cc_dw_w[0]), cols(cc_dw_b[0]), cols(cc_ln_g[0]), cols(cc_ln_b[0]),
         cols(pool_scale[0]), cols(g_q_a_2[0]), cols(g_kv_a_2[0])], axis=1))
    for n, v in (("sg_ln_g", sg_ln_g), ("sg_ln_b", sg_ln_b), ("ln_g", ln_g), ("ln_b", ln_b),
                 ("g_q_gqa_2", g_q_gqa_2), ("g_k_gqa_2", g_k_gqa_2), ("ln1_g_2", ln1_g_2), ("ln1_b_2", ln1_b_2),
                 ("ln2_g_2", ln2_g_2), ("ln2_b_2", ln2_b_2), ("b_router_2", b_router_2)):
        A[n] = v[0]
    A["g_o"] = np.concatenate([g_o_mla_2[0], g_o_gqa_2[0]])
    A["ln_emb_g_2"], A["ln_emb_b_2"] = ln_emb_g_2, ln_emb_b_2
    A["meta"] = meta_tokens_2
    A["w2"] = kp(w_in_2[0])
    A["wqb"] = kp(w_q_b_2[0])
    A["wkvb"] = w_kv_b_2[0]
    A["wo2"] = kp(w_o_2[0])
    A["wr"] = kp(w_router_2[0])
    gu = w_gate_up_2[0].reshape(32, 8, 128, 4, 256, 2)
    A["wgu"] = np.ascontiguousarray(gu.transpose(0, 3, 2, 1, 5, 4)).reshape(32, 4, 128, 4096)
    A["bgu"] = np.ascontiguousarray(b_gate_up_2[0].reshape(32, 4, 256, 2).transpose(0, 1, 3, 2)).reshape(32, 2048)
    A["wdn"] = np.ascontiguousarray(w_down_2[0].reshape(32, 8, 128, 2, 512).transpose(0, 3, 2, 1, 4)).reshape(32, 2, 128, 4096)
    A["bdn"] = b_down_2[0]
    return A


def shape_constants():
    C = {}
    f = np.float32
    C["onm"] = np.full((128, 128), 1.0 / 256, f)
    i = np.arange(128)
    C["tri"] = (i[:, None] <= i[None, :]).astype(f)
    C["ident"] = np.eye(128, dtype=f)
    C["before"] = (i[:, None] < i[None, :]).astype(f)
    prc = np.zeros((128, 2, 17), f)
    for g, w in enumerate((2, 4, 8, 16)):
        lo = 64 * (g % 2)
        prc[lo:lo + 64, g // 2, 0:16] = f(1) / np.minimum(np.arange(16) + 1, w).astype(f)
        prc[lo:lo + 64, g // 2, 16] = 1.0 / w
    C["prc"] = prc
    t = np.arange(S)
    pos = np.concatenate([t + NM, np.arange(NM)])
    row = np.concatenate([t // 64, np.full(NM, -1)])
    col = np.concatenate([t % 64, np.arange(NM)])

    def rope(p_, dim):
        inv = f(10000.0) ** (-np.arange(0, dim, 2, dtype=f) / f(dim))
        ang = p_.astype(f)[:, None] * inv[None, :].astype(f)
        return np.cos(ang).astype(f), np.sin(ang).astype(f)

    c1, s1 = rope(pos, 64)
    cr, sr = rope(row, 64)
    cc, sc = rope(col, 64)
    R = np.concatenate([c1, c1, -s1, s1, cr, cr, cc, cc, -sr, sr, -sc, sc], axis=1)
    pad = np.zeros((17 * 128 - L, R.shape[1]), f)
    C["rope"] = np.ascontiguousarray(np.concatenate([R, pad]).reshape(17, 128, 384))
    C["qcol"] = np.arange(128, dtype=f).reshape(128, 1)
    C["erow"] = np.broadcast_to(np.arange(32, dtype=f), (128, 32)).copy()
    C["thr"] = np.broadcast_to(np.arange(1, 16, dtype=f) * 128, (128, 15)).copy()
    C["tokid"] = np.ascontiguousarray(np.arange(S, dtype=np.int32).reshape(16, 128).T)
    return C


def kernel(**inputs):
    import numpy as _np
    import concourse.bacc as _bacc
    from concourse import mybir as _mybir
    from concourse.bass_utils import run_bass_kernel_spmd as _run

    nc = _bacc.Bacc("TRN2", target_bir_lowering=False, num_devices=1)
    arrays = host_arrays(**{k: _np.asarray(v) for k, v in inputs.items()})
    arrays.update(shape_constants())
    arrays = {"in_" + k: _np.ascontiguousarray(v) for k, v in arrays.items()}
    A = {k[3:]: nc.dram_tensor(k, v.shape, _mybir.dt.from_np(v.dtype), kind="ExternalInput").ap()
         for k, v in arrays.items()}
    out = nc.dram_tensor("out_0", (S, D), _mybir.dt.float32, kind="ExternalOutput").ap()
    build(nc, A, out)
    r = _run(nc, [arrays], core_ids=[0])
    return r.results[0]["out_0"].reshape(1, S, D)
```

```python
from contextlib import ExitStack

import numpy as np

import concourse.bass as bass
from concourse import mybir

ALU = mybir.AluOpType
ACT = mybir.ActivationFunctionType
AX = mybir.AxisListType.X
F32 = mybir.dt.float32
I32 = mybir.dt.int32
U32 = mybir.dt.uint32

S = 2048
D = 1024
NM = 16
L = S + NM
NE = 32
CAP = 2048
GT = 49
YB = 96
ALPHA = 2.0 ** 0.25
LN_EPS = 1e-5
RMS_EPS = 1e-6
CH = 512
SQK_M = 192 ** -0.5
SQK_G = 128 ** -0.5

PC_CONVA, PC_DW, PC_DWB, PC_CLG, PC_CLB, PC_PS, PC_GQA, PC_GKV = 0, 6, 68, 70, 72, 74, 76, 78
PC_N = 79


class Slot:

    def __init__(self, ap, sem=None):
        self.ap, self.sem, self.n = ap, sem, 0
        self.full, self.free = [], []


class Ring:
    def __init__(self, slots):
        self.slots, self.i = slots, 0

    def next(self):
        s = self.slots[self.i % len(self.slots)]
        self.i += 1
        return s


class Prog:

    def __init__(self, nc):
        self.nc = nc
        self.eng = {"pe": nc.tensor, "dve": nc.vector, "act": nc.scalar, "pool": nc.gpsimd, "sp": nc.sync}
        self.nphase = 0
        self.open()

    def open(self):
        self.sem = {e: self.nc.alloc_semaphore(f"s{self.nphase}_{e}") for e in ("pe", "dve", "act", "pool")}
        self.cnt = {e: 0 for e in self.sem}
        self.seen = {}
        self.dmas = []
        self.nphase += 1

    def inc(self, e, ins):
        ins.then_inc(self.sem[e], 1)
        self.cnt[e] += 1
        return (self.sem[e], self.cnt[e])

    def wait(self, e, *toks):
        for sem, n in toks:
            key = (e, sem.name)
            if self.seen.get(key, 0) < n:
                self.eng[e].wait_ge(sem, n)
                self.seen[key] = n

    def slot_sem(self, name):
        return self.nc.alloc_semaphore(name)

    def dma(self, e, slot, out, in_, **kw):
        self.eng[e].dma_start(out, in_, **kw).then_inc(slot.sem, 16)
        slot.n += 16
        t = (slot.sem, slot.n)
        self.dmas.append(t)
        return t

    def close(self, last_phase=False):
        last = {}
        for sem, n in self.dmas:
            last[sem.name] = (sem, n)
        ends = list(last.values()) + [(self.sem[e], self.cnt[e]) for e in self.sem if self.cnt[e]]
        for e in self.eng:
            self.wait(e, *ends)
        if not last_phase:
            self.open()


def bcast(ap1d, n):
    return ap1d.rearrange("(o n) -> o n", o=1).broadcast_to([128, n])


def layer_norm(p, x, n, rows, st, mv, sd, rs, eps_t, out, g, b, ready, out_free, eng2="dve"):
    nc = p.nc
    k = max(1, n // 512)
    w = n // k
    p.wait("dve", *ready)
    for i in range(k):
        t = p.inc("dve", nc.vector.bn_stats(st[:rows, i * 6:(i + 1) * 6], x[:rows, i * w:(i + 1) * w]))
    p.wait("dve", t)
    t = p.inc("dve", nc.vector.bn_aggr(mv[:rows, :], st[:rows, 0:6 * k]))
    p.wait("act", t)
    t = p.inc("act", nc.scalar.activation(sd[:rows, :], mv[:rows, 1:2], ACT.Sqrt, bias=eps_t[:rows, :], scale=1.0))
    p.wait("dve", t)
    t = p.inc("dve", nc.vector.reciprocal(rs[:rows, :], sd[:rows, :]))
    p.wait("dve", t, *out_free)
    t = p.inc("dve", nc.vector.tensor_scalar(out[:rows, :n], x[:rows, :n], mv[:rows, 0:1], rs[:rows, 0:1],
                                             ALU.subtract, ALU.mult))
    p.wait(eng2, t)
    t = p.inc(eng2, p.eng[eng2].tensor_tensor(out[:rows, :n], out[:rows, :n], g[:rows, :n], ALU.mult))
    p.wait(eng2, t)
    return p.inc(eng2, p.eng[eng2].tensor_tensor(out[:rows, :n], out[:rows, :n], b[:rows, :n], ALU.add))


def phase_mixer(p, A, h0d, ident, eps_ln):
    nc = p.nc
    with ExitStack() as ctx:
        def sb(name, shape, dt=F32):
            return ctx.enter_context(nc.sbuf_tensor("m_" + name, shape, dt))

        banks = [ctx.enter_context(nc.psum_tensor(f"m_ps{i}", [128, 512], F32)) for i in range(8)]
        PR = Ring([Slot(b) for b in banks[0:3]])
        MS = Ring([Slot(b) for b in banks[3:8]])

        xT = sb("xT", [128, 2, 8, CH])
        xTs = [Slot(xT[:, i], p.slot_sem(f"m_xT{i}")) for i in range(2)]
        NW = 4
        wt = sb("wt", [128, NW, 8, 256])
        W = Ring([Slot(wt[:, i], p.slot_sem(f"m_w{i}")) for i in range(NW)])
        wo = sb("wo", [128, 10, 1024])
        yT = sb("yT", [128, 10, CH])
        pc = sb("pc", [128, PC_N])
        wsg = sb("wsg", [128, 4, 128])
        tri = sb("tri", [128, 128])
        sgb = sb("sgb", [128, 2, 128])
        poolw = sb("poolw", [128, 2, 128])
        pw = sb("pw", [128, 2, 256])
        prc = sb("prc", [128, 2, 17])
        onm = sb("onm", [128, 128])
        lngb = sb("lngb", [128, 2, 256])
        LN = sb("LN", [128, 4, 1024])
        kT = sb("kT", [128, 2, 256])
        vm = sb("vm", [128, 2, 256])
        At = sb("At", [128, 2, 2 + CH])
        Dt = sb("Dt", [128, 2, 30 + CH])
        Ct = sb("Ct", [128, 2, 15 + CH])
        qT = sb("qT", [128, 2, CH])
        acc = sb("acc", [128, 2, CH])
        tmp = sb("tmp", [128, 2, CH])
        tmp2 = sb("tmp2", [128, 2, 15 + CH])
        gvn = sb("gvn", [128, 4, 256])
        pe_ = sb("pe_", [128, 4, 256])
        pT = sb("pT", [128, 8, 128])
        st = sb("st", [128, 64])
        xr = sb("xr", [128, 2, 1024])
        h0 = sb("h0", [128, 1, 1024])

        cs = p.slot_sem("m_const")
        cslot = Slot(None, cs)

        def const(dst, src, e="sp"):
            cslot.full.append(p.dma(e, cslot, dst, src))

        const(pc[:], A["pc"], "act")
        memT = xT[:, 1, 0:4, :].rearrange("p a b -> p (a b)").rearrange("p (k m) -> p k m", k=8)
        wkv = wt[:, 2:4].rearrange("p a k n -> p (a k n)").rearrange("p (k n) -> p k n", k=8)
        const(memT, A["memT"])
        const(wkv, A["wkv"])
        xTs[0].full = [p.dma("sp", xTs[0], xTs[0].ap, A["xT"][:, :, 0:CH])]
        const(onm[:], A["onm"], "act")
        const(wsg[:], A["sgw"], "act")
        const(tri[:], A["tri"], "act")
        const(sgb[:], A["sgb"], "act")
        const(poolw[:], A["poolw"], "act")
        const(pw[:], A["pw"], "act")
        const(prc[:], A["prc"], "act")
        const(lngb[:, 0, :], bcast(A["sg_ln_g"], 256), "act")
        const(lngb[:, 1, :], bcast(A["sg_ln_b"], 256), "act")
        consts = [cslot.full[-1]]
        lnslot = Slot(None, p.slot_sem("m_LN"))
        for i, n in enumerate(("ln_g", "ln_b", "ln_emb_g_2", "ln_emb_b_2")):
            ln_ok = p.dma("act", lnslot, LN[:, i, :], bcast(A[n], 1024))
        for e in ("pe", "dve", "act", "pool"):
            p.wait(e, *consts)
        t = p.inc("pool", nc.gpsimd.memset(At[:, :, 0:2], 0.0))
        t = p.inc("pool", nc.gpsimd.memset(Dt[:, :, 0:30], 0.0))
        halo0 = p.inc("pool", nc.gpsimd.memset(Ct[:, :, 0:15], 0.0))
        halo = {"A": [halo0], "D": [halo0], "C": [halo0]}
        t = [p.inc("pool", nc.gpsimd.tensor_tensor(wsg[:, h, :], wsg[:, h, :], tri[:], ALU.mult)) for h in range(4)]
        wsg_ok = t[-1]
        s = MS.next()
        for j in range(2):
            for k in range(8):
                t = nc.tensor.matmul(s.ap[:, j * 256:(j + 1) * 256], wkv[:, k, j * 128:(j + 1) * 128], memT[:, k, :],
                                     start=(k == 0), stop=(k == 7))
        t = p.inc("pe", t)
        p.wait("act", t)
        kv_ok = p.inc("act", nc.scalar.copy(kT[:].rearrange("p a b -> p (a b)"), s.ap[:, :]))
        s.free = [kv_ok]
        s = MS.next()
        for j in range(2):
            for k in range(8):
                t = nc.tensor.matmul(s.ap[:, j * 256:(j + 1) * 256], memT[:, k, j * 128:(j + 1) * 128], wkv[:, k, 256:512],
                                     start=(k == 0), stop=(k == 7))
        kvpe = p.inc("pe", t)
        p.wait("act", kvpe)
        kv_ok = p.inc("act", nc.scalar.copy(vm[:].rearrange("p a b -> p (a b)"), s.ap[:, :]))
        s.free = [kv_ok]
        W.slots[2].free = W.slots[3].free = [kvpe]
        xTs[1].free = [kvpe]

        order = [7, 6, 8, 5, 4, 0, 2, 1, 3, 9, 10, 11, 12, 13]
        loads = [(c, g) for c in range(4) for g in order]
        issued = {}

        def issue(n):
            if n >= len(loads):
                return
            c, g = loads[n]
            s = W.next()
            p.wait("sp", *s.free)
            s.full = [p.dma("sp", s, s.ap, A["w1"][g])]
            issued[(c, g)] = s

        for n in range(NW):
            issue(n)
        wos = Slot(wo[:], p.slot_sem("m_wo"))
        wos.full = [p.dma("sp", wos, wo[:], A["wout"])]
        nl = [NW]

        xrs = Ring([Slot(xr[:, i], p.slot_sem(f"m_xr{i}")) for i in range(2)])
        h0s = Ring([Slot(h0[:, 0], p.slot_sem("m_h00"))])

        def proj(c, g, each, also=None):
            if also:
                next(also)
            w = issued[(c, g)]
            x = xTs[c % 2]
            p.wait("pe", *w.full, *x.full)
            for j in range(2):
                s = PR.next()
                p.wait("pe", *s.free)
                for k in range(8):
                    t = nc.tensor.matmul(s.ap[:, :], w.ap[:, k, j * 128:(j + 1) * 128], x.ap[:, k, :],
                                         start=(k == 0), stop=(k == 7))
                t = p.inc("pe", t)
                s.free = [each(j, s.ap, t)]
                if also:
                    next(also, None)
            w.free = [t]
            x.free = [t]
            issue(nl[0])
            nl[0] += 1

        sgq = {}
        Y = {}
        free = {}

        def fr(name):
            return free.get(name, [])

        for c in range(4):
            def e_dg(j, ps, t):
                p.wait("act", t, *fr("tmp"))
                sgq[j] = p.inc("act", nc.scalar.activation(tmp[:, j, :], ps[:, :], ACT.Sigmoid))
                return sgq[j]

            proj(c, 7, e_dg)
            dok = {}

            def e_da(j, ps, t):
                p.wait("dve", t, sgq[j], *fr("D"))
                dok[j] = p.inc("dve", nc.vector.tensor_tensor(Dt[:, j, 30:], ps[:, :], tmp[:, j, :], ALU.mult))
                return dok[j]

            proj(c, 6, e_da)
            free["tmp"] = [dok[1]]

            def e_q(j, ps, t):
                p.wait("act", t, *fr("q"))
                sgq["q"] = p.inc("act", nc.scalar.copy(qT[:, j, :], ps[:, :]))
                return sgq["q"]

            proj(c, 8, e_q)
            q_ok = sgq["q"]

            t2 = {}
            for j in range(2):
                p.wait("dve", dok[j], *halo["D"], *fr("acc"))
                t2[j] = p.inc("dve", nc.vector.tensor_scalar(acc[:, j, :], Dt[:, j, 0:CH], pc[:, PC_DW + j:PC_DW + j + 1],
                                                             pc[:, PC_DWB + j:PC_DWB + j + 1], ALU.mult, ALU.add))
            for k in range(1, 31):
                for j in range(2):
                    p.wait("dve", t2[j])
                    t2[j] = p.inc("dve", nc.vector.scalar_tensor_tensor(
                        out=acc[:, j, :], in0=Dt[:, j, k:k + CH], scalar=pc[:, PC_DW + 2 * k + j:PC_DW + 2 * k + j + 1],
                        in1=acc[:, j, :], op0=ALU.mult, op1=ALU.add))
            conv_ok = t2[1]
            p.wait("dve", conv_ok)
            t = p.inc("dve", nc.vector.tensor_copy(Dt[:, :, 0:30], Dt[:, :, CH:CH + 30]))
            halo["D"] = [t]
            free["D"] = [t]

            def cross(m):
                sc = []
                for pr in range(2):
                    s = MS.next()
                    p.wait("pe", *s.free, q_ok, kv_ok)
                    lo = 64 * pr
                    for hh in range(2):
                        t = nc.tensor.matmul(s.ap[:, hh * 256:(hh + 1) * 256], qT[lo:lo + 64, hh, m * 128:(m + 1) * 128],
                                             kT[lo:lo + 64, hh, :], start=True, stop=True)
                    sc.append((s, p.inc("pe", t)))
                free["q"] = [sc[1][1]]
                mx, nb, sm, rc = st[:, 0:4], st[:, 4:8], st[:, 8:12], st[:, 12:16]
                for pr, (s, t) in enumerate(sc):
                    p.wait("dve", t, *fr("nb"))
                    t = p.inc("dve", nc.vector.tensor_reduce(mx[:, pr:4:2],
                                                             s.ap[:, :].rearrange("p (a b) -> p a b", a=2), AX, ALU.max))
                p.wait("dve", t)
                t = p.inc("dve", nc.vector.tensor_scalar(nb, mx, -0.125, None, ALU.mult))
                p.wait("act", t, *fr("pe_"))
                for h in range(4):
                    s = sc[h % 2][0]
                    t = p.inc("act", nc.scalar.activation(pe_[:, h, :], s.ap[:, (h // 2) * 256:(h // 2 + 1) * 256], ACT.Exp,
                                                          bias=nb[:, h:h + 1], scale=0.125, accum_out=sm[:, h:h + 1]))
                    s.free = [t]
                free["nb"] = [t]
                p.wait("dve", t)
                t = p.inc("dve", nc.vector.reciprocal(rc, sm))
                p.wait("dve", t)
                for h in range(4):
                    t = p.inc("dve", nc.vector.tensor_scalar(pe_[:, h, :], pe_[:, h, :], rc[:, h:h + 1], None, ALU.mult))
                yield
                pt = []
                for pr in range(2):
                    s = MS.next()
                    p.wait("pe", t, *s.free)
                    for i in range(4):
                        h, j = 2 * pr + i // 2, i % 2
                        u = nc.tensor.transpose(s.ap[:, i * 128:(i + 1) * 128], pe_[:, h, j * 128:(j + 1) * 128], ident[:])
                    u = p.inc("pe", u)
                    p.wait("act", u, *fr("pT"))
                    v = p.inc("act", nc.scalar.copy(pT[:, 4 * pr:4 * pr + 4, :].rearrange("p a b -> p (a b)"), s.ap[:, :]))
                    s.free = [v]
                    pt.append(v)
                free["pe_"] = [u]
                yield
                s = MS.next()
                p.wait("pe", *pt, *s.free)
                for h in range(4):
                    lo = 64 * (h % 2)
                    for j in range(2):
                        t = nc.tensor.matmul(s.ap[lo:lo + 64, (h // 2) * 128:(h // 2 + 1) * 128],
                                             vm[:, j, h * 64:(h + 1) * 64], pT[:, 2 * h + j, :],
                                             start=(j == 0), stop=(j == 1), skip_group_check=True)
                t = p.inc("pe", t)
                free["pT"] = [t]
                p.wait("act", t, *fr("yT"))
                t = p.inc("act", nc.scalar.copy(yT[:, 8:10, m * 128:(m + 1) * 128],
                                                s.ap[:, 0:256].rearrange("p (a b) -> p a b", a=2)))
                s.free = [t]
                Y[8] = Y[9] = t

            cok = {}

            def e_xc(j, ps, t):
                p.wait("act", t, *fr("C"))
                cok[j] = p.inc("act", nc.scalar.copy(Ct[:, j, 15:], ps[:, :]))
                return cok[j]

            proj(c, 5, e_xc)
            w, x = issued[(c, 4)], xTs[c % 2]
            p.wait("pe", *w.full)
            vb = []
            for pr in range(2):
                s = PR.next()
                p.wait("pe", *s.free)
                for m in range(2):
                    for k in range(8):
                        t = nc.tensor.matmul(s.ap[:, m * 256:(m + 1) * 256],
                                             x.ap[:, k, (2 * pr + m) * 128:(2 * pr + m + 1) * 128], w.ap[:, k, :],
                                             start=(k == 0), stop=(k == 7))
                t = p.inc("pe", t)
                p.wait("act", t, *fr("gvn"))
                u = p.inc("act", nc.scalar.activation(gvn[:, 2 * pr:2 * pr + 2, :].rearrange("p a b -> p (a b)"),
                                                      s.ap[:, :], ACT.Gelu_apprx_tanh))
                s.free = [u]
                vb.append(u)
            w.free = [t]
            issue(nl[0])
            nl[0] += 1
            cross0 = cross(0)
            next(cross0)
            N = 15 + CH
            for j in range(2):
                src, off = Ct[:, j, :], 0
                p.wait("pool", cok[j], *halo["C"], *fr("tmp2"))
                w, b = 1, 0
                res = {}
                steps = 2 if j == 0 else 4
                for i in range(steps):
                    lo = 2 * w - 1
                    t = p.inc("pool", nc.gpsimd.tensor_tensor(tmp2[:, b, lo:N], src[:, lo:N], src[:, lo - w:N - w], ALU.add))
                    p.wait("pool", t)
                    src = tmp2[:, b, :]
                    res[2 * w] = (src, t)
                    w *= 2
                    b = 1 - b
                a, z = (2, 4) if j == 0 else (8, 16)
                p.wait("dve", res[z][1], *fr("tmp"))
                for lo, win in ((0, a), (64, z)):
                    src = res[win][0]
                    if c == 0:
                        t = p.inc("dve", nc.vector.tensor_tensor(tmp[lo:lo + 64, j, 0:16], src[lo:lo + 64, 15:31],
                                                                 prc[lo:lo + 64, j, 0:16], ALU.mult))
                        p.wait("dve", t)
                        t = p.inc("dve", nc.vector.tensor_tensor(tmp[lo:lo + 64, j, 0:16], tmp[lo:lo + 64, j, 0:16],
                                                                 Ct[lo:lo + 64, j, 15:31], ALU.subtract))
                    o = 16 if c == 0 else 0
                    t = p.inc("dve", nc.vector.scalar_tensor_tensor(
                        out=tmp[lo:lo + 64, j, o:CH], in0=src[lo:lo + 64, 15 + o:N], scalar=prc[lo:lo + 64, j, 16:17],
                        in1=Ct[lo:lo + 64, j, 15 + o:N], op0=ALU.mult, op1=ALU.subtract))
                free["tmp2"] = [t]
                s = MS.next()
                p.wait("pe", t, *s.free)
                u = p.inc("pe", nc.tensor.matmul(s.ap[:, :], poolw[:, j, :], tmp[:, j, :], start=True, stop=True))
                p.wait("act", u, *fr("yT"))
                Y[4 + j] = p.inc("act", nc.scalar.activation(yT[:, 4 + j, :], s.ap[:, :], ACT.Copy,
                                                             scale=pc[:, PC_PS + j:PC_PS + j + 1]))
                s.free = [Y[4 + j]]
                free["tmp"] = [u]
            p.wait("pool", t)
            t = p.inc("pool", nc.gpsimd.tensor_copy(Ct[:, :, 0:15], Ct[:, :, CH:CH + 15]))
            halo["C"] = [t]
            free["C"] = [t]

            next(cross0)
            s = MS.next()
            p.wait("pe", conv_ok, *s.free)
            for j in range(2):
                t = nc.tensor.matmul(s.ap[:, :], onm[:], acc[:, j, :], start=(j == 0), stop=(j == 1))
            t = p.inc("pe", t)
            p.wait("dve", t, *fr("D2"))
            for j in range(2):
                t = p.inc("dve", nc.vector.tensor_tensor(acc[:, j, :], acc[:, j, :], s.ap[:, :], ALU.subtract))
            s.free = [t]
            p.wait("act", t, *free["tmp"])
            for j in range(2):
                t = p.inc("act", nc.scalar.activation(tmp[:, j, :], acc[:, j, :], ACT.Square))
            sq_ok = t
            next(cross0, None)
            t = sq_ok
            s = MS.next()
            p.wait("pe", t, *s.free)
            for j in range(2):
                t = nc.tensor.matmul(s.ap[:, :], onm[:], tmp[:, j, :], start=(j == 0), stop=(j == 1))
            t = p.inc("pe", t)
            p.wait("act", t)
            t = p.inc("act", nc.scalar.activation(tmp[:, 0, :], s.ap[:, :], ACT.Sqrt, bias=eps_ln[:], scale=1.0))
            s.free = [t]
            p.wait("dve", t)
            t = p.inc("dve", nc.vector.reciprocal(tmp[:, 1, :], tmp[:, 0, :]))
            p.wait("dve", t)
            for j in range(2):
                t = p.inc("dve", nc.vector.tensor_tensor(acc[:, j, :], acc[:, j, :], tmp[:, 1, :], ALU.mult))
            free["tmp"] = [t]
            p.wait("act", t)
            for j in range(2):
                t = p.inc("act", nc.scalar.activation(acc[:, j, :], acc[:, j, :], ACT.Silu,
                                                      bias=pc[:, PC_CLB + j:PC_CLB + j + 1],
                                                      scale=pc[:, PC_CLG + j:PC_CLG + j + 1]))
            cn_ok = t

            xa_ok = {}

            def e_xa(j, ps, t):
                p.wait("act", t, *free["tmp"])
                xa_ok[j] = p.inc("act", nc.scalar.copy(tmp[:, j, :], ps[:, :]))
                return xa_ok[j]

            proj(c, 0, e_xa, cross(1))
            ca_ok = {}

            def e_ca(j, ps, t):
                p.wait("dve", t, xa_ok[j], *halo["A"], *fr("A"))
                ca_ok[j] = p.inc("dve", nc.vector.tensor_tensor(At[:, j, 2:], ps[:, :], tmp[:, j, :], ALU.mult))
                return ca_ok[j]

            proj(c, 2, e_ca)
            for j in range(2):
                p.wait("dve", ca_ok[j])
                t = p.inc("dve", nc.vector.tensor_scalar(tmp[:, j, :], At[:, j, 0:CH], pc[:, j:j + 1], None, ALU.mult))
                for k in range(1, 3):
                    p.wait("dve", t)
                    t = p.inc("dve", nc.vector.scalar_tensor_tensor(
                        out=tmp[:, j, :], in0=At[:, j, k:k + CH], scalar=pc[:, 2 * k + j:2 * k + j + 1],
                        in1=tmp[:, j, :], op0=ALU.mult, op1=ALU.add))
            p.wait("dve", t)
            ha = p.inc("dve", nc.vector.tensor_copy(At[:, :, 0:2], At[:, :, CH:CH + 2]))
            halo["A"] = [ha]

            def e_ba(j, ps, t):
                p.wait("dve", t, ha, *fr("yT"))
                Y[j] = p.inc("dve", nc.vector.tensor_tensor(yT[:, j, :], ps[:, :], tmp[:, j, :], ALU.mult))
                return Y[j]

            for j in range(2):
                s = MS.next()
                p.wait("pe", cn_ok, *s.free)
                for i in range(2):
                    t = nc.tensor.matmul(s.ap[:, :], pw[:, i, j * 128:(j + 1) * 128], acc[:, i, :],
                                         start=(i == 0), stop=(i == 1))
                t = p.inc("pe", t)
                p.wait("act", t, *fr("yT"))
                Y[6 + j] = p.inc("act", nc.scalar.copy(yT[:, 6 + j, :], s.ap[:, :]))
                s.free = [Y[6 + j]]
            free["acc"] = [t]
            proj(c, 1, e_ba, cross(2))
            free["tmp"] = [Y[1]]

            gu_ok = {}

            def e_u(j, ps, t):
                p.wait("act", t, *free["tmp"])
                gu_ok[j] = p.inc("act", nc.scalar.activation(tmp[:, j, :], ps[:, :], ACT.Gelu_apprx_tanh))
                return gu_ok[j]

            proj(c, 3, e_u, cross(3))
            p.wait("dve", *vb)
            for m in range(4):
                t = p.inc("dve", nc.vector.bn_stats(st[:, 16 + 6 * m:22 + 6 * m], gvn[:, m, :]))
            p.wait("dve", t)
            for m in range(4):
                t = p.inc("dve", nc.vector.bn_aggr(st[:, 40 + 2 * m:42 + 2 * m], st[:, 16 + 6 * m:22 + 6 * m]))
            p.wait("act", t)
            t = p.inc("act", nc.scalar.activation(st[:, 48:52], st[:, 41:48:2], ACT.Sqrt, bias=eps_ln[:], scale=1.0))
            p.wait("dve", t)
            t = p.inc("dve", nc.vector.reciprocal(st[:, 52:56], st[:, 48:52]))
            p.wait("dve", t)
            for m in range(4):
                t = p.inc("dve", nc.vector.tensor_scalar(gvn[:, m, :], gvn[:, m, :], st[:, 40 + 2 * m:41 + 2 * m],
                                                         st[:, 52 + m:53 + m], ALU.subtract, ALU.mult))
                p.wait("pool", t)
                t = p.inc("pool", nc.gpsimd.tensor_tensor(gvn[:, m, :], gvn[:, m, :], lngb[:, 0, :], ALU.mult))
                p.wait("pool", t)
                vn_ok = p.inc("pool", nc.gpsimd.tensor_tensor(gvn[:, m, :], gvn[:, m, :], lngb[:, 1, :], ALU.add))

            def gate(g, ys):
                def e_g(j, ps, t):
                    y = ys[j]
                    p.wait("act", t, *fr("tmp2"))
                    u = p.inc("act", nc.scalar.activation(tmp2[:, j, 0:CH], ps[:, :], ACT.Silu))
                    p.wait("dve", u, Y[y])
                    Y[y] = p.inc("dve", nc.vector.tensor_tensor(yT[:, y, :], yT[:, y, :], tmp2[:, j, 0:CH], ALU.mult))
                    free["tmp2"] = [Y[y]]
                    return u
                proj(c, g, e_g)

            gate(9, [0, 1])
            for m in range(4):
                s = MS.next()
                p.wait("pe", vn_ok, wsg_ok, *s.free)
                for h in range(4):
                    lo = 64 * (h % 2)
                    t = nc.tensor.matmul(s.ap[lo:lo + 64, (h // 2) * 128:(h // 2 + 1) * 128],
                                         gvn[:, m, h * 64:(h + 1) * 64], wsg[:, h, :], start=True, stop=True,
                                         skip_group_check=True)
                t = p.inc("pe", t)
                p.wait("dve", t, *fr("yT"))
                u = p.inc("dve", nc.vector.tensor_tensor(yT[:, 2:4, m * 128:(m + 1) * 128],
                                                         s.ap[:, 0:256].rearrange("p (a b) -> p a b", a=2),
                                                         sgb[:], ALU.add))
                s.free = [u]
            free["gvn"] = [t]
            p.wait("dve", gu_ok[0], gu_ok[1], u)
            for j in range(2):
                Y[2 + j] = p.inc("dve", nc.vector.tensor_tensor(yT[:, 2 + j, :], yT[:, 2 + j, :], tmp[:, j, :], ALU.mult))
            free["tmp"] = [Y[3]]
            if c < 3:
                x = xTs[(c + 1) % 2]
                p.wait("sp", *x.free)
                x.full = [p.dma("sp", x, x.ap, A["xT"][:, :, (c + 1) * CH:(c + 2) * CH])]
            for g in range(10, 14):
                gate(g, [2 * (g - 9), 2 * (g - 9) + 1])

            if c == 0:
                p.wait("dve", ln_ok)
                p.wait("pool", ln_ok)
                xs, hs = xrs.next(), h0s.next()
                p.wait("sp", *xs.free)
                xs.full = [p.dma("sp", xs, xs.ap[0:NM, :], A["meta"])]
                t = layer_norm(p, xs.ap, 1024, NM, st[:, 16:28], st[:, 56:58], st[:, 58:59], st[:, 59:60], eps_ln,
                               hs.ap, LN[:, 2, :], LN[:, 3, :], xs.full, hs.free, "pool")
                p.wait("sp", t)
                hs.free = [p.dma("sp", hs, h0d[S:L, :], hs.ap[0:NM, :])]
            for m in range(4):
                xs = xrs.next()
                tok = (4 * c + m) * 128
                p.wait("sp", *xs.free)
                xs.full = [p.dma("sp", xs, xs.ap, A["x"][tok:tok + 128, :])]
                hs = h0s.next()
                for n in range(2):
                    s = MS.next()
                    p.wait("pe", *s.free, *[Y[i] for i in range(10)], *wos.full)
                    for k in range(10):
                        t = nc.tensor.matmul(s.ap[:, :], yT[:, k, m * 128:(m + 1) * 128], wo[:, k, n * 512:(n + 1) * 512],
                                             start=(k == 0), stop=(k == 9))
                    t = p.inc("pe", t)
                    p.wait("dve", t, *xs.full)
                    u = p.inc("dve", nc.vector.scalar_tensor_tensor(
                        out=xs.ap[:, n * 512:(n + 1) * 512], in0=xs.ap[:, n * 512:(n + 1) * 512], scalar=ALPHA,
                        in1=s.ap[:, :], op0=ALU.mult, op1=ALU.add))
                    s.free = [u]
                free["yT"] = [t]
                t = layer_norm(p, xs.ap, 1024, 128, st[:, 16:28], st[:, 56:58], st[:, 58:59], st[:, 59:60], eps_ln,
                               xs.ap, LN[:, 0, :], LN[:, 1, :], [u], [], "dve")
                t = layer_norm(p, xs.ap, 1024, 128, st[:, 28:40], st[:, 60:62], st[:, 62:63], st[:, 63:64], eps_ln,
                               hs.ap, LN[:, 2, :], LN[:, 3, :], [t], hs.free, "dve")
                xs.free = [t]
                p.wait("sp", t)
                hs.free = [p.dma("sp", hs, h0d[tok:tok + 128, :], hs.ap)]
        p.close()


NT = 17


F32R = mybir.dt.float32r


def phase_project(p, A, h0d, qTd, kTd, vd, ident, eps_rms):
    nc = p.nc
    with ExitStack() as ctx:
        def sb(name, shape, dt=F32):
            return ctx.enter_context(nc.sbuf_tensor("p_" + name, shape, dt))

        banks = [ctx.enter_context(nc.psum_tensor(f"p_ps{i}", [128, 512], F32)) for i in range(8)]
        Z = Ring([Slot(b) for b in banks[0:5]])
        B = Ring([Slot(b) for b in banks[5:8]])
        w2r = sb("w2r", [128, 4, 1472])
        w2h = sb("w2h", [128, 8, 1472], F32R)
        w2l = sb("w2l", [128, 8, 1472], F32R)
        wqb = sb("wqb", [128, 2, 768])
        wkvb = sb("wkvb", [128, 1024])
        pc = sb("pc", [128, 3])
        gg = sb("gg", [128, 2, 128])
        ht = sb("ht", [128, 2, 1024])
        hTh = sb("hTh", [128, 8, 128], F32R)
        hTl = sb("hTl", [128, 8, 128], F32R)
        rp2 = sb("rp", [128, 2, 384])
        an = sb("an", [128, 384])
        aT = sb("aT", [128, 3, 128])
        ra = sb("ra", [128, 1024])
        rb = sb("rb", [128, 1024])
        qt = sb("qt", [128, 2, 10, 128], F32R)
        kt = sb("kt", [128, 2, 7, 128], F32R)
        vt = sb("vt", [128, 6, 128])
        sq = sb("sq", [128, 256])
        st = sb("st", [128, 32])

        cslot = Slot(None, p.slot_sem("p_const"))
        for dst, src in ((pc[:], A["pc"][:, PC_GQA:PC_N]), (gg[:, 0, :], bcast(A["g_q_gqa_2"], 128)),
                         (gg[:, 1, :], bcast(A["g_k_gqa_2"], 128)), (wqb[:], A["wqb"]), (wkvb[:], A["wkvb"])):
            cok = p.dma("pool", cslot, dst, src)
        w2s = Ring([Slot(w2r[:, i], p.slot_sem(f"p_w2{i}")) for i in range(4)])
        hts = Ring([Slot(ht[:, i], p.slot_sem(f"p_ht{i}")) for i in range(2)])
        kts = Slot(kt[:], p.slot_sem("p_kt"))
        vts = Slot(vt[:], p.slot_sem("p_vt"))
        rpr = Ring([Slot(rp2[:, i], p.slot_sem(f"p_rp{i}")) for i in range(2)])
        qts = Slot(qt[:], p.slot_sem("p_qt"))

        def load(i):
            n = 128 if i < 16 else NM
            s = hts.next()
            p.wait("sp", *s.free)
            s.full = [p.dma("sp", s, s.ap[0:n, :], h0d[i * 128:i * 128 + n, :])]
            return s

        cur = load(0)
        w2_ok = []
        for k in range(8):
            s = w2s.next()
            p.wait("sp", *s.free)
            t = p.dma("sp", s, s.ap, A["w2"][:, k, :])
            p.wait("act", t)
            u = p.inc("act", nc.scalar.copy(w2h[:, k, :], s.ap))
            p.wait("dve", u)
            u = p.inc("dve", nc.vector.tensor_tensor(w2l[:, k, :], s.ap, w2h[:, k, :].bitcast(F32), ALU.subtract))
            s.free = [u]
            w2_ok.append(u)
        for e in ("pe", "dve", "act", "pool"):
            p.wait(e, cok)
        free = {}

        def fr(n):
            return free.get(n, [])

        def evac(e, dst, src, *toks):
            p.wait(e, *toks)
            if e == "act":
                return p.inc("act", nc.scalar.copy(dst, src))
            return p.inc("dve", nc.vector.tensor_copy(dst, src))

        def split(hi, lo, src, *toks):
            p.wait("act", *toks)
            u = p.inc("act", nc.scalar.copy(hi, src))
            p.wait("dve", u)
            return p.inc("dve", nc.vector.tensor_tensor(lo, src, hi.bitcast(F32), ALU.subtract))

        turned, zbanks = {}, {}

        def turn(i, cur):
            n = 128 if i < 16 else NM
            tt = []
            for hf in range(2):
                s = B.next()
                p.wait("pe", *cur.full, *s.free)
                for k in range(4):
                    t = nc.tensor.transpose(s.ap[:, k * 128:k * 128 + n],
                                            cur.ap[0:n, (4 * hf + k) * 128:(4 * hf + k + 1) * 128], ident[0:n, 0:n])
                t = p.inc("pe", t)
                ks = slice(4 * hf, 4 * hf + 4)
                s.free = [split(hTh[:, ks, 0:n], hTl[:, ks, 0:n], s.ap[:, :].rearrange("p (a b) -> p a b", a=4)[:, :, 0:n],
                                t, *fr("hT"))]
                tt += s.free
            cur.free = [t]
            turned[i] = tt

        def project(i, m):
            if i >= NT:
                return
            n = 128 if i < 16 else NM
            lo, w = ((0, 448), (448, 512), (960, 512))[m]
            s = Z.next()
            p.wait("pe", *turned[i], *s.free)
            for k in range(8):
                p.wait("pe", w2_ok[k])
                for a, (x, y) in enumerate(((hTh, w2h), (hTh, w2l), (hTl, w2h))):
                    t = nc.tensor.matmul(s.ap[0:n, 0:w], x[:, k, 0:n], y[:, k, lo:lo + w],
                                         start=(k == 0 and a == 0), stop=(k == 7 and a == 2))
            t = p.inc("pe", t)
            zbanks.setdefault(i, []).append((s, t))
            if m == 2:
                free["hT"] = [t]

        turn(0, cur)
        cur = load(1)
        for m in range(3):
            project(0, m)
        for i in range(NT):
            n = 128 if i < 16 else NM
            rps = rpr.next()
            rp = rps.ap
            p.wait("sp", *rps.free)
            rps.full = [p.dma("sp", rps, rp, A["rope"][i])]
            if i + 1 < NT:
                turn(i + 1, cur)
                if i + 2 < NT:
                    cur = load(i + 2)
            zs = zbanks[i]
            (z0, t0), (z1, t1), (z2, t2) = zs
            p.wait("act", t0, *fr("st"))
            parts = [(z0, 0, 256), (z0, 256, 128)] + [(z1, 128 * h, 128) for h in range(4)] + [(z2, 128 * h, 128) for h in range(2)]
            for m, (z, lo, w) in enumerate(parts):
                if m == 2:
                    p.wait("act", t1)
                if m == 6:
                    p.wait("act", t2)
                if m:
                    p.wait("act", u)
                u = p.inc("act", nc.scalar.activation(sq[0:n, 0:w], z.ap[0:n, lo:lo + w], ACT.Square, accum_out=st[0:n, m:m + 1]))
            p.wait("act", *vts.free)
            u = p.inc("act", nc.scalar.copy(vt[0:n, 4:6, :].rearrange("p a b -> p (a b)"), z2.ap[0:n, 256:512]))
            p.wait("act", u)
            p.inc("act", nc.scalar.activation(st[0:n, 8:9], st[0:n, 0:1], ACT.Sqrt, bias=eps_rms[0:n, :], scale=1.0 / 256))
            u = p.inc("act", nc.scalar.activation(st[0:n, 9:16], st[0:n, 1:8], ACT.Sqrt, bias=eps_rms[0:n, :], scale=1.0 / 128))
            p.wait("dve", u)
            r = p.inc("dve", nc.vector.reciprocal(st[0:n, 16:24], st[0:n, 8:16]))
            p.wait("act", r, *fr("an"))
            p.inc("act", nc.scalar.activation(an[0:n, 0:256], z0.ap[0:n, 0:256], ACT.Copy, scale=st[0:n, 16:17]))
            ua = p.inc("act", nc.scalar.activation(an[0:n, 256:384], z0.ap[0:n, 256:384], ACT.Copy, scale=st[0:n, 17:18]))
            p.wait("dve", *rps.full)

            def rot(dst, tmp, src, heads, w, c0, s0, e, toks):
                p.wait(e, *toks)
                eng = p.eng[e]
                h_ = w // 64
                cb = rp[0:n, c0:c0 + w].unsqueeze(1).to_broadcast([n, heads, w])
                t = p.inc(e, eng.tensor_tensor(dst, src, cb, ALU.mult))
                s4 = src.rearrange("p h (f two c) -> p h f two c", f=h_, two=2)
                t4 = tmp.rearrange("p h (f two c) -> p h f two c", f=h_, two=2)
                sv = rp[0:n, s0:s0 + w].rearrange("p (f two c) -> p f two c", f=h_, two=2)
                for a in range(2):
                    for f in range(h_):
                        sb_ = sv[:, f, a, :].unsqueeze(1).to_broadcast([n, heads, 32])
                        t = p.inc(e, eng.tensor_tensor(t4[:, :, f, a, :], s4[:, :, f, 1 - a, :], sb_, ALU.mult))
                p.wait(e, t)
                return p.inc(e, eng.tensor_tensor(dst, dst, tmp, ALU.add))

            kr3 = ra[0:n, 0:64].rearrange("p (h w) -> p h w", h=1)
            t = rot(kr3, rb[0:n, 0:64].rearrange("p (h w) -> p h w", h=1),
                    z0.ap[0:n, 384:448].rearrange("p (h w) -> p h w", h=1), 1, 64, 0, 64, "dve", [ua, *fr("ra")])
            p.wait("dve", t)
            krt = p.inc("dve", nc.vector.tensor_copy(ra[0:n, 64:128], ra[0:n, 0:64]))
            z0.free = [krt, ua]
            rq = st[0:n, 18:22].unsqueeze(2).to_broadcast([n, 4, 128])
            rk = st[0:n, 22:24].unsqueeze(2).to_broadcast([n, 2, 128])
            xg = ra[0:n, 256:1024].rearrange("p (h w) -> p h w", h=6)
            p.wait("dve", *fr("xg"))
            a1 = p.inc("dve", nc.vector.tensor_tensor(xg[:, 0:4, :], z1.ap[0:n, :].rearrange("p (h w) -> p h w", h=4), rq, ALU.mult))
            a2 = p.inc("dve", nc.vector.tensor_tensor(xg[:, 4:6, :], z2.ap[0:n, 0:256].rearrange("p (h w) -> p h w", h=2), rk, ALU.mult))
            z1.free = [a1]
            z2.free = [a2]
            free["st"] = [a2]
            p.wait("pool", a2)
            p.inc("pool", nc.gpsimd.tensor_tensor(xg[:, 0:4, :], xg[:, 0:4, :], gg[0:n, 0:1, :].to_broadcast([n, 4, 128]), ALU.mult))
            a2 = p.inc("pool", nc.gpsimd.tensor_tensor(xg[:, 4:6, :], xg[:, 4:6, :], gg[0:n, 1:2, :].to_broadcast([n, 2, 128]), ALU.mult))
            yg = rb[0:n, 256:1024].rearrange("p (h w) -> p h w", h=6)
            yq = rot2(p, yg, xg, rp, n, [a2, *rps.full], fr("yg"))
            free["xg"] = [yq]
            project(i + 1, 0)
            s = B.next()
            p.wait("pe", ua, *s.free)
            for k in range(3):
                t = nc.tensor.transpose(s.ap[:, k * 128:k * 128 + n], an[0:n, k * 128:(k + 1) * 128], ident[0:n, 0:n])
            t = p.inc("pe", t)
            free["an"] = [t]
            p.wait("act", t, *fr("aT"))
            for k in range(3):
                a_ok = p.inc("act", nc.scalar.activation(aT[:, k, 0:n], s.ap[:, k * 128:k * 128 + n], ACT.Copy, scale=pc[:, k:k + 1]))
            s.free = [a_ok]
            project(i + 1, 1)
            s = B.next()
            p.wait("pe", a_ok, *s.free)
            for h in range(4):
                t = nc.tensor.matmul(s.ap[:, h * 128:h * 128 + n], wkvb[:, h * 256:h * 256 + 128], aT[:, 2, 0:n], start=True, stop=True)
            t = p.inc("pe", t)
            s.free = [split(kt[:, 0, 0:4, 0:n], kt[:, 1, 0:4, 0:n],
                            s.ap[:, :].rearrange("p (a b) -> p a b", a=4)[:, :, 0:n], t, *kts.free)]
            s = B.next()
            p.wait("pe", *s.free)
            for h in range(4):
                t = nc.tensor.matmul(s.ap[0:n, h * 128:(h + 1) * 128], aT[:, 2, 0:n], wkvb[:, h * 256 + 128:(h + 1) * 256], start=True, stop=True)
            t = p.inc("pe", t)
            s.free = [evac("act", vt[0:n, 0:4, :].rearrange("p a b -> p (a b)"), s.ap[0:n, :], t)]
            p.wait("sp", *s.free)
            vts.free = [p.dma("sp", vts, vd[:, 0:n, i, :].rearrange("h p d -> p h d"), vt[0:n])]
            if i < 16:
                s = B.next()
                p.wait("pe", *s.free)
                for h in range(4):
                    for k in range(2):
                        t = nc.tensor.matmul(s.ap[:, h * 128:(h + 1) * 128], wqb[:, k, h * 192:h * 192 + 128], aT[:, k, :],
                                             start=(k == 0), stop=(k == 1))
                t = p.inc("pe", t)
                s.free = [split(qt[:, 0, 0:4, :].rearrange("p a b -> p (a b)"), qt[:, 1, 0:4, :].rearrange("p a b -> p (a b)"),
                                s.ap[:, :], t, *qts.free)]
                s = B.next()
                p.wait("pe", *s.free)
                for k in range(2):
                    t = nc.tensor.matmul(s.ap[:, 0:256], aT[:, k, :],
                                         wqb[:, k, :].rearrange("p (h w) -> p h w", h=4)[:, :, 128:192],
                                         start=(k == 0), stop=(k == 1))
                t = p.inc("pe", t)
                qr = an[:, 0:256].rearrange("p (h w) -> p h w", h=4)
                qu = rot(qr, rb[:, 0:256].rearrange("p (h w) -> p h w", h=4),
                         s.ap[:, 0:256].rearrange("p (h w) -> p h w", h=4), 4, 64, 0, 64, "dve", [t, krt, *free["an"]])
                s.free = [qu]
            free["aT"] = [t]
            project(i + 1, 2)
            s = B.next()
            p.wait("pe", krt, *s.free)
            t = nc.tensor.transpose(s.ap[:, 0:n], ra[0:n, 0:128], ident[0:n, 0:n])
            if i < 16:
                p.wait("pe", qu)
                for k in range(2):
                    t = nc.tensor.transpose(s.ap[:, 128 + k * 128:256 + k * 128], an[:, k * 128:(k + 1) * 128], ident[:])
            t = p.inc("pe", t)
            free["ra"] = [t]
            free["an"] = [t]
            s.free = [split(kt[:, 0, 4, 0:n], kt[:, 1, 4, 0:n], s.ap[:, 0:n], t)]
            if i < 16:
                s.free = [split(qt[:, 0, 4:6, :].rearrange("p a b -> p (a b)"), qt[:, 1, 4:6, :].rearrange("p a b -> p (a b)"),
                                s.ap[:, 128:384], t, *s.free)]
            s = B.next()
            p.wait("pe", yq, *s.free)
            for k in range(2):
                t = nc.tensor.transpose(s.ap[:, k * 128:k * 128 + n], rb[0:n, 768 + k * 128:896 + k * 128], ident[0:n, 0:n])
            t = p.inc("pe", t)
            s.free = [split(kt[:, 0, 5:7, 0:n], kt[:, 1, 5:7, 0:n],
                            s.ap[:, 0:256].rearrange("p (a b) -> p a b", a=2)[:, :, 0:n], t)]
            p.wait("sp", *s.free)
            kts.free = [p.dma("sp", kts, kTd[z, :, :, i * 128:i * 128 + n].rearrange("h p n -> p h n"),
                              kt[:, z, :, 0:n].bitcast(F32)) for z in range(2)]
            if i < 16:
                s = B.next()
                p.wait("pe", *s.free)
                for k in range(4):
                    t = nc.tensor.transpose(s.ap[:, k * 128:(k + 1) * 128], rb[:, 256 + k * 128:384 + k * 128], ident[:])
                t = p.inc("pe", t)
                s.free = [split(qt[:, 0, 6:10, :].rearrange("p a b -> p (a b)"), qt[:, 1, 6:10, :].rearrange("p a b -> p (a b)"),
                                s.ap[:, :], t)]
                p.wait("sp", *s.free)
                qts.free = [p.dma("sp", qts, qTd[z, :, :, i * 128:(i + 1) * 128].rearrange("h p n -> p h n"),
                                  qt[:, z].bitcast(F32)) for z in range(2)]
            free["yg"] = [t]
            rps.free = [yq, krt] + ([qu] if i < 16 else [])
        p.close()


def rot2(p, out, x, rp, n, toks, out_free):
    eng = p.nc.gpsimd
    p.wait("pool", *toks, *out_free)
    x5 = x.rearrange("p h (f two c) -> p h f two c", f=2, two=2)
    o5 = out.rearrange("p h (f two c) -> p h f two c", f=2, two=2)
    sv = rp[0:n, 256:384].rearrange("p (f two c) -> p f two c", f=2, two=2)
    for a in range(2):
        for f in range(2):
            t = p.inc("pool", eng.tensor_tensor(o5[:, :, f, a, :], x5[:, :, f, 1 - a, :],
                                                sv[:, f, a, :].unsqueeze(1).to_broadcast([n, 6, 32]), ALU.mult))
    p.wait("pool", t)
    t = p.inc("pool", eng.tensor_tensor(x, x, rp[0:n, 128:256].unsqueeze(1).to_broadcast([n, 6, 128]), ALU.mult))
    p.wait("pool", t)
    return p.inc("pool", eng.tensor_tensor(out, out, x, ALU.add))


SCW = [(416 * c, 416 if c < 4 else 400) for c in range(5)]


def phase_attend(p, qTd, kTd, vd, od, yd, ident):
    nc = p.nc
    with ExitStack() as ctx:
        def sb(name, shape, dt=F32):
            return ctx.enter_context(nc.sbuf_tensor("a_" + name, shape, dt))

        banks = [ctx.enter_context(nc.psum_tensor(f"a_ps{i}", [128, 512], F32)) for i in range(8)]
        SB = [Slot(b) for b in banks[0:5]]
        TB = Ring([Slot(banks[5]), Slot(banks[6])])
        OB = Slot(banks[7])
        K = sb("K", [128, 2, 2, L], F32R)
        Ks = Ring([Slot(K[:, i], p.slot_sem(f"a_K{i}")) for i in range(2)])
        KR = sb("KR", [128, 2, L], F32R)
        KRs = Slot(KR[:], p.slot_sem("a_KR"))
        V = sb("V", [128, 2, NT, 128])
        Vs = Ring([Slot(V[:, i], p.slot_sem(f"a_V{i}")) for i in range(2)])
        Q = sb("Q", [128, 2, 2, S], F32R)
        Qs = Ring([Slot(Q[:, i], p.slot_sem(f"a_Q{i}")) for i in range(2)])
        QR = sb("QR", [128, 2, 2, S], F32R)
        QRs = Ring([Slot(QR[:, i], p.slot_sem(f"a_QR{i}")) for i in range(2)])
        P = sb("P", [128, 2, L])
        Ps = [Slot(P[:, i]) for i in range(2)]
        PT = sb("PT", [128, 2, NT * 128])
        PTs = [Slot(PT[:, i]) for i in range(2)]
        o = sb("o", [128, 1, 16, 128])
        os_ = Ring([Slot(o[:, i], p.slot_sem(f"a_o{i}")) for i in range(1)])
        sc = sb("sc", [128, 2, 32])
        scs = [Slot(sc[:, i]) for i in range(2)]

        def fetch(slot, dst, src):
            slot.full = [p.dma("sp", slot, dst, src)]

        def parts(d, h):
            return d[:, h].rearrange("z p n -> p z n")

        heads = {}

        first = {n: Slot(None, p.slot_sem("a_first_" + n)) for n in ("q", "qr")}
        CUT = 256

        def load(h):
            prev = heads.get(h - 1)
            if h < 4:
                qr = prev["qr"] if h % 2 else QRs.next()
                if h % 2 == 0:
                    p.wait("sp", *qr.free)
                    fetch(qr, qr.ap.bitcast(F32), parts(qTd, 4 + h // 2))
            else:
                qr = None
            if h in (5, 7):
                k, v = prev["k"], prev["v"]
            else:
                kh = h if h < 4 else 5 + (h - 4) // 2
                vh = h if h < 4 else 4 + (h - 4) // 2
                k, v = Ks.next(), Vs.next()
                p.wait("sp", *k.free)
                fetch(k, k.ap.bitcast(F32), parts(kTd, kh))
                p.wait("sp", *v.free)
                p.dma("sp", v, v.ap[0:NM, 16, :], vd[vh, 0:NM, 16, :])
                fetch(v, v.ap[:, 0:16, :], vd[vh, :, 0:16, :])
            q = Qs.next()
            p.wait("sp", *q.free)
            fetch(q, q.ap.bitcast(F32), parts(qTd, h if h < 4 else 2 + h))
            heads[h] = {"qr": qr, "k": k, "v": v, "q": q, "o": os_.next()}

        qr, k, v, q = QRs.next(), Ks.next(), Vs.next(), Qs.next()
        H0 = []
        for n, slot, h in (("q", q, 0), ("qr", qr, 4)):
            H0.append(p.dma("sp", first[n], slot.ap[:, :, 0:CUT].bitcast(F32), parts(qTd, h)[:, :, 0:CUT]))
        fetch(k, k.ap.bitcast(F32), parts(kTd, 0))
        fetch(KRs, KR[:].bitcast(F32), parts(kTd, 4))
        p.dma("sp", v, v.ap[0:NM, 16, :], vd[0, 0:NM, 16, :])
        fetch(v, v.ap[:, 0:16, :], vd[0, :, 0:16, :])
        for slot, h in ((q, 0), (qr, 4)):
            fetch(slot, slot.ap[:, :, CUT:].bitcast(F32), parts(qTd, h)[:, :, CUT:])
        heads[0] = {"qr": qr, "k": k, "v": v, "q": q, "o": os_.next()}
        load(1)
        zt = sb("zt", [128, 1024])
        zs = Slot(None, p.slot_sem("a_zt"))
        zok = p.inc("pool", nc.gpsimd.memset(zt[:], 0.0))
        p.wait("sp", zok)
        for b in range(64, YB):
            p.dma("sp", zs, yd[b * 128:(b + 1) * 128, :], zt[:])
        steps = [(h, i) for h in range(8) for i in range(16)]

        def scores(m, c):
            h, i = steps[m]
            H = heads[h]
            b = SB[c]
            lo, w = SCW[c]
            qs = slice(i * 128, (i + 1) * 128)
            early = h == 0 and i < CUT // 128
            p.wait("pe", *(H0 if early else H["q"].full), *H["k"].full, *b.free)
            todo = [(H["q"].ap[:, x, qs], H["k"].ap[:, y, lo:lo + w]) for x, y in ((0, 0), (0, 1), (1, 0))]
            if h < 4:
                r = 64 * (h % 2)
                p.wait("pe", *([] if early else H["qr"].full), *KRs.full)
                todo += [(H["qr"].ap[r:r + 64, x, qs], KR[r:r + 64, y, lo:lo + w]) for x, y in ((0, 0), (0, 1), (1, 0))]
            for n, (x, y) in enumerate(todo):
                t = nc.tensor.matmul(b.ap[:, 0:w], x, y, start=(n == 0), stop=(n == len(todo) - 1))
            t = p.inc("pe", t)
            if i == 15:
                for n in ("q", "k", "qr"):
                    if H[n]:
                        H[n].free = [t]
            return t

        def maximum(m, c, t):
            z = scs[m % 2]
            p.wait("dve", t, *z.free)
            return p.inc("dve", nc.vector.tensor_reduce(z.ap[:, c:c + 1], SB[c].ap[:, 0:SCW[c][1]], AX, ALU.max))

        def weights(m, t):
            h, i = steps[m]
            scale = SQK_M if h < 4 else SQK_G
            z, P_ = scs[m % 2], Ps[m % 2]
            p.wait("dve", t)
            t = p.inc("dve", nc.vector.tensor_reduce(z.ap[:, 5:6], z.ap[:, 0:5], AX, ALU.max))
            p.wait("dve", t)
            t = p.inc("dve", nc.vector.tensor_scalar(z.ap[:, 6:7], z.ap[:, 5:6], -scale, None, ALU.mult))
            p.wait("act", t, *P_.free)
            P_.full = []
            for c in range(5):
                lo, w = SCW[c]
                u = p.inc("act", nc.scalar.activation(P_.ap[:, lo:lo + w], SB[c].ap[:, 0:w], ACT.Exp, bias=z.ap[:, 6:7],
                                                      scale=scale, accum_out=z.ap[:, 8 + c:9 + c]))
                SB[c].free = [u]
                P_.full.append(u)
            z.full = [u]

        def turn(m, c):
            P_, T = Ps[m % 2], PTs[m % 2]
            s = TB.next()
            k = 4 if c < 4 else 1
            n = 128 if c < 4 else NM
            p.wait("pe", P_.full[min(4, (c * 512 + 511) // 416)], *s.free)
            for a in range(k):
                t = nc.tensor.transpose(s.ap[0:n, a * 128:(a + 1) * 128], P_.ap[:, c * 512 + a * 128:c * 512 + a * 128 + n], ident[:])
            t = p.inc("pe", t)
            e = ("act", "dve", "act", "dve", "dve")[c]
            p.wait(e, t, *T.free)
            dst, src = T.ap[0:n, c * 512:c * 512 + k * 128], s.ap[0:n, 0:k * 128]
            u = p.inc(e, nc.scalar.copy(dst, src) if e == "act" else nc.vector.tensor_copy(dst, src))
            s.free = [u]
            T.full.append(u)
            if c == 4:
                P_.free = [t]

        def values(m):
            h, i = steps[m]
            H = heads[h]
            T, z, O = PTs[m % 2], scs[m % 2], H["o"]
            p.wait("pe", *OB.free, *H["v"].full)
            for j in range(NT):
                n = 128 if j < 16 else NM
                p.wait("pe", T.full[j // 4])
                t = nc.tensor.matmul(OB.ap[:, 0:128], T.ap[0:n, j * 128:(j + 1) * 128], H["v"].ap[0:n, j, :],
                                     start=(j == 0), stop=(j == NT - 1))
            t = p.inc("pe", t)
            T.free = [t]
            if i == 15:
                H["v"].free = [t]
            p.wait("dve", *z.full)
            u = p.inc("dve", nc.vector.tensor_reduce(z.ap[:, 14:15], z.ap[:, 8:13], AX, ALU.add))
            p.wait("dve", u)
            u = p.inc("dve", nc.vector.reciprocal(z.ap[:, 15:16], z.ap[:, 14:15]))
            p.wait("dve", u, t, *(O.free if i == 0 else []))
            u = p.inc("dve", nc.vector.tensor_scalar(O.ap[:, i, :], OB.ap[:, 0:128], z.ap[:, 15:16], None, ALU.mult))
            OB.free = [u]
            z.free = [u]
            if i % 8 == 7:
                g = slice(i - 7, i + 1)
                p.wait("sp", u)
                t = p.dma("sp", O, od[(i - 7) * 128:(i + 1) * 128, h * 128:(h + 1) * 128].rearrange("(i p) d -> p i d", p=128),
                          O.ap[:, g, :])
                O.free = [t]
                if i == 15 and h + 2 < 8:
                    load(h + 2)

        for m in range(len(steps)):
            for c in range(5):
                t = scores(m, c)
                if m:
                    if c == 0:
                        PTs[(m - 1) % 2].full = []
                    turn(m - 1, c)
                t = maximum(m, c, t)
            weights(m, t)
            if m:
                values(m - 1)
        m = len(steps) - 1
        PTs[m % 2].full = []
        for c in range(5):
            turn(m, c)
        values(m)
        p.close()


class Route:
    pass


def alloc_route(nc):
    r = Route()
    r.slot = nc.alloc_sbuf_tensor("r_slot", [128, 16, 4], U32)
    r.pos = nc.alloc_sbuf_tensor("r_pos", [128, 16, 4], F32)
    r.idf = nc.alloc_sbuf_tensor("r_idf", [128, 16, 4], F32)
    r.base = nc.alloc_sbuf_tensor("r_base", [128, 32], F32)
    r.gate = nc.alloc_sbuf_tensor("r_gate", [128, 16, 4], F32)
    r.ngr = nc.alloc_sbuf_tensor("r_ngr", [1, 1], I32)
    r.raw = nc.alloc_sbuf_tensor("r_raw", [128, 2, 8, 512], F32)
    r.raw_full = [nc.alloc_semaphore(f"r_raw_full{i}") for i in range(2)]
    r.tab = nc.alloc_sbuf_tensor("r_tab", [4, GT], I32)
    return r


def phase_route(p, A, h0d, od, h1d, tabd, R, ident, eps_ln, eps_rms):
    nc = p.nc
    with ExitStack() as ctx:
        def sb(name, shape, dt=F32):
            return ctx.enter_context(nc.sbuf_tensor("o_" + name, shape, dt))

        banks = [ctx.enter_context(nc.psum_tensor(f"o_ps{i}", [128, 512], F32)) for i in range(8)]
        B = Ring([Slot(b) for b in banks])
        wor = sb("wor", [128, 2, 1024])
        woh = sb("woh", [128, 8, 1024], F32R)
        wol = sb("wol", [128, 8, 1024], F32R)
        wr = sb("wr", [128, 8, 32])
        go = sb("go", [128, 1024])
        LN = sb("LN", [128, 2, 1024])
        br = sb("br", [128, 32])
        erow = sb("erow", [128, 32])
        before = sb("before", [128, 128])
        ones = sb("ones", [128, 128])
        tokid = sb("tokid", [128, 16], I32)
        thr = sb("thr", [128, 15])
        zt = sb("zt", [128, NE * CAP // 128], I32)
        ob = sb("ob", [128, 3, 1024])
        hb = sb("hb", [128, 3, 1024])
        h1 = sb("h1", [128, 3, 1024])
        oTh = sb("oTh", [128, 2, 8, 128], F32R)
        oTl = sb("oTl", [128, 2, 8, 128], F32R)
        hT = sb("hT", [128, 2, 8, 128])
        sq = sb("sq", [128, 512])
        st = sb("st", [128, 2, 8])
        sl_ = sb("sl", [128, 16])
        lg = sb("lg", [128, 2, 32])
        m8 = sb("m8", [128, 8])
        i8 = sb("i8", [128, 8], U32)
        ex2 = sb("ex", [128, 2, 8])
        oh2 = sb("oh", [128, 2, 4, 32])
        pr = sb("pr", [128, 4, 32])
        M2 = sb("M", [128, 2, 32])
        Macc = sb("Macc", [128, 32])
        C = sb("C", [128, 32])
        sf = sb("sf", [128, 4])
        cnt = sb("cnt", [128, 9, 32])
        gt = sb("gt", [128, 12])
        qcol = sb("qcol", [128, 1])
        tb = sb("tb", [128, 32, 15])

        cslot = Slot(None, p.slot_sem("o_const"))
        for dst, src in ((go[:], bcast(A["g_o"], 1024)), (LN[:, 0, :], bcast(A["ln1_g_2"], 1024)),
                         (LN[:, 1, :], bcast(A["ln1_b_2"], 1024)), (br[:], bcast(A["b_router_2"], 32)),
                         (erow[:], A["erow"]), (qcol[:], A["qcol"]), (before[:], A["before"]),
                         (tokid[:], A["tokid"]), (thr[:], A["thr"]), (wr[:], A["wr"])):
            cok = p.dma("pool", cslot, dst, src)
        z = p.inc("dve", nc.vector.memset(zt[:], 0))
        p.inc("dve", nc.vector.memset(ones[:], 1.0))
        m0 = p.inc("dve", nc.vector.memset(Macc[:], 0.0))
        zs = Slot(None, p.slot_sem("o_zt"))
        p.wait("sp", z)
        tab_ok = p.dma("sp", zs, tabd.rearrange("(p n) o -> p (n o)", p=128), zt[:])
        obs = Ring([Slot(ob[:, i], p.slot_sem(f"o_ob{i}")) for i in range(3)])
        hbs = Ring([Slot(hb[:, i], p.slot_sem(f"o_hb{i}")) for i in range(3)])
        h1s = Ring([Slot(h1[:, i], p.slot_sem(f"o_h1{i}")) for i in range(3)])
        wors = Ring([Slot(wor[:, i], p.slot_sem(f"o_wo{i}")) for i in range(2)] + h1s.slots)
        oTs = [Slot((oTh[:, i], oTl[:, i])) for i in range(2)]
        hTs = [Slot(hT[:, i]) for i in range(2)]
        scs = Slot(None, p.slot_sem("o_scatter"))
        tiles = {}

        def load(i):
            a, b = obs.next(), hbs.next()
            p.wait("sp", *a.free)
            a.full = [p.dma("sp", a, a.ap, od[i * 128:(i + 1) * 128, :])]
            p.wait("sp", *b.free)
            b.full = [p.dma("sp", b, b.ap, h0d[i * 128:(i + 1) * 128, :])]
            tiles[i] = {"a": a, "b": b}

        load(0)
        wo_ok = []
        for k in range(8):
            s = wors.next()
            p.wait("sp", *s.free)
            t = p.dma("sp", s, s.ap, A["wo2"][:, k, :])
            p.wait("act", t)
            u = p.inc("act", nc.scalar.copy(woh[:, k, :], s.ap))
            p.wait("dve", u)
            u = p.inc("dve", nc.vector.tensor_tensor(wol[:, k, :], s.ap, woh[:, k, :].bitcast(F32), ALU.subtract))
            s.free = [u]
            wo_ok.append(u)
        load(1)
        for e in ("pe", "dve", "act", "pool"):
            p.wait(e, cok, m0)
        free = {}

        def fr(n):
            return free.get(n, [])

        def v(ins):
            tok = p.inc("dve", ins)
            p.wait("dve", tok)
            return tok

        def norms(i):
            a, z = tiles[i]["a"], st[:, i % 2]
            p.wait("act", *a.full, *fr(("st", i % 2)))
            for hf in range(2):
                if hf:
                    p.wait("act", u)
                u = p.inc("act", nc.scalar.activation(sq[:], a.ap[:, hf * 512:(hf + 1) * 512], ACT.Square, accum_out=z[:, hf:hf + 1]))
            p.wait("act", u)
            u = p.inc("act", nc.scalar.activation(z[:, 2:4], z[:, 0:2], ACT.Sqrt, bias=eps_rms[:], scale=1.0 / 512))
            p.wait("dve", u)
            v(nc.vector.reciprocal(z[:, 4:6], z[:, 2:4]))
            for hf in range(2):
                w = a.ap[:, hf * 512:(hf + 1) * 512]
                u = p.inc("dve", nc.vector.scalar_tensor_tensor(out=w, in0=w, scalar=z[:, 4 + hf:5 + hf],
                                                                in1=go[:, hf * 512:(hf + 1) * 512], op0=ALU.mult, op1=ALU.mult))
            free[("st", i % 2)] = [u]
            a.full = [u]

        def turn(src, ready, dst):
            dst.full = []
            for hf in range(2):
                s = B.next()
                p.wait("pe", *ready, *s.free)
                for k in range(4):
                    t = nc.tensor.transpose(s.ap[:, k * 128:(k + 1) * 128], src[:, (4 * hf + k) * 128:(4 * hf + k + 1) * 128], ident[:])
                t = p.inc("pe", t)
                p.wait("act", t, *dst.free)
                parts = dst.ap if isinstance(dst.ap, tuple) else (dst.ap,)
                hi, *lo = (x[:, 4 * hf:4 * hf + 4, :].rearrange("p a b -> p (a b)") for x in parts)
                u = p.inc("act", nc.scalar.copy(hi, s.ap[:, :]))
                if lo:
                    p.wait("dve", u)
                    u = p.inc("dve", nc.vector.tensor_tensor(lo[0], s.ap[:, :], hi.bitcast(F32), ALU.subtract))
                s.free = [u]
                dst.full.append(u)
            return t

        def turn_o(i):
            a = tiles[i]["a"]
            a.free = [turn(a.ap, a.full, oTs[i % 2])]

        def project(i, n):
            T, b = oTs[i % 2], tiles[i]["b"]
            s = B.next()
            p.wait("pe", *T.full, *s.free)
            for k in range(8):
                p.wait("pe", wo_ok[k])
                for m, (x, y) in enumerate(((0, woh), (0, wol), (1, woh))):
                    t = nc.tensor.matmul(s.ap[:, :], T.ap[x][:, k, :], y[:, k, n * 512:(n + 1) * 512],
                                         start=(k == 0 and m == 0), stop=(k == 7 and m == 2))
            t = p.inc("pe", t)
            T.free = [t]
            p.wait("dve", t, *b.full)
            u = p.inc("dve", nc.vector.scalar_tensor_tensor(
                out=b.ap[:, n * 512:(n + 1) * 512], in0=b.ap[:, n * 512:(n + 1) * 512], scalar=ALPHA,
                in1=s.ap[:, :], op0=ALU.mult, op1=ALU.add))
            s.free = [u]
            tiles[i]["sum"] = u

        def norm(i):
            b, h = tiles[i]["b"], h1s.next()
            t = layer_norm(p, b.ap, 1024, 128, sl_[:, 0:12], sl_[:, 12:14], sl_[:, 14:15], sl_[:, 15:16], eps_ln,
                           h.ap, LN[:, 0, :], LN[:, 1, :], [tiles[i]["sum"]], h.free, "pool")
            b.free = [t]
            p.wait("sp", t)
            h.free = [p.dma("sp", h, h1d[i * 128:(i + 1) * 128, :], h.ap)]
            tiles[i]["h"], tiles[i]["ok"] = h, t

        def router(i):
            h, T = tiles[i]["h"], hTs[i % 2]
            h.free = h.free + [turn(h.ap, [tiles[i]["ok"]], T)]
            s = B.next()
            p.wait("pe", *T.full, *s.free)
            for k in range(8):
                t = nc.tensor.matmul(s.ap[:, 0:32], T.ap[:, k, :], wr[:, k, :], start=(k == 0), stop=(k == 7))
            t = p.inc("pe", t)
            T.free = [t]
            tiles[i]["lg"] = (s, t)

        def choose(i):
            s, t = tiles[i]["lg"]
            ex, oh, M, l = ex2[:, i % 2], oh2[:, i % 2], M2[:, i % 2], lg[:, i % 2, :]
            p.wait("dve", t)
            s.free = [v(nc.vector.tensor_tensor(l, s.ap[:, 0:32], br[:], ALU.add))]
            v(nc.vector.max(m8[:], l))
            v(nc.vector.max_index(i8[:], m8[:], l))
            v(nc.vector.tensor_copy(R.idf[:, i, :], i8[:, 0:4]))
            v(nc.vector.tensor_copy(ex[:, 0:4], m8[:, 0:4]))
            t = v(nc.vector.tensor_scalar(ex[:, 4:5], m8[:, 0:1], -1.0, None, ALU.mult))
            p.wait("act", t)
            g = p.inc("act", nc.scalar.activation(ex[:, 0:4], ex[:, 0:4], ACT.Exp, bias=ex[:, 4:5], scale=1.0, accum_out=ex[:, 5:6]))
            v(nc.vector.tensor_tensor(oh, erow[:].unsqueeze(1).to_broadcast([128, 4, 32]),
                                      R.idf[:, i, :].unsqueeze(2).to_broadcast([128, 4, 32]), ALU.is_equal))
            p.wait("dve", *fr(("M", i % 2)))
            m = v(nc.vector.tensor_reduce(M, oh.rearrange("p k e -> p e k"), AX, ALU.add))
            p.wait("dve", g)
            v(nc.vector.reciprocal(ex[:, 6:7], ex[:, 5:6]))
            v(nc.vector.tensor_scalar(R.gate[:, i, :], ex[:, 0:4], ex[:, 6:7], None, ALU.mult))
            tiles[i]["M"] = m

        carry = {"Macc": [m0]}

        def count(i):
            s = B.next()
            p.wait("pe", tiles[i]["M"], *s.free, *carry["Macc"])
            nc.tensor.matmul(s.ap[:, 0:32], before[:], M2[:, i % 2], start=True, stop=False)
            t = p.inc("pe", nc.tensor.matmul(s.ap[:, 0:32], ones[:], Macc[:], start=False, stop=True))
            free[("M", i % 2)] = [t]
            tiles[i]["C"] = (s, t)

        def place(i):
            s, t = tiles[i]["C"]
            p.wait("dve", t)
            s.free = [v(nc.vector.tensor_copy(C[:], s.ap[:, 0:32]))]
            carry["Macc"] = [v(nc.vector.tensor_tensor(Macc[:], Macc[:], M2[:, i % 2], ALU.add))]
            v(nc.vector.tensor_tensor(pr[:], oh2[:, i % 2], C[:].unsqueeze(1).to_broadcast([128, 4, 32]), ALU.mult))
            v(nc.vector.tensor_reduce(R.pos[:, i, :], pr[:], AX, ALU.add))
            v(nc.vector.scalar_tensor_tensor(out=sf[:], in0=R.idf[:, i, :], scalar=float(CAP), in1=R.pos[:, i, :],
                                             op0=ALU.mult, op1=ALU.add))
            sl = v(nc.vector.tensor_copy(R.slot[:, i, :], sf[:]))
            p.wait("pool", sl, tab_ok)
            for k in range(4):
                nc.gpsimd.indirect_dma_start(
                    out=tabd, out_offset=bass.IndirectOffsetOnAxis(ap=R.slot[:, i, k:k + 1], axis=0),
                    in_=tokid[:, i:i + 1], in_offset=None).then_inc(scs.sem, 16)
                scs.n += 16
                p.dmas.append((scs.sem, scs.n))

        norms(0)
        norms(1)
        turn_o(0)
        for i in range(18):
            if i + 2 < 16:
                load(i + 2)
            if i == 4:
                for c in range(2):
                    nc.sync.dma_start(R.raw[:, c].rearrange("p k n -> p (k n)"), A["wgu"][0, c]).then_inc(R.raw_full[c], 16)
            if i < 16:
                project(i, 0)
            if i + 1 < 16:
                turn_o(i + 1)
            if i < 16:
                project(i, 1)
            if 2 <= i:
                count(i - 2)
            if 1 <= i < 17:
                router(i - 1)
            if i < 16:
                norm(i)
            if i + 2 < 16:
                norms(i + 2)
            if 2 <= i:
                place(i - 2)
            if 1 <= i < 17:
                choose(i - 1)
        s = B.next()
        p.wait("pe", *carry["Macc"], *s.free)
        t = p.inc("pe", nc.tensor.matmul(s.ap[:, 0:32], ones[:], Macc[:], start=True, stop=True))
        p.wait("dve", t)
        v(nc.vector.tensor_copy(cnt[:, 0, :], s.ap[:, 0:32]))
        v(nc.vector.tensor_tensor(tb[:], cnt[:, 0, :].unsqueeze(2).to_broadcast([128, 32, 15]),
                                  thr[:].unsqueeze(1).to_broadcast([128, 32, 15]), ALU.is_gt))
        v(nc.vector.tensor_reduce(cnt[:, 1, :], tb[:], AX, ALU.add))
        v(nc.vector.tensor_scalar(cnt[:, 1, :], cnt[:, 1, :], 1.0, None, ALU.add))
        nb, inc, exc, grp, ginc, gexc = (cnt[:, j, :] for j in range(1, 7))
        v(nc.vector.tensor_tensor_scan(inc, ones[:, 0:32], nb, 0.0, ALU.mult, ALU.add))
        v(nc.vector.tensor_tensor(exc, inc, nb, ALU.subtract))
        v(nc.vector.tensor_scalar(R.base[:], exc, 128.0, None, ALU.mult))
        v(nc.vector.tensor_reduce(grp, tb[:, :, 3:12:4], AX, ALU.add))
        v(nc.vector.tensor_scalar(grp, grp, 1.0, None, ALU.add))
        v(nc.vector.tensor_tensor_scan(ginc, ones[:, 0:32], grp, 0.0, ALU.mult, ALU.add))
        v(nc.vector.tensor_tensor(gexc, ginc, grp, ALU.subtract))
        v(nc.vector.tensor_copy(R.ngr[:], cnt[0:1, 5, 31:32]))
        oh8, sel = cnt[:, 7, :], cnt[:, 8, :]
        v(nc.vector.tensor_scalar(oh8, gexc, qcol[:, 0:1], None, ALU.is_le))
        v(nc.vector.tensor_scalar(sel, ginc, qcol[:, 0:1], None, ALU.is_le))
        v(nc.vector.tensor_tensor(oh8, oh8, sel, ALU.subtract))
        for j, src in enumerate((erow[:], nb, gexc, exc)):
            v(nc.vector.tensor_tensor(sel, oh8, src, ALU.mult))
            v(nc.vector.tensor_reduce(gt[:, j:j + 1], sel, AX, ALU.add))
        e_, n_, gx, bx, s_ = (gt[:, j:j + 1] for j in range(5))
        o_ = gt[:, 8:12]
        v(nc.vector.tensor_tensor(s_, qcol[:], gx, ALU.subtract))
        v(nc.vector.tensor_copy(o_[:, 0:1], e_))
        v(nc.vector.scalar_tensor_tensor(out=o_[:, 1:2], in0=s_, scalar=-4.0, in1=n_, op0=ALU.mult, op1=ALU.add))
        v(nc.vector.tensor_scalar(o_[:, 1:2], o_[:, 1:2], 4.0, 0.0, ALU.min, ALU.max))
        v(nc.vector.tensor_scalar(gt[:, 5:6], s_, 512.0, None, ALU.mult))
        v(nc.vector.scalar_tensor_tensor(out=o_[:, 2:3], in0=e_, scalar=float(CAP), in1=gt[:, 5:6], op0=ALU.mult, op1=ALU.add))
        v(nc.vector.scalar_tensor_tensor(out=o_[:, 3:4], in0=s_, scalar=4.0, in1=bx, op0=ALU.mult, op1=ALU.add))
        s = B.next()
        p.wait("pe", (p.sem["dve"], p.cnt["dve"]), *s.free)
        t = p.inc("pe", nc.tensor.transpose(s.ap[0:4, 0:128], o_, ident[:]))
        p.wait("dve", t)
        v(nc.vector.tensor_copy(R.tab[:], s.ap[0:4, 0:GT]))
        p.close()


def phase_combine(p, A, h1d, yd, R, out, eps_ln):
    nc = p.nc
    with ExitStack() as ctx:
        def sb(name, shape, dt=F32):
            return ctx.enter_context(nc.sbuf_tensor("c_" + name, shape, dt))

        LN = sb("LN", [128, 2, 1024])
        y = sb("y", [128, 12, 1024])
        h = sb("h", [128, 4, 1024])
        o = sb("o", [128, 3, 1024])
        st = sb("st", [128, 2, 32])
        cslot = Slot(None, p.slot_sem("c_const"))
        p.dma("act", cslot, LN[:, 0, :], bcast(A["ln2_g_2"], 1024))
        cok = p.dma("act", cslot, LN[:, 1, :], bcast(A["ln2_b_2"], 1024))
        for e in ("dve", "pool"):
            p.wait(e, cok)
        ys = Ring([Slot(y[:, i], p.slot_sem(f"c_y{i}")) for i in range(12)])
        hs = Ring([Slot(h[:, i], p.slot_sem(f"c_h{i}")) for i in range(4)])
        os_ = Ring([Slot(o[:, i], p.slot_sem(f"c_o{i}")) for i in range(3)])
        erow = sb("erow", [128, 32])
        eq = sb("eq", [128, 64, 32])
        eok = p.dma("act", cslot, erow[:], A["erow"])
        p.wait("dve", eok)

        def v(ins):
            tok = p.inc("dve", ins)
            p.wait("dve", tok)
            return tok

        v(nc.vector.tensor_tensor(eq[:], erow[:].unsqueeze(1).to_broadcast([128, 64, 32]),
                                  R.idf[:].rearrange("p a b -> p (a b)").unsqueeze(2).to_broadcast([128, 64, 32]), ALU.is_equal))
        v(nc.vector.tensor_tensor(eq[:], eq[:], R.base[:].unsqueeze(1).to_broadcast([128, 64, 32]), ALU.mult))
        sf = sb("sf", [128, 64])
        v(nc.vector.tensor_reduce(sf[:], eq[:], AX, ALU.add))
        v(nc.vector.tensor_tensor(sf[:], sf[:], R.pos[:].rearrange("p a b -> p (a b)"), ALU.add))
        sl = v(nc.vector.tensor_copy(R.slot[:].rearrange("p a b -> p (a b)"), sf[:]))
        p.wait("pool", sl)
        loaded = {}

        def load(i):
            a = hs.next()
            p.wait("sp", *a.free)
            a.full = [p.dma("sp", a, a.ap, h1d[i * 128:(i + 1) * 128, :])]
            g = []
            for k in range(4):
                s = ys.next()
                p.wait("pool", *s.free)
                nc.gpsimd.indirect_dma_start(out=s.ap, out_offset=None, in_=yd[0:YB * 128, :],
                                             in_offset=bass.IndirectOffsetOnAxis(ap=R.slot[:, i, k:k + 1], axis=0)).then_inc(s.sem, 16)
                s.n += 16
                s.full = [(s.sem, s.n)]
                p.dmas.append((s.sem, s.n))
                g.append(s)
            loaded[i] = (a, g)

        def gather(i):
            a, g = loaded[i]
            p.wait("act", *a.full)
            t = p.inc("act", nc.scalar.activation(a.ap, a.ap, ACT.Copy, scale=ALPHA))
            for k, s in enumerate(g):
                p.wait("dve", t, *s.full)
                t = p.inc("dve", nc.vector.scalar_tensor_tensor(out=a.ap, in0=s.ap, scalar=R.gate[:, i, k:k + 1], in1=a.ap,
                                                                op0=ALU.mult, op1=ALU.add))
                s.free = [t]
            z = st[:, i % 2, :]
            p.wait("dve", t)
            for k in range(2):
                t = p.inc("dve", nc.vector.bn_stats(z[:, 6 * k:6 * k + 6], a.ap[:, k * 512:(k + 1) * 512]))
            p.wait("dve", t)
            t = p.inc("dve", nc.vector.bn_aggr(z[:, 12:14], z[:, 0:12]))
            p.wait("act", t)
            t = p.inc("act", nc.scalar.activation(z[:, 14:15], z[:, 13:14], ACT.Sqrt, bias=eps_ln[:], scale=1.0))
            return a, z, t

        def finish(i, a, z, t):
            p.wait("dve", t)
            t = p.inc("dve", nc.vector.reciprocal(z[:, 15:16], z[:, 14:15]))
            q = os_.next()
            p.wait("dve", t, *q.free)
            t = p.inc("dve", nc.vector.tensor_scalar(q.ap, a.ap, z[:, 12:13], z[:, 15:16], ALU.subtract, ALU.mult))
            a.free = [t]
            p.wait("pool", t)
            t = p.inc("pool", nc.gpsimd.tensor_tensor(q.ap, q.ap, LN[:, 0, :], ALU.mult))
            return q, t

        def store(i, q, t):
            p.wait("dve", t)
            t = p.inc("dve", nc.vector.tensor_tensor(q.ap, q.ap, LN[:, 1, :], ALU.add))
            p.wait("sp", t)
            q.free = [p.dma("sp", q, out[i * 128:(i + 1) * 128, :], q.ap)]

        load(0)
        load(1)
        load(2)
        at, done = {}, {}
        for i in range(18):
            if i < 16:
                at[i] = gather(i)
            if 1 <= i < 17:
                done[i - 1] = finish(i - 1, *at[i - 1])
            if i >= 2:
                store(i - 2, *done[i - 2])
            if i + 3 < 16:
                load(i + 3)
        p.close(last_phase=True)


F32R = mybir.dt.float32r


def phase_experts(p, A, h1d, tabd, yd, R, ident):
    nc = p.nc
    with ExitStack() as ctx:
        def sb(name, shape, dt=F32):
            return ctx.enter_context(nc.sbuf_tensor("e_" + name, shape, dt))

        def sem(name):
            return nc.alloc_semaphore("e_" + name)

        def sems(name, n):
            return [sem(f"{name}{i}") for i in range(n)]

        banks = [ctx.enter_context(nc.psum_tensor(f"e_ps{i}", [128, 512], F32)) for i in range(8)]
        G, TX, TA = banks[0:4], banks[4:6], banks[6:8]
        raw = R.raw
        wh = sb("wh", [128, 2, 8, 512], F32R)
        wl = sb("wl", [128, 2, 8, 512], F32R)
        bg = sb("bg", [128, 2048])
        bd = sb("bd", [128, 1024])
        idx = sb("idx", [128, 4], I32)
        hx = sb("hx", [128, 2, 1024])
        hTh = sb("hTh", [128, 4, 8, 128], F32R)
        hTl = sb("hTl", [128, 4, 8, 128], F32R)
        aTh = sb("aTh", [128, 4, 8, 128], F32R)
        aTl = sb("aTl", [128, 4, 8, 128], F32R)
        tt = sb("tt", [128, 512])
        gg = sb("gg", [128, 256])
        uu = sb("uu", [128, 256])
        sg = sb("sg", [128, 256])
        act = sb("act", [128, 4, 256])
        Y = sb("Y", [128, 4, 512])
        junk = sb("junk", [1, 8])

        raw_full, raw_free = R.raw_full, sems("raw_free", 2)
        hi_full = sem("hi_full")
        w_full, w_free = sem("w_full"), sem("w_free")
        bg_full, bg_free = sem("bg_full"), sem("bg_free")
        bd_full, bd_free = sem("bd_full"), sem("bd_free")
        idx_full, idx_seen = sem("idx_full"), sem("idx_seen")
        rows_in = sem("rows_in")
        hx_full, hx_free = sems("hx_full", 2), sems("hx_free", 2)
        x_full, x_hi, x_free = sems("x_full", 2), sems("x_hi", 2), sems("x_free", 2)
        hT_full = sems("hT_full", 4)
        a_full, a_hi, a_free = sems("a_full", 2), sems("a_hi", 2), sems("a_free", 2)
        aT_full = sems("aT_full", 4)
        g_full, g_free = sems("g_full", 4), sems("g_free", 4)
        glu, sig = sem("glu"), sem("sig")
        act_full = sems("act_full", 4)
        out_full, out_free = sems("out_full", 4), sems("out_free", 4)
        dv = sem("dv")

        def take(eng, s, n=1):
            eng.wait_ge(s, n)
            eng.sem_inc(s, -n)

        sp, pe, dve, act_e, pool = nc.sync, nc.tensor, nc.vector, nc.scalar, nc.gpsimd
        for s in g_free + a_free + x_free + [bg_free, bd_free]:
            dve.sem_inc(s, 1)
        for s in hx_free:
            pe.sem_inc(s, 1)
        pe.sem_inc(w_free, 1)
        for s in out_free:
            act_e.sem_inc(s, 16)

        def bank(c, b):
            return (b + 2 * c) % 4

        def tab(eng, row, q, lo, hi):
            return eng.value_load(R.tab[row:row + 1, bass.ds(q, 1)], min_val=lo, max_val=hi)

        def groups(eng):
            return eng.Fori(0, eng.value_load(R.ngr[0:1, 0:1], min_val=1, max_val=GT - 1))

        def below(eng, b, r):
            return eng.If(r > b)

        def load_raw(c, src):
            take(sp, raw_free[c % 2])
            sp.dma_start(raw[:, c % 2].rearrange("p k n -> p (k n)"), src).then_inc(raw_full[c % 2], 16)

        with groups(sp) as q:
            e = tab(sp, 0, q, 0, NE - 1)
            en = tab(sp, 0, q + 1, 0, NE - 1)
            for c in range(6):
                if c == 0:
                    take(sp, bg_free)
                    sp.dma_start(bg[:], A["bgu"][bass.ds(e, 1), :].broadcast_to([128, 2048])).then_inc(bg_full, 16)
                if c == 2:
                    take(sp, bd_free)
                    sp.dma_start(bd[:], A["bdn"][bass.ds(e, 1), :].broadcast_to([128, 1024])).then_inc(bd_full, 16)
                d = (c + 2) % 6
                src = A["wgu"][bass.ds(e if c < 2 else en, 1), d] if d < 4 else A["wdn"][bass.ds(e, 1), d - 4]
                load_raw(d, src.rearrange("o p n -> p (o n)"))
        take(sp, raw_full[1], 16)

        with groups(pool) as q:
            r = tab(pool, 1, q, 1, 4)
            row = tab(pool, 2, q, 0, NE * CAP - 512)
            blk = tab(pool, 3, q, 0, YB)
            pool.dma_start(idx[:], tabd[bass.ds(row, 512), :].rearrange("(j p) o -> p (j o)", p=128),
                           allow_slow_non_contiguous=True).then_inc(idx_full, 16)
            pool.wait_ge(idx_full, q * 16 + 16)
            pool.sem_inc(idx_seen, 1)
            for b in range(4):
                with below(pool, b, r):
                    take(pool, hx_free[b % 2])
                    pool.indirect_dma_start(out=hx[:, b % 2, :], out_offset=None, in_=h1d,
                                            in_offset=bass.IndirectOffsetOnAxis(ap=idx[:, b:b + 1], axis=0)).then_inc(rows_in, 16)
                    pool.wait_ge(rows_in, blk * 16 + (16 * b + 16))
                    pool.sem_inc(hx_full[b % 2], 1)

        def pe_rows(b):
            take(pe, hx_full[b % 2])
            for hf in range(2):
                take(pe, x_free[hf])
                for k in range(4):
                    t = pe.transpose(TX[hf][:, k * 128:(k + 1) * 128],
                                     hx[:, b % 2, (4 * hf + k) * 128:(4 * hf + k + 1) * 128], ident[:])
                t.then_inc(x_full[hf], 1)

        def pe_product(c, b, between):
            ph, pl = (hTh, hTl) if c < 4 else (aTh, aTl)
            g = bank(c, b)
            take(pe, g_free[g])
            if c == 4:
                take(pe, aT_full[b])
            n = 0
            for k in range(8):
                if b == 0 and k % 2 == 0:
                    take(pe, w_full)
                between(k)
                if k == 6 and c == 4:
                    take(pe, aT_full[b])
                for x, y in ((ph, wh), (ph, wl), (pl, wh)):
                    t = pe.matmul(G[g][:, :], x[:, b, k, :], y[:, c % 2, k, :], start=(n == 0), stop=(n == 23))
                    if n == 0 and b == 0:
                        t.then_inc(w_free, 1)
                    n += 1
            t.then_inc(g_full[g], 1)

        def pe_acts(c, b):
            take(pe, act_full[b])
            take(pe, a_free[b % 2])
            for k in range(2):
                t = pe.transpose(TA[b % 2][:, k * 128:(k + 1) * 128], act[:, b, k * 128:(k + 1) * 128], ident[:])
            t.then_inc(a_full[b % 2], 1)

        def act_hi(c, between=None):
            n = (c + 1) % 6
            take(act_e, raw_full[n % 2], 16)
            take(act_e, w_free)
            for i in range(4):
                if between:
                    between(2 * i)
                act_e.copy(wh[:, n % 2, 2 * i:2 * i + 2, :].rearrange("p k n -> p (k n)"),
                           raw[:, n % 2, 2 * i:2 * i + 2, :].rearrange("p k n -> p (k n)")).then_inc(hi_full, 1)

        def act_rows(b):
            for hf in range(2):
                take(act_e, x_full[hf])
                act_e.copy(hTh[:, b, 4 * hf:4 * hf + 4, :].rearrange("p a b -> p (a b)"), TX[hf][:, :]).then_inc(x_hi[hf], 1)

        def act_acts(c, b):
            take(act_e, a_full[b % 2])
            act_e.copy(aTh[:, b, 2 * c:2 * c + 2, :].rearrange("p a b -> p (a b)"), TA[b % 2][:, 0:256]).then_inc(a_hi[b % 2], 1)

        def act_sig(b):
            take(act_e, glu)
            act_e.activation(sg[:], gg[:], ACT.Sigmoid, scale=1.702).then_inc(sig, 1)

        def act_store(c, b, blk):
            take(act_e, out_full[b])
            act_e.dma_start(yd[bass.ds((blk + b) * 128, 128), (c - 4) * 512:(c - 3) * 512], Y[:, b, :]).then_inc(out_free[b], 16)

        def link(ins):
            ins.then_inc(dv, 1)
            take(dve, dv)

        def tell(s, cell):
            link(dve.memset(junk[0:1, cell:cell + 1], 0.0))
            dve.sem_inc(s, 1)

        def f(ap):
            return ap.bitcast(F32)

        def dve_lo(c, between=None):
            n = (c + 1) % 6
            for i in range(4):
                if between:
                    between(2 * i)
                take(dve, hi_full)
                dve.tensor_tensor(wl[:, n % 2, 2 * i:2 * i + 2, :].rearrange("p k n -> p (k n)"),
                                  raw[:, n % 2, 2 * i:2 * i + 2, :].rearrange("p k n -> p (k n)"),
                                  f(wh[:, n % 2, 2 * i:2 * i + 2, :].rearrange("p k n -> p (k n)")), ALU.subtract).then_inc(w_full, 1)
            tell(raw_free[n % 2], n % 2)

        def dve_rows(b):
            for hf in range(2):
                take(dve, x_hi[hf])
                dve.tensor_tensor(hTl[:, b, 4 * hf:4 * hf + 4, :].rearrange("p a b -> p (a b)"), TX[hf][:, :],
                                  f(hTh[:, b, 4 * hf:4 * hf + 4, :].rearrange("p a b -> p (a b)")), ALU.subtract).then_inc(x_free[hf], 1)
            link(dve.memset(junk[0:1, 2:3], 0.0))
            dve.sem_inc(hT_full[b], 1)
            dve.sem_inc(hx_free[b % 2], 1)

        def dve_acts(c, b):
            take(dve, a_hi[b % 2])
            dve.tensor_tensor(aTl[:, b, 2 * c:2 * c + 2, :].rearrange("p a b -> p (a b)"), TA[b % 2][:, 0:256],
                              f(aTh[:, b, 2 * c:2 * c + 2, :].rearrange("p a b -> p (a b)")), ALU.subtract).then_inc(a_free[b % 2], 1)
            if c >= 2:
                link(dve.memset(junk[0:1, 2:3], 0.0))
                dve.sem_inc(aT_full[b], 1)

        def dve_item(c, b):
            g = bank(c, b)
            take(dve, g_full[g])
            dve.tensor_tensor(tt[:], G[g][:, :], bg[:, c * 512:(c + 1) * 512], ALU.add).then_inc(g_free[g], 1)
            link(dve.memset(junk[0:1, 3:4], 0.0))
            dve.tensor_scalar(gg[:], tt[:, 0:256], 7.0, None, ALU.min).then_inc(glu, 1)
            link(dve.tensor_scalar(uu[:], tt[:, 256:512], 7.0, -7.0, ALU.min, ALU.max))
            link(dve.scalar_tensor_tensor(out=uu[:], in0=uu[:], scalar=1.0, in1=gg[:], op0=ALU.add, op1=ALU.mult))
            take(dve, sig)
            dve.tensor_tensor(act[:, b, :], uu[:], sg[:], ALU.mult).then_inc(act_full[b], 1)

        def dve_out(c, b):
            g = bank(c, b)
            take(dve, g_full[g])
            take(dve, out_free[b], 16)
            dve.tensor_tensor(Y[:, b, :], G[g][:, :], bd[:, (c - 4) * 512:(c - 3) * 512], ALU.add).then_inc(out_full[b], 1)
            tell(g_free[g], 4)

        def between(eng, c, b, r, rn, acts, rows, k):
            if k == (2 if b else 4) and 1 <= c <= 4:
                acts(c - 1, b)
            if k == 6 and c == 4:
                with below(eng, b, rn):
                    rows(b)
            if k == 6 and c == 5 and b == 0:
                for j in range(1, 4):
                    with eng.If(r <= j):
                        with below(eng, j, rn):
                            rows(j)

        r0 = tab(pe, 1, 0, 1, 4)
        for b in range(4):
            with below(pe, b, r0):
                pe_rows(b)
        with groups(pe) as q:
            r = tab(pe, 1, q, 1, 4)
            rn = tab(pe, 1, q + 1, 0, 4)
            for c in range(6):
                for b in range(4):
                    with below(pe, b, r):
                        if c == 0:
                            take(pe, hT_full[b])
                        pe_product(c, b, lambda k: between(pe, c, b, r, rn, pe_acts, pe_rows, k))

        ra = tab(act_e, 1, 0, 1, 4)
        act_hi(-1)
        for b in range(4):
            with below(act_e, b, ra):
                act_rows(b)
        with groups(act_e) as q:
            r = tab(act_e, 1, q, 1, 4)
            rn = tab(act_e, 1, q + 1, 0, 4)
            blk = tab(act_e, 3, q, 0, YB)
            for c in range(6):
                if c == 5:
                    for b in range(4):
                        with below(act_e, b, r):
                            act_store(4, b, blk)
                act_hi(c, lambda k: between(act_e, c, 0, r, rn, act_acts, act_rows, k))
                for b in range(4):
                    with below(act_e, b, r):
                        if b > 0:
                            for k in (2, 6):
                                between(act_e, c, b, r, rn, act_acts, act_rows, k)
                        if c < 4:
                            act_sig(b)
                        if c == 5:
                            act_store(5, b, blk)

        rd = tab(dve, 1, 0, 1, 4)
        dve_lo(-1)
        for b in range(4):
            with below(dve, b, rd):
                dve_rows(b)
        with groups(dve) as q:
            r = tab(dve, 1, q, 1, 4)
            rn = tab(dve, 1, q + 1, 0, 4)
            for c in range(6):
                if c == 0:
                    take(dve, bg_full, 16)
                if c == 4:
                    take(dve, bd_full, 16)
                dve_lo(c, lambda k: between(dve, c, 0, r, rn, dve_acts, dve_rows, k))
                for b in range(4):
                    with below(dve, b, r):
                        if b > 0:
                            for k in (2, 6):
                                between(dve, c, b, r, rn, dve_acts, dve_rows, k)
                        if c < 4:
                            dve_item(c, b)
                        else:
                            dve_out(c, b)
                if c == 3:
                    tell(bg_free, 5)
                if c == 5:
                    tell(bd_free, 6)
        for s in out_free:
            dve.wait_ge(s, 16)
        p.inc("dve", dve.memset(junk[0:1, 7:8], 0.0))
        p.close()


def build(nc, A, out, stop=9, dbg=None):
    p = Prog(nc)
    ident = nc.alloc_sbuf_tensor("ident", [128, 128], F32)
    eps_ln = nc.alloc_sbuf_tensor("eps_ln", [128, 1], F32)
    eps_rms = nc.alloc_sbuf_tensor("eps_rms", [128, 1], F32)
    h0d = nc.dram_tensor("h0d", (L, D), F32).ap()
    isl = Slot(None, p.slot_sem("ident_in"))
    t = p.dma("sp", isl, ident[:], A["ident"])
    a = p.inc("dve", nc.vector.memset(eps_ln[:], LN_EPS))
    b = p.inc("dve", nc.vector.memset(eps_rms[:], RMS_EPS))
    for e in ("pe", "dve", "act", "pool"):
        p.wait(e, t, a, b)
    phase_mixer(p, A, h0d, ident, eps_ln)
    if stop == 1:
        return h0d
    yd = nc.dram_tensor("yd", ((YB + 16) * 128, D), F32).ap()
    qTd = nc.dram_tensor("qTd", (2, 10, 128, S), F32).ap()
    kTd = nc.dram_tensor("kTd", (2, 7, 128, L), F32).ap()
    vd = nc.dram_tensor("vd", (6, 128, NT, 128), F32).ap()
    od = nc.dram_tensor("od", (S, D), F32).ap()
    phase_project(p, A, h0d, qTd, kTd, vd, ident, eps_rms)
    phase_attend(p, qTd, kTd, vd, od, yd, ident)
    if stop == 2:
        return
    h1d = nc.dram_tensor("h1d", (S, D), F32).ap()
    tabd = nc.dram_tensor("tabd", (NE * CAP, 1), I32).ap()
    R = alloc_route(nc)
    phase_route(p, A, h0d, od, h1d, tabd, R, ident, eps_ln, eps_rms)
    if stop == 3:
        return
    phase_experts(p, A, h1d, tabd, yd, R, ident)
    if stop == 4:
        return
    phase_combine(p, A, h1d, yd, R, out, eps_ln)


def host_arrays(x, mem, w_in, conv_a_w, sg_ln_g, sg_ln_b, sg_w, sg_b, pool_w, pool_scale, cc_dw_w, cc_dw_b,
                cc_ln_g, cc_ln_b, cc_pw_w, w_kv, w_out, ln_g, ln_b, meta_tokens_2, ln_emb_g_2, ln_emb_b_2,
                w_in_2, g_q_a_2, w_q_b_2, g_kv_a_2, w_kv_b_2, g_q_gqa_2, g_k_gqa_2, g_o_mla_2, g_o_gqa_2,
                w_o_2, ln1_g_2, ln1_b_2, w_router_2, b_router_2, w_gate_up_2, b_gate_up_2, w_down_2,
                b_down_2, ln2_g_2, ln2_b_2):
    def kp(w):
        k = w.shape[0] // 128
        return np.ascontiguousarray(w.reshape(k, 128, -1).transpose(1, 0, 2))

    def cols(v):
        return v.reshape(-1, 128).T

    A = {}
    A["x"] = x[0]
    A["xT"] = kp(x[0].T)
    A["memT"] = kp(mem[0].T)
    A["w1"] = np.ascontiguousarray(w_in[0].reshape(8, 128, 14, 256).transpose(2, 1, 0, 3))
    A["wkv"] = kp(w_kv[0])
    A["wout"] = kp(w_out[0])
    A["sgw"] = np.ascontiguousarray(sg_w[0].transpose(2, 0, 1))
    A["sgb"] = np.ascontiguousarray(np.repeat(sg_b[0], 64, axis=0).reshape(2, 128, 128).transpose(1, 0, 2))
    bd = np.zeros((128, 2, 128), pool_w.dtype)
    for g in range(4):
        lo = 64 * (g % 2)
        bd[lo:lo + 64, g // 2, lo:lo + 64] = pool_w[0, g]
    A["poolw"] = bd
    A["pw"] = kp(cc_pw_w[0])
    A["pc"] = np.ascontiguousarray(np.concatenate(
        [cols(conv_a_w[0]), cols(cc_dw_w[0]), cols(cc_dw_b[0]), cols(cc_ln_g[0]), cols(cc_ln_b[0]),
         cols(pool_scale[0]), cols(g_q_a_2[0]), cols(g_kv_a_2[0])], axis=1))
    for n, v in (("sg_ln_g", sg_ln_g), ("sg_ln_b", sg_ln_b), ("ln_g", ln_g), ("ln_b", ln_b),
                 ("g_q_gqa_2", g_q_gqa_2), ("g_k_gqa_2", g_k_gqa_2), ("ln1_g_2", ln1_g_2), ("ln1_b_2", ln1_b_2),
                 ("ln2_g_2", ln2_g_2), ("ln2_b_2", ln2_b_2), ("b_router_2", b_router_2)):
        A[n] = v[0]
    A["g_o"] = np.concatenate([g_o_mla_2[0], g_o_gqa_2[0]])
    A["ln_emb_g_2"], A["ln_emb_b_2"] = ln_emb_g_2, ln_emb_b_2
    A["meta"] = meta_tokens_2
    A["w2"] = kp(w_in_2[0])
    A["wqb"] = kp(w_q_b_2[0])
    A["wkvb"] = w_kv_b_2[0]
    A["wo2"] = kp(w_o_2[0])
    A["wr"] = kp(w_router_2[0])
    gu = w_gate_up_2[0].reshape(32, 8, 128, 4, 256, 2)
    A["wgu"] = np.ascontiguousarray(gu.transpose(0, 3, 2, 1, 5, 4)).reshape(32, 4, 128, 4096)
    A["bgu"] = np.ascontiguousarray(b_gate_up_2[0].reshape(32, 4, 256, 2).transpose(0, 1, 3, 2)).reshape(32, 2048)
    A["wdn"] = np.ascontiguousarray(w_down_2[0].reshape(32, 8, 128, 2, 512).transpose(0, 3, 2, 1, 4)).reshape(32, 2, 128, 4096)
    A["bdn"] = b_down_2[0]
    return A


def shape_constants():
    C = {}
    f = np.float32
    C["onm"] = np.full((128, 128), 1.0 / 256, f)
    i = np.arange(128)
    C["tri"] = (i[:, None] <= i[None, :]).astype(f)
    C["ident"] = np.eye(128, dtype=f)
    C["before"] = (i[:, None] < i[None, :]).astype(f)
    prc = np.zeros((128, 2, 17), f)
    for g, w in enumerate((2, 4, 8, 16)):
        lo = 64 * (g % 2)
        prc[lo:lo + 64, g // 2, 0:16] = f(1) / np.minimum(np.arange(16) + 1, w).astype(f)
        prc[lo:lo + 64, g // 2, 16] = 1.0 / w
    C["prc"] = prc
    t = np.arange(S)
    pos = np.concatenate([t + NM, np.arange(NM)])
    row = np.concatenate([t // 64, np.full(NM, -1)])
    col = np.concatenate([t % 64, np.arange(NM)])

    def rope(p_, dim):
        inv = f(10000.0) ** (-np.arange(0, dim, 2, dtype=f) / f(dim))
        ang = p_.astype(f)[:, None] * inv[None, :].astype(f)
        return np.cos(ang).astype(f), np.sin(ang).astype(f)

    c1, s1 = rope(pos, 64)
    cr, sr = rope(row, 64)
    cc, sc = rope(col, 64)
    R = np.concatenate([c1, c1, -s1, s1, cr, cr, cc, cc, -sr, sr, -sc, sc], axis=1)
    pad = np.zeros((17 * 128 - L, R.shape[1]), f)
    C["rope"] = np.ascontiguousarray(np.concatenate([R, pad]).reshape(17, 128, 384))
    C["qcol"] = np.arange(128, dtype=f).reshape(128, 1)
    C["erow"] = np.broadcast_to(np.arange(32, dtype=f), (128, 32)).copy()
    C["thr"] = np.broadcast_to(np.arange(1, 16, dtype=f) * 128, (128, 15)).copy()
    C["tokid"] = np.ascontiguousarray(np.arange(S, dtype=np.int32).reshape(16, 128).T)
    return C


def kernel(**inputs):
    import numpy as _np
    import concourse.bacc as _bacc
    from concourse import mybir as _mybir
    from concourse.bass_utils import run_bass_kernel_spmd as _run

    nc = _bacc.Bacc("TRN2", target_bir_lowering=False, num_devices=1)
    arrays = host_arrays(**{k: _np.asarray(v) for k, v in inputs.items()})
    arrays.update(shape_constants())
    arrays = {"in_" + k: _np.ascontiguousarray(v) for k, v in arrays.items()}
    A = {k[3:]: nc.dram_tensor(k, v.shape, _mybir.dt.from_np(v.dtype), kind="ExternalInput").ap()
         for k, v in arrays.items()}
    out = nc.dram_tensor("out_0", (S, D), _mybir.dt.float32, kind="ExternalOutput").ap()
    build(nc, A, out)
    r = _run(nc, [arrays], core_ids=[0])
    return r.results[0]["out_0"].reshape(1, S, D)
```
